# Optimizing a Trainium2 kernel written in Bass

```python
import jax, jax.numpy as jnp
from jax import lax
import numpy as np

D_MODEL = 1024
BATCH = 1
SEQ = 1024
DEPTH = 1

D_MIX = D_MODEL
POOL_WIDTH = D_MIX // 4
POOL_WINDOWS = (2, 4, 8, 16)
N_POOL_GROUPS = len(POOL_WINDOWS)
POOL_GROUP_DIM = POOL_WIDTH // N_POOL_GROUPS
SSD_WIDTH = D_MIX - POOL_WIDTH
SSD_HEAD_DIM = 64
SSD_HEADS = SSD_WIDTH // SSD_HEAD_DIM
SSD_GROUPS = 4
SSD_HEADS_PER_GROUP = SSD_HEADS // SSD_GROUPS
SSD_STATE = 128
SSD_CONV = 4
SSD_CHUNK = 128
SSD_CONV_DIM = SSD_WIDTH + 2 * SSD_GROUPS * SSD_STATE
IN_PROJ_DIM = POOL_WIDTH + SSD_WIDTH + SSD_CONV_DIM + SSD_HEADS
N_EXPERT_GROUPS = 4
EXPERTS_PER_GROUP = 8
N_EXPERTS = N_EXPERT_GROUPS * EXPERTS_PER_GROUP
TOP_K = 2
EXPERT_FF = 512
MOE_BLOCK = 128
NORM_EPS = 1e-6


def rms_norm(x, eps=NORM_EPS):
    xf = x.astype(jnp.float32)
    y = xf * lax.rsqrt(jnp.mean(xf * xf, axis=-1, keepdims=True) + eps)
    return y.astype(x.dtype)

def modulate(x, shift, scale):
    return rms_norm(x) * (1 + scale[:, None, :]) + shift[:, None, :]

def pool_mixer(u, w_pool, pool_scale):
    b, s, _ = u.shape
    ug = u.reshape(b, s, N_POOL_GROUPS, POOL_GROUP_DIM)
    cs = jnp.cumsum(ug.astype(jnp.float32), axis=1)
    pos = jnp.arange(1, s + 1, dtype=jnp.float32)
    means = []
    for g, w in enumerate(POOL_WINDOWS):
        csg = cs[:, :, g]
        lagged = jnp.pad(csg, ((0, 0), (w, 0), (0, 0)))[:, :s]
        cnt = jnp.minimum(pos, float(w))
        means.append((csg - lagged) / cnt[None, :, None])
    mean = jnp.stack(means, axis=2).astype(u.dtype)
    y = jnp.einsum('bsgc,gcd->bsgd', mean - ug, w_pool)
    return y.reshape(b, s, POOL_WIDTH) * pool_scale

def causal_depthwise_conv(x, w, bias):
    ch = x.shape[-1]
    y = lax.conv_general_dilated(
        x, w[:, None, :].astype(x.dtype), window_strides=(1,),
        padding=((SSD_CONV - 1, 0),), dimension_numbers=('NWC', 'WIO', 'NWC'),
        feature_group_count=ch)
    return y + bias

def ssd_scan(xh, dt, a, bmat, cmat):
    b, s = xh.shape[:2]
    L = SSD_CHUNK
    nc = s // L
    G, R, P, N = SSD_GROUPS, SSD_HEADS_PER_GROUP, SSD_HEAD_DIM, SSD_STATE
    xc = (xh.astype(jnp.float32) * dt[..., None]).reshape(b, nc, L, G, R, P)
    bc = bmat.astype(jnp.float32).reshape(b, nc, L, G, N)
    cc = cmat.astype(jnp.float32).reshape(b, nc, L, G, N)
    a_cs = jnp.cumsum((dt * a).reshape(b, nc, L, G, R), axis=2)
    causal = jnp.tril(jnp.ones((L, L), dtype=bool))
    seg = a_cs[:, :, :, None] - a_cs[:, :, None, :]
    decay = jnp.exp(jnp.where(causal[None, None, :, :, None, None], seg, -jnp.inf))
    cb = jnp.einsum('bclgn,bcsgn->bclsg', cc, bc)
    y_diag = jnp.einsum('bclsgr,bcsgrp->bclgrp', cb[..., None] * decay, xc)
    decay_to_end = jnp.exp(a_cs[:, :, -1:] - a_cs)
    chunk_states = jnp.einsum('bclgn,bclgrp->bcgrpn', bc, xc * decay_to_end[..., None])
    chunk_decay = jnp.exp(a_cs[:, :, -1])

    def step(state, inp):
        st, dec = inp
        return state * dec[..., None, None] + st, state

    init = jnp.zeros((b, G, R, P, N), jnp.float32)
    _, prev = lax.scan(step, init, (jnp.moveaxis(chunk_states, 1, 0),
                                    jnp.moveaxis(chunk_decay, 1, 0)))
    prev = jnp.moveaxis(prev, 0, 1)
    y_off = jnp.einsum('bclgn,bcgrpn->bclgrp', cc, prev) * jnp.exp(a_cs)[..., None]
    return (y_diag + y_off).reshape(b, s, G, R, P)

def ssd_mixer(z, xbc, dt_raw, conv_w, conv_b, dt_bias, a_log, d_skip, norm_w):
    b, s, _ = z.shape
    G, R, P, N = SSD_GROUPS, SSD_HEADS_PER_GROUP, SSD_HEAD_DIM, SSD_STATE
    xbc = jax.nn.silu(causal_depthwise_conv(xbc, conv_w, conv_b))
    xs, bm, cm = jnp.split(xbc, [SSD_WIDTH, SSD_WIDTH + G * N], axis=-1)
    xh = xs.reshape(b, s, G, R, P)
    bm = bm.reshape(b, s, G, N)
    cm = cm.reshape(b, s, G, N)
    dt = jax.nn.softplus(dt_raw.astype(jnp.float32) + dt_bias.astype(jnp.float32)).reshape(b, s, G, R)
    a = -jnp.exp(a_log.astype(jnp.float32)).reshape(G, R)
    y = ssd_scan(xh, dt, a, bm, cm) + xh.astype(jnp.float32) * d_skip.astype(jnp.float32).reshape(G, R)[..., None]
    y = y.reshape(b, s, SSD_WIDTH).astype(z.dtype) * jax.nn.silu(z)
    y = rms_norm(y.reshape(b, s, G, SSD_WIDTH // G)).reshape(b, s, SSD_WIDTH)
    return y * norm_w

def hier_moe(h, w_group, b_group, w_router, b_router, w13, w2):
    b, s, d = h.shape
    T = b * s
    hf = h.reshape(T, d)
    g_logits = (hf @ w_group + b_group).astype(jnp.float32)
    g_prob = jax.nn.softmax(g_logits, axis=-1)
    p_g, g_idx = lax.top_k(g_prob, 1)
    e_logits = (hf @ w_router + b_router).astype(jnp.float32).reshape(T, N_EXPERT_GROUPS, EXPERTS_PER_GROUP)
    within = jnp.take_along_axis(e_logits, g_idx[:, :, None], axis=1)[:, 0]
    top_v, top_i = lax.top_k(within, TOP_K)
    gate = p_g * jax.nn.softmax(top_v, axis=-1)
    expert_id = (g_idx * EXPERTS_PER_GROUP + top_i).astype(jnp.int32)
    A = T * TOP_K
    flat_e = expert_id.reshape(A)
    flat_tok = jnp.repeat(jnp.arange(T, dtype=jnp.int32), TOP_K)
    flat_w = gate.reshape(A)
    order = jnp.argsort(flat_e)
    se, stok, sw = flat_e[order], flat_tok[order], flat_w[order]
    counts = jnp.bincount(flat_e, length=N_EXPERTS)
    starts = jnp.cumsum(counts) - counts
    padded = ((counts + MOE_BLOCK - 1) // MOE_BLOCK) * MOE_BLOCK
    pends = jnp.cumsum(padded)
    pstarts = pends - padded
    dest = pstarts[se] + (jnp.arange(A, dtype=jnp.int32) - starts[se])
    R = A + N_EXPERTS * MOE_BLOCK
    n_blk = R // MOE_BLOCK
    row_tok = jnp.zeros((R,), jnp.int32).at[dest].set(stok)
    row_w = jnp.zeros((R,), h.dtype).at[dest].set(sw.astype(h.dtype))
    blk_start = jnp.arange(n_blk, dtype=jnp.int32) * MOE_BLOCK
    blk_e = jnp.clip(jnp.searchsorted(pends, blk_start, side='right'), 0, N_EXPERTS - 1)
    xs = hf[row_tok].reshape(n_blk, MOE_BLOCK, d)

    def expert_block(args):
        xb, e = args
        hu = xb @ w13[e]
        a_, b_ = jnp.split(hu, 2, axis=-1)
        return (jax.nn.silu(a_) * b_) @ w2[e]

    ys = lax.map(expert_block, (xs, blk_e)).reshape(R, d)
    out = jax.ops.segment_sum(ys * row_w[:, None], row_tok, num_segments=T)
    return out.reshape(b, s, d)

def first_inputs(seed: int = 0) -> dict:
    key = jax.random.key(seed)
    ks = jax.random.split(key, 24)
    f32 = jnp.float32
    nrm = lambda k, shape, scale: jax.random.normal(k, shape, f32) * scale
    x = jax.random.normal(ks[0], (BATCH, SEQ, D_MODEL), f32)
    c = jax.random.normal(ks[1], (BATCH, D_MODEL), f32)
    w_ada = nrm(ks[2], (DEPTH, D_MODEL, 6 * D_MODEL), D_MODEL ** -0.5)
    b_ada = nrm(ks[3], (DEPTH, 6 * D_MODEL), 0.02)
    w_in = nrm(ks[4], (DEPTH, D_MODEL, IN_PROJ_DIM), D_MODEL ** -0.5)
    w_pool = nrm(ks[5], (DEPTH, N_POOL_GROUPS, POOL_GROUP_DIM, POOL_GROUP_DIM), POOL_GROUP_DIM ** -0.5)
    pool_scale = 1.0 + nrm(ks[6], (DEPTH, POOL_WIDTH), 0.1)
    conv_w = nrm(ks[7], (DEPTH, SSD_CONV, SSD_CONV_DIM), SSD_CONV ** -0.5)
    conv_b = nrm(ks[8], (DEPTH, SSD_CONV_DIM), 0.02)
    dt0 = jnp.exp(jax.random.uniform(ks[9], (DEPTH, SSD_HEADS), f32, np.log(1e-3), np.log(1e-1)))
    dt_bias = dt0 + jnp.log(-jnp.expm1(-dt0))
    a_log = jnp.log(jax.random.uniform(ks[10], (DEPTH, SSD_HEADS), f32, 1.0, 16.0))
    d_skip = 1.0 + nrm(ks[11], (DEPTH, SSD_HEADS), 0.1)
    ssd_norm_w = 1.0 + nrm(ks[12], (DEPTH, SSD_WIDTH), 0.1)
    w_out = nrm(ks[13], (DEPTH, D_MIX, D_MODEL), D_MIX ** -0.5)
    w_group = nrm(ks[14], (DEPTH, D_MODEL, N_EXPERT_GROUPS), D_MODEL ** -0.5)
    b_group = nrm(ks[15], (DEPTH, N_EXPERT_GROUPS), 0.01)
    w_router = nrm(ks[16], (DEPTH, D_MODEL, N_EXPERTS), D_MODEL ** -0.5)
    b_router = nrm(ks[17], (DEPTH, N_EXPERTS), 0.01)
    w13 = nrm(ks[18], (DEPTH, N_EXPERTS, D_MODEL, 2 * EXPERT_FF), D_MODEL ** -0.5)
    w2 = nrm(ks[19], (DEPTH, N_EXPERTS, EXPERT_FF, D_MODEL), EXPERT_FF ** -0.5)
    final_norm_w = 1.0 + nrm(ks[20], (D_MODEL,), 0.1)
    return {"x": x, "c": c, "w_ada": w_ada, "b_ada": b_ada, "w_in": w_in,
            "w_pool": w_pool, "pool_scale": pool_scale, "conv_w": conv_w, "conv_b": conv_b,
            "dt_bias": dt_bias, "a_log": a_log, "d_skip": d_skip, "ssd_norm_w": ssd_norm_w,
            "w_out": w_out, "w_group": w_group, "b_group": b_group, "w_router": w_router,
            "b_router": b_router, "w13": w13, "w2": w2, "final_norm_w": final_norm_w}

def first_block(x, c, w_ada, b_ada, w_in, w_pool, pool_scale, conv_w, conv_b, dt_bias, a_log,
              d_skip, ssd_norm_w, w_out, w_group, b_group, w_router, b_router, w13, w2,
              final_norm_w):
    split_at = [POOL_WIDTH, POOL_WIDTH + SSD_WIDTH, POOL_WIDTH + SSD_WIDTH + SSD_CONV_DIM]
    for layer in range(DEPTH):
        mod = jax.nn.silu(c) @ w_ada[layer] + b_ada[layer]
        sh1, sc1, g1, sh2, sc2, g2 = jnp.split(mod, 6, axis=-1)
        h = modulate(x, sh1, sc1)
        proj = h @ w_in[layer]
        u, z, xbc, dt_raw = jnp.split(proj, split_at, axis=-1)
        y_pool = pool_mixer(u, w_pool[layer], pool_scale[layer])
        y_ssd = ssd_mixer(z, xbc, dt_raw, conv_w[layer], conv_b[layer], dt_bias[layer],
                          a_log[layer], d_skip[layer], ssd_norm_w[layer])
        mix = jnp.concatenate([y_pool, y_ssd], axis=-1) @ w_out[layer]
        x = x + g1[:, None, :] * mix
        h = modulate(x, sh2, sc2)
        x = x + g2[:, None, :] * hier_moe(h, w_group[layer], b_group[layer], w_router[layer],
                                           b_router[layer], w13[layer], w2[layer])
    return rms_norm(x) * final_norm_w


N_MIXERS = 4
HEAD_DIM = 64
N_Q_HEADS = D_MODEL // HEAD_DIM
N_KV_HEADS = 4
GQA_GROUP = N_Q_HEADS // N_KV_HEADS
ATTN_Q_DIM = N_Q_HEADS * HEAD_DIM
ATTN_KV_DIM = N_KV_HEADS * HEAD_DIM
ATTN_IN_DIM = ATTN_Q_DIM + 2 * ATTN_KV_DIM
SWA_WINDOW = 128
SWA_BLOCK = 128
MOBA_BLOCK = 256
MOBA_TOP_K = 3
MOBA_Q_CHUNK = 64
GLA_HEADS = 4
GLA_KEY_DIM = D_MODEL // (2 * GLA_HEADS)
GLA_VAL_DIM = D_MODEL // GLA_HEADS
GLA_GATE_RANK = 16
GLA_GATE_TEMP = 16.0
GLA_IN_DIM = 2 * GLA_HEADS * GLA_KEY_DIM + 2 * GLA_HEADS * GLA_VAL_DIM + GLA_GATE_RANK
HGRN_EXPAND = 128
HGRN_HEADS = D_MODEL // HGRN_EXPAND
HGRN_KEY_DIM = HGRN_EXPAND
HGRN_VAL_DIM = D_MODEL // HGRN_HEADS
HGRN_IN_DIM = 4 * D_MODEL
LIN_CHUNK = 64
D_FF = ((8 * D_MODEL + 3 * 256 - 1) // (3 * 256)) * 256
RMS_EPS = 1e-6


def rms_norm_2(x, w):
    xf = x.astype(jnp.float32)
    y = xf * lax.rsqrt(jnp.mean(xf * xf, axis=-1, keepdims=True) + RMS_EPS)
    return (y * w.astype(jnp.float32)).astype(x.dtype)

def head_rms_norm(o, w):
    return o * lax.rsqrt(jnp.mean(o * o, axis=-1, keepdims=True) + RMS_EPS) * w.astype(jnp.float32)

def alibi_slopes(n_heads):
    return jnp.exp2(-8.0 * jnp.arange(1, n_heads + 1, dtype=jnp.float32) / n_heads)

def split_qkv(h, w_in):
    B, T, _ = h.shape
    proj = h @ w_in
    q = proj[..., :ATTN_Q_DIM].reshape(B, T, N_KV_HEADS, GQA_GROUP, HEAD_DIM)
    k = proj[..., ATTN_Q_DIM:ATTN_Q_DIM + ATTN_KV_DIM].reshape(B, T, N_KV_HEADS, HEAD_DIM)
    v = proj[..., ATTN_Q_DIM + ATTN_KV_DIM:].reshape(B, T, N_KV_HEADS, HEAD_DIM)
    return q, k, v

def sliding_window_sink_attention(h, w_in, sinks, w_out):
    B, T, _ = h.shape
    L = SWA_BLOCK
    nb = T // L
    q, k, v = split_qkv(h, w_in)
    qb = q.reshape(B, nb, L, N_KV_HEADS, GQA_GROUP, HEAD_DIM)

    def with_prev(a):
        a = a.reshape(B, nb, L, N_KV_HEADS, HEAD_DIM)
        prev = jnp.concatenate([jnp.zeros_like(a[:, :1]), a[:, :-1]], axis=1)
        return jnp.concatenate([prev, a], axis=2)

    kw, vw = with_prev(k), with_prev(v)
    s = jnp.einsum('bnqhgd,bnkhd->bnhgqk', qb, kw, preferred_element_type=jnp.float32) * (HEAD_DIM ** -0.5)
    dist = (L + jnp.arange(L))[:, None] - jnp.arange(2 * L)[None, :]
    band = (dist >= 0) & (dist < SWA_WINDOW)
    has_prev = (jnp.arange(nb)[:, None, None] > 0) | (jnp.arange(2 * L)[None, None, :] >= L)
    mask = band[None] & has_prev
    slopes = alibi_slopes(N_Q_HEADS).reshape(N_KV_HEADS, GQA_GROUP)
    s = s - slopes[:, :, None, None] * dist.astype(jnp.float32)
    s = jnp.where(mask[None, :, None, None], s, -jnp.inf)
    sink = sinks.astype(jnp.float32).reshape(N_KV_HEADS, GQA_GROUP)[:, :, None, None]
    m = jnp.maximum(jnp.max(s, axis=-1, keepdims=True), sink)
    p = jnp.exp(s - m)
    denom = jnp.sum(p, axis=-1, keepdims=True) + jnp.exp(sink - m)
    o = jnp.einsum('bnhgqk,bnkhd->bnqhgd', p / denom, vw.astype(jnp.float32))
    return o.reshape(B, T, ATTN_Q_DIM).astype(h.dtype) @ w_out

def moba_attention(h, w_in, w_out):
    B, T, _ = h.shape
    Lb, Qc = MOBA_BLOCK, MOBA_Q_CHUNK
    q, k, v = split_qkv(h, w_in)
    Tp = ((T + Lb - 1) // Lb) * Lb
    pad = Tp - T
    q = jnp.pad(q.astype(jnp.float32), ((0, 0), (0, pad), (0, 0), (0, 0), (0, 0))) * (HEAD_DIM ** -0.5)
    k = jnp.pad(k.astype(jnp.float32), ((0, 0), (0, pad), (0, 0), (0, 0)))
    v = jnp.pad(v.astype(jnp.float32), ((0, 0), (0, pad), (0, 0), (0, 0)))
    nblk, nq = Tp // Lb, Tp // Qc
    n_sel = min(MOBA_TOP_K, nblk)
    kb = k.reshape(B, nblk, Lb, N_KV_HEADS, HEAD_DIM).transpose(0, 3, 1, 2, 4)
    vb = v.reshape(B, nblk, Lb, N_KV_HEADS, HEAD_DIM).transpose(0, 3, 1, 2, 4)
    k_mean = jnp.mean(kb, axis=3)
    gate = jnp.einsum('bthgd,bhnd->bhtn', q, k_mean)
    t_blk = jnp.arange(Tp) // Lb
    past = jnp.arange(nblk)[None, :] < t_blk[:, None]
    gate = jnp.where(past, gate, -jnp.inf)
    _, sel_idx = lax.top_k(gate, n_sel)
    sel_valid = jnp.arange(n_sel)[None, :] < t_blk[:, None]
    q_chunks = q.reshape(B, nq, Qc, N_KV_HEADS, GQA_GROUP, HEAD_DIM).transpose(1, 0, 2, 3, 4, 5)
    idx_chunks = sel_idx.reshape(B, N_KV_HEADS, nq, Qc, n_sel).transpose(2, 0, 1, 3, 4)
    valid_chunks = sel_valid.reshape(nq, Qc, n_sel)
    slopes = alibi_slopes(N_Q_HEADS).reshape(N_KV_HEADS, GQA_GROUP)
    gather_blocks = jax.vmap(jax.vmap(lambda blocks, ix: blocks[ix]))

    def attend(args):
        c, qc, idx, valid = args
        t_q = c * Qc + jnp.arange(Qc)
        own = (c * Qc) // Lb
        k_own = lax.dynamic_index_in_dim(kb, own, axis=2, keepdims=False)
        v_own = lax.dynamic_index_in_dim(vb, own, axis=2, keepdims=False)
        k_sel = gather_blocks(kb, idx)
        v_sel = gather_blocks(vb, idx)
        s_sel = jnp.einsum('bqhgd,bhqnkd->bhgqnk', qc, k_sel)
        dist_sel = (t_q[:, None, None] - (idx[..., None] * Lb + jnp.arange(Lb))).astype(jnp.float32)
        s_sel = s_sel - slopes[None, :, :, None, None, None] * dist_sel[:, :, None]
        s_sel = jnp.where(valid[:, :, None], s_sel, -jnp.inf)
        s_own = jnp.einsum('bqhgd,bhkd->bhgqk', qc, k_own)
        dist_own = t_q[:, None] - (own * Lb + jnp.arange(Lb))[None, :]
        s_own = s_own - slopes[:, :, None, None] * dist_own.astype(jnp.float32)
        s_own = jnp.where(dist_own >= 0, s_own, -jnp.inf)
        s_all = jnp.concatenate([s_sel.reshape(B, N_KV_HEADS, GQA_GROUP, Qc, n_sel * Lb), s_own], axis=-1)
        p = jax.nn.softmax(s_all, axis=-1)
        p_sel = p[..., :n_sel * Lb].reshape(B, N_KV_HEADS, GQA_GROUP, Qc, n_sel, Lb)
        p_own = p[..., n_sel * Lb:]
        return (jnp.einsum('bhgqnk,bhqnkd->bqhgd', p_sel, v_sel)
                + jnp.einsum('bhgqk,bhkd->bqhgd', p_own, v_own))

    o = lax.map(attend, (jnp.arange(nq), q_chunks, idx_chunks, valid_chunks))
    o = o.transpose(1, 0, 2, 3, 4, 5).reshape(B, Tp, ATTN_Q_DIM)[:, :T]
    return o.astype(h.dtype) @ w_out

def chunked_gated_linear_attention(q, k, v, log_g):
    B, T, H, K = q.shape
    V = v.shape[-1]
    L = LIN_CHUNK
    nc = T // L

    def to_chunks(a):
        return a.astype(jnp.float32).reshape(B, nc, L, H, a.shape[-1]).transpose(1, 0, 3, 2, 4)

    causal = jnp.tril(jnp.ones((L, L), dtype=bool))

    def step(S, inp):
        qc, kc, vc, gc = inp
        b = jnp.cumsum(gc, axis=2)
        b_last = b[:, :, -1:, :]
        q_dec = qc * jnp.exp(b)
        attn = jnp.einsum('bhtk,bhsk->bhts', q_dec, kc * jnp.exp(-b))
        attn = jnp.where(causal, attn, 0.0)
        o = jnp.einsum('bhts,bhsv->bhtv', attn, vc) + jnp.einsum('bhtk,bhkv->bhtv', q_dec, S)
        S = S * jnp.exp(b_last).swapaxes(-1, -2) + jnp.einsum('bhsk,bhsv->bhkv', kc * jnp.exp(b_last - b), vc)
        return S, o

    S0 = jnp.zeros((B, H, K, V), jnp.float32)
    _, o = lax.scan(step, S0, (to_chunks(q), to_chunks(k), to_chunks(v), to_chunks(log_g)))
    return o.transpose(1, 0, 3, 2, 4).reshape(B, T, H, V)

def gla_mixer(h, w_in, w_decay_up, b_decay, out_norm, w_out):
    B, T, _ = h.shape
    proj = h @ w_in
    dk, dv = GLA_HEADS * GLA_KEY_DIM, GLA_HEADS * GLA_VAL_DIM
    q = proj[..., :dk].reshape(B, T, GLA_HEADS, GLA_KEY_DIM).astype(jnp.float32) * (GLA_KEY_DIM ** -0.5)
    k = proj[..., dk:2 * dk].reshape(B, T, GLA_HEADS, GLA_KEY_DIM)
    v = proj[..., 2 * dk:2 * dk + dv].reshape(B, T, GLA_HEADS, GLA_VAL_DIM)
    g = proj[..., 2 * dk + dv:2 * dk + 2 * dv].reshape(B, T, GLA_HEADS, GLA_VAL_DIM)
    a = proj[..., 2 * dk + 2 * dv:]
    log_alpha = jax.nn.log_sigmoid((a @ w_decay_up + b_decay).astype(jnp.float32)) / GLA_GATE_TEMP
    log_alpha = log_alpha.reshape(B, T, GLA_HEADS, GLA_KEY_DIM)
    o = chunked_gated_linear_attention(q, k, v, log_alpha)
    o = head_rms_norm(o, out_norm) * jax.nn.silu(g.astype(jnp.float32))
    return o.reshape(B, T, dv).astype(h.dtype) @ w_out

def hgrn2_mixer(h, w_in, lower_bound, out_norm, w_out):
    B, T, _ = h.shape
    proj = h @ w_in
    d = D_MODEL
    q = jax.nn.silu(proj[..., :d].astype(jnp.float32)) * (HGRN_KEY_DIM ** -0.5)
    f = lower_bound + (1.0 - lower_bound) * jax.nn.sigmoid(proj[..., d:2 * d].astype(jnp.float32))
    i = proj[..., 2 * d:3 * d]
    g = proj[..., 3 * d:]
    shp_k = (B, T, HGRN_HEADS, HGRN_KEY_DIM)
    o = chunked_gated_linear_attention(q.reshape(shp_k), (1.0 - f).reshape(shp_k),
                                       i.reshape(B, T, HGRN_HEADS, HGRN_VAL_DIM), jnp.log(f).reshape(shp_k))
    o = head_rms_norm(o, out_norm) * jax.nn.silu(g.astype(jnp.float32)).reshape(B, T, HGRN_HEADS, HGRN_VAL_DIM)
    return o.reshape(B, T, HGRN_HEADS * HGRN_VAL_DIM).astype(h.dtype) @ w_out

def swiglu_ffn(h, w_gate_up, w_down):
    gu = h @ w_gate_up
    return (jax.nn.silu(gu[..., :D_FF]) * gu[..., D_FF:]) @ w_down

def second_inputs(seed: int = 0) -> dict:
    key = jax.random.key(seed)
    ks = jax.random.split(key, 20)
    n_a, n_b, n_c, n_d = [(DEPTH - kind + N_MIXERS - 1) // N_MIXERS for kind in range(N_MIXERS)]

    def normal(k, shape):
        return jax.random.normal(k, shape, jnp.float32)

    def dense(k, shape, fan_in):
        return normal(k, shape) * (fan_in ** -0.5)

    def gain(k, shape):
        return 1.0 + 0.02 * normal(k, shape)

    return {
        'x': normal(ks[0], (BATCH, SEQ, D_MODEL)),
        'norm_mix': gain(ks[1], (DEPTH, D_MODEL)),
        'norm_ffn': gain(ks[2], (DEPTH, D_MODEL)),
        'swa_w_in': dense(ks[3], (n_a, D_MODEL, ATTN_IN_DIM), D_MODEL),
        'swa_sinks': 0.5 * normal(ks[4], (n_a, N_Q_HEADS)),
        'swa_w_out': dense(ks[5], (n_a, ATTN_Q_DIM, D_MODEL), ATTN_Q_DIM),
        'moba_w_in': dense(ks[6], (n_b, D_MODEL, ATTN_IN_DIM), D_MODEL),
        'moba_w_out': dense(ks[7], (n_b, ATTN_Q_DIM, D_MODEL), ATTN_Q_DIM),
        'gla_w_in': dense(ks[8], (n_c, D_MODEL, GLA_IN_DIM), D_MODEL),
        'gla_w_decay_up': dense(ks[9], (n_c, GLA_GATE_RANK, GLA_HEADS * GLA_KEY_DIM), GLA_GATE_RANK),
        'gla_b_decay': 0.1 * normal(ks[10], (n_c, GLA_HEADS * GLA_KEY_DIM)),
        'gla_out_norm': gain(ks[11], (n_c, GLA_VAL_DIM)),
        'gla_w_out': dense(ks[12], (n_c, GLA_HEADS * GLA_VAL_DIM, D_MODEL), GLA_HEADS * GLA_VAL_DIM),
        'hgrn_w_in': dense(ks[13], (n_d, D_MODEL, HGRN_IN_DIM), D_MODEL),
        'hgrn_lb_logits': 0.5 * normal(ks[14], (DEPTH, HGRN_HEADS * HGRN_KEY_DIM)),
        'hgrn_out_norm': gain(ks[15], (n_d, HGRN_VAL_DIM)),
        'hgrn_w_out': dense(ks[16], (n_d, HGRN_HEADS * HGRN_VAL_DIM, D_MODEL), HGRN_HEADS * HGRN_VAL_DIM),
        'ffn_w_gate_up': dense(ks[17], (DEPTH, D_MODEL, 2 * D_FF), D_MODEL),
        'ffn_w_down': dense(ks[18], (DEPTH, D_FF, D_MODEL), D_FF),
        'final_norm': gain(ks[19], (D_MODEL,)),
    }

def second_block(x, norm_mix, norm_ffn, swa_w_in, swa_sinks, swa_w_out, moba_w_in, moba_w_out,
              gla_w_in, gla_w_decay_up, gla_b_decay, gla_out_norm, gla_w_out,
              hgrn_w_in, hgrn_lb_logits, hgrn_out_norm, hgrn_w_out,
              ffn_w_gate_up, ffn_w_down, final_norm):
    lb_p = jax.nn.softmax(hgrn_lb_logits.astype(jnp.float32), axis=0)
    lb_table = jnp.cumsum(lb_p, axis=0) - lb_p[0]
    for i in range(DEPTH):
        kind, j = i % N_MIXERS, i // N_MIXERS
        h = rms_norm_2(x, norm_mix[i])
        if kind == 0:
            mix = sliding_window_sink_attention(h, swa_w_in[j], swa_sinks[j], swa_w_out[j])
        elif kind == 1:
            mix = moba_attention(h, moba_w_in[j], moba_w_out[j])
        elif kind == 2:
            mix = gla_mixer(h, gla_w_in[j], gla_w_decay_up[j], gla_b_decay[j], gla_out_norm[j], gla_w_out[j])
        else:
            mix = hgrn2_mixer(h, hgrn_w_in[j], lb_table[i], hgrn_out_norm[j], hgrn_w_out[j])
        x = x + mix.astype(x.dtype)
        x = x + swiglu_ffn(rms_norm_2(x, norm_ffn[i]), ffn_w_gate_up[i], ffn_w_down[i]).astype(x.dtype)
    return rms_norm_2(x, final_norm)


def setup_inputs(seed=0):
    out = dict(first_inputs(seed))
    for name, value in second_inputs(seed + 1).items():
        if name != "x":
            out[name + "_2"] = value
    return out


def reference(
    x, c, w_ada, b_ada, w_in, w_pool, pool_scale, conv_w, conv_b, dt_bias, a_log, d_skip,
    ssd_norm_w, w_out, w_group, b_group, w_router, b_router, w13, w2, final_norm_w, norm_mix_2,
    norm_ffn_2, swa_w_in_2, swa_sinks_2, swa_w_out_2, moba_w_in_2, moba_w_out_2, gla_w_in_2,
    gla_w_decay_up_2, gla_b_decay_2, gla_out_norm_2, gla_w_out_2, hgrn_w_in_2, hgrn_lb_logits_2,
    hgrn_out_norm_2, hgrn_w_out_2, ffn_w_gate_up_2, ffn_w_down_2, final_norm_2,
):
    x = first_block(
        x, c, w_ada, b_ada, w_in, w_pool, pool_scale, conv_w, conv_b, dt_bias, a_log, d_skip,
        ssd_norm_w, w_out, w_group, b_group, w_router, b_router, w13, w2, final_norm_w,
    )
    return second_block(
        x, norm_mix_2, norm_ffn_2, swa_w_in_2, swa_sinks_2, swa_w_out_2, moba_w_in_2,
        moba_w_out_2, gla_w_in_2, gla_w_decay_up_2, gla_b_decay_2, gla_out_norm_2, gla_w_out_2,
        hgrn_w_in_2, hgrn_lb_logits_2, hgrn_out_norm_2, hgrn_w_out_2, ffn_w_gate_up_2,
        ffn_w_down_2, final_norm_2,
    )


_drawn_inputs = setup_inputs


def setup_inputs(seed=0):
    import zlib

    import numpy as np

    out = dict(_drawn_inputs(seed))
    spreads = {}
    factors = {'b_group': 6.06,
     'b_router': 4.984,
     'norm_mix_2': 5.799,
     'norm_ffn_2': 4.076,
     'swa_sinks_2': 31.464}
    for name, (base, spread) in spreads.items():
        noise = np.random.default_rng([zlib.crc32(name.encode()), seed]).standard_normal(out[name].shape)
        drawn = base * np.exp(spread * noise) if base else spread * noise
        out[name] = __import__('jax').numpy.asarray(drawn.astype(out[name].dtype))
    for name, factor in factors.items():
        out[name] = (out[name] * factor).astype(out[name].dtype)
    return out
```

```python
from contextlib import ExitStack, contextmanager

import concourse.bass as bass
from concourse import mybir
import numpy as np

ALU = mybir.AluOpType
ACT = mybir.ActivationFunctionType
AX = mybir.AxisListType
F32 = mybir.dt.float32
F32R = mybir.dt.float32r
I32 = mybir.dt.int32

P = 128
T = 1024
D = 1024
KT = D // P
NT = T // P
HALF = 512
POOL_T, SSD_T, CONV_T = 2, 6, 14
CONV = 4
HEADS, HD, GROUPS, STATE = 12, 64, 4, 128
HPG = HEADS // GROUPS
CH = 128
NCH = T // CH
EG, EPG = 4, 8
NE = EG * EPG
FF = 512
NBLK = 2 * T // P + NE - 1
Q_HEADS, KV_HEADS = 16, 4
FFT = 2816 // P
FF_PARTS = (8, 8, 6)
EPS = 1e-6
BIG = 3.0e38
CREDIT = 400

COLS = {}
_at = 0
for _n, _w in (("b_ada", 48), ("c", 8), ("conv_w", CONV_T * CONV), ("conv_b", CONV_T), ("d_skip", SSD_T),
               ("pool_scale", POOL_T), ("ssd_norm_w", SSD_T), ("final_norm_w", KT), ("norm_mix", KT),
               ("norm_ffn", KT), ("final_norm", KT), ("router_b", EG + NE), ("sinks", Q_HEADS),
               ("dt_bias", 1), ("a_log", 1)):
    COLS[_n] = slice(_at, _at + _w)
    _at += _w
NCOLS = _at
CONSTS = {}
_at = 0
for _n, _w in (("ident", P), ("ones", P), ("upto", P), ("before", P), ("pool_first", 32), ("pool_inv", 2),
               ("iota8", 8), ("iota8x128", 8), ("iotab", NBLK + 1), ("tokid", NT)):
    CONSTS[_n] = slice(_at, _at + _w)
    _at += _w
NCONST = _at


class Lane:

    def __init__(self, stage, key):
        self.stage, self.key = stage, key
        self.sem = stage.sem("n_" + key)
        self.count, self.i, self.per, self.base, self.loops = CREDIT, None, 0, 0, 0

    def start(self, eng):
        self.e = eng
        eng.sem_inc(self.sem, CREDIT)
        return eng

    def at(self):
        return self.count if self.i is None else self.i * self.per + self.count

    def __call__(self, ins, name=None):
        ins.then_inc(self.sem, 1)
        self.count += 1
        if name:
            self.stage.marks[self.stage.name, self.key, name] = (self.count, self.per, self.trips if self.i is not None else 0)
        return ins

    def settle(self):
        self.e.wait_ge(self.sem, self.at())

    @contextmanager
    def loop(self, trips):
        key = (self.stage.name, self.key, "loop", self.loops)
        self.loops += 1
        start = self.count
        self.per = self.stage.counts.get(key, 1)
        self.trips = trips
        with self.e.Fori(0, trips) as i:
            self.i = i
            yield i
            self.i = None
        self.stage.marks[key] = self.count - start
        self.count = start + trips * self.per
        self.per = 0


class Stage:

    def __init__(self, nc, name, counts, marks):
        self.nc, self.name, self.counts, self.marks = nc, name, counts, marks
        self.ctx = ExitStack()

    def __enter__(self):
        self.pe, self.act, self.dve, self.pool = (Lane(self, k) for k in ("pe", "act", "dve", "pool"))
        return self

    def __exit__(self, *a):
        self.ctx.close()

    def sb(self, name, shape, dt=F32):
        return self.ctx.enter_context(self.nc.sbuf_tensor(f"{self.name}_{name}", shape, dt))

    def ps(self, name, shape, dt=F32):
        return self.ctx.enter_context(self.nc.psum_tensor(f"{self.name}_{name}", shape, dt))

    def sem(self, name):
        return self.ctx.enter_context(self.nc.semaphore(f"{self.name}_{name}"))

    def block(self):
        return self.nc.Block()

    def wait(self, eng, lane, name, i=None):
        count, per, trips = self.counts.get((self.name, lane.key, name), (CREDIT + 1, 0, 0))
        if trips and i is None:
            i = trips - 1
        eng.wait_ge(lane.sem, count + per * i if trips and per else count)


class Gemm:

    def __init__(self, st, kt=KT):
        self.st = st
        self.raw = st.sb("w_raw", [P, 2, kt * P])
        self.hi = st.sb("w_hi", [P, 2, kt * P], F32R)
        self.lo = st.sb("w_lo", [P, 2, kt * P], F32R)
        self.acc = [st.ps(f"acc{b}", [P, T]) for b in range(2)]
        self.s_loaded = [st.sem(f"w_loaded{b}") for b in range(2)]
        self.s_hi, self.s_split, self.s_mult, self.s_emptied = (
            st.sem(n) for n in ("w_hi", "w_split", "w_mult", "w_emptied"))

    def load(self, sp, i, base, b, src, kt=KT):
        sp.wait_ge(self.s_split, 2 * i + (base + b + 1))
        sp.dma_start(self.raw[:, b, 0:kt * P], src).then_inc(self.s_loaded[b], 16)

    def split(self, pool, i, base, b, kt=KT):
        raw, hi, lo = (x[:, b, 0:kt * P] for x in (self.raw, self.hi, self.lo))
        pool.wait_ge(self.s_loaded[b], 16 * i + 16 * (base // 2 + 1))
        pool.wait_ge(self.s_mult, 2 * i + (base + b + 1))
        pool.nop(nofuse=True)
        pool.tensor_copy(hi, raw).then_inc(self.s_hi, 1)
        pool.wait_ge(self.s_hi, 2 * i + (base + b + 1))
        pool.tensor_tensor(lo, raw, hi.bitcast(F32), ALU.subtract).then_inc(self.s_split, 1)

    def mult(self, pe, i, base, b, xh, xl, kt=KT):
        pe.wait_ge(self.s_split, 2 * i + (base + b + 3))
        pe.wait_ge(self.s_emptied, 2 * i + (base + b + 1))
        for h in range(0, T, HALF):
            for k in range(kt):
                for t, (w, x) in enumerate(((self.hi, xh), (self.hi, xl), (self.lo, xh))):
                    m = pe.matmul(self.acc[b][:, h:h + HALF], w[:, b, k * P:(k + 1) * P], x[:, k, h:h + HALF],
                                  start=(k == 0 and t == 0), stop=(k == kt - 1 and t == 2))
        m.then_inc(self.s_mult, 1)

    def ready(self, eng, i, base, b):
        eng.wait_ge(self.s_mult, 2 * i + (base + b + 3))

    def empty(self, ins):
        return ins.then_inc(self.s_emptied, 1)

    def emptied(self, eng, i, base, b):
        eng.wait_ge(self.s_emptied, 2 * i + (base + b + 3))


def tile_of(x, i, b=0, step=2):
    return x[:, bass.ds(step * i + b, 1), :].rearrange("p a t -> p (a t)")


class Kernel:
    def __init__(self, nc, ins, out, counts, marks):
        self.nc, self.ins, self.out, self.counts, self.marks = nc, ins, out, counts, marks

    def stage(self, name):
        return Stage(self.nc, name, self.counts, self.marks)

    def build(self, upto=None):
        nc = self.nc
        with ExitStack() as ctx:
            sb = lambda n, s, d=F32: ctx.enter_context(nc.sbuf_tensor(n, s, d))
            self.cols = sb("cols", [P, NCOLS])
            self.consts = sb("consts", [P, NCONST])
            self.mod = sb("mod", [P, 48])
            self.xh = sb("xh", [P, KT, T], F32R)
            self.xl = sb("xl", [P, KT, T], F32R)
            self.xt_dram = nc.dram_tensor("xt_scratch", (P, KT, T), F32).ap()
            self.h_dram = nc.dram_tensor("h_scratch", (T, D), F32).ap()
            self.y_dram = nc.dram_tensor("y_scratch", (NBLK * P, D), F32).ap()
            self.tok_dram = nc.dram_tensor("token_of_slot", ((NBLK + 1) * P, 1), F32).ap()
            with nc.sbuf_tensor("x_first", [P, KT, T], F32) as self.x:
                self.prepare()
            self.mixer_in()
            self.ssd()
            self.gate_norm()
            self.x = sb("x_res", [P, KT, T])
            self.acc_sq = sb("acc_sq", [P, T])
            self.dense_out("mixout", self.ins["w_out"], reload=True, gate=slice(16, 24))
            self.route()
            self.experts()
            self.combine()
            self.attention_in()
            self.attention()
            self.dense_out("attout", self.ins["swa_w_out"])
            self.feed_forward()
            self.finish()

    def col(self, name, k=0, n=1):
        a = COLS[name].start + k
        return self.cols[:, a:a + n]

    def const(self, name, rows=P):
        return self.consts[0:rows, CONSTS[name]]

    def rstd(self, st, sq_sum, total, rstd, name="rstd", after=None):
        def pe(e):
            after(e)
            for h in range(0, T, HALF):
                m = e.matmul(total[:, h:h + HALF], self.const("ones"), sq_sum[:, h:h + HALF], start=True, stop=True)
            st.pe(m, name + "_sum")

        def dve(e):
            st.wait(e, st.pe, name + "_sum")
            st.dve(e.tensor_scalar(rstd[:, :], total[:, :], 1.0 / D, EPS, ALU.mult, ALU.add))
            st.dve.settle()
            st.dve(e.reciprocal(rstd[:, :], rstd[:, :]), name + "_inv")

        def act(e):
            st.wait(e, st.dve, name + "_inv")
            st.act(e.activation(rstd[:, :], rstd[:, :], ACT.Sqrt), name)
        return pe, dve, act

    def scale_split(self, st, rstd, scale, shift, tmp, rstd_name):
        lanes = {0: st.dve, 1: st.dve if shift is not None else st.pool}

        def lo(e, k):
            st.wait(e, st.act, f"hi{k}")
            hi, out, t = self.xh[:, k, :].bitcast(F32), self.xl[:, k, :], tmp[:, k % 4, :]
            if shift is None:
                ins = e.tensor_tensor(out, t, hi, ALU.subtract)
            else:
                ins = e.scalar_tensor_tensor(out, t, shift[:, k:k + 1], hi, ALU.add, ALU.subtract)
            lanes[k % 2](ins, f"lo{k}")

        def dve(e):
            for k in range(KT + 1):
                if k < KT:
                    if k >= 4:
                        st.wait(e, lanes[k % 2], f"lo{k - 4}")
                    elif k == 0:
                        st.wait(e, st.act, rstd_name)
                    st.dve(e.scalar_tensor_tensor(tmp[:, k % 4, :], self.x[:, k, :], scale[:, k:k + 1], rstd[:, :],
                                                  ALU.mult, ALU.mult), f"scaled{k}")
                if k >= 1 and lanes[(k - 1) % 2] is st.dve:
                    lo(e, k - 1)

        def act(e):
            for k in range(KT):
                st.wait(e, st.dve, f"scaled{k}")
                if shift is None:
                    st.act(e.activation(self.xh[:, k, :], tmp[:, k % 4, :], ACT.Copy), f"hi{k}")
                else:
                    st.act(e.activation(self.xh[:, k, :], tmp[:, k % 4, :], ACT.Identity, bias=shift[:, k:k + 1]), f"hi{k}")

        def pool(e):
            for k in range(1, KT, 2) if shift is None else ():
                lo(e, k)
        return dve, act, pool

    def sum_squares(self, st, sq, acc, ready=None):
        def act(e):
            ready(e)
            for k in range(KT):
                if k >= 2:
                    st.wait(e, st.dve, f"sq_added{k - 2}")
                st.act(e.activation(sq[:, k % 2, :], self.x[:, k, :], ACT.Square), f"sq{k}")

        def dve(e):
            for k in range(KT):
                st.wait(e, st.act, f"sq{k}")
                if k == 0:
                    st.dve(e.tensor_copy(acc[:, :], sq[:, 0, :]), "sq_added0")
                else:
                    st.dve.settle()
                    st.dve(e.tensor_tensor(acc[:, :], acc[:, :], sq[:, k % 2, :], ALU.add), f"sq_added{k}")
        return act, dve

    def prepare(self):
        ins, ones = self.ins, self.const("ones")
        with self.stage("prep") as st:
            xtok = st.sb("xtok", [P, 2, D])
            wa = st.sb("wa", [P, 2, KT * P])
            sc = st.sb("silu_c", [P, KT])
            sq, acc, rstd, tmp = st.sb("sq", [P, 2, T]), st.sb("acc", [P, T]), st.sb("rstd", [P, T]), st.sb("tmp", [P, 4, T])
            turned = [st.ps(f"turned{b}", [P, D]) for b in range(2)]
            pm = [st.ps(f"mod{b}", [P, HALF]) for b in range(2)]
            total = st.ps("total", [P, T])
            s_cols, s_out = st.sem("cols"), st.sem("xt_out")
            s_x, s_wa = [st.sem(f"x{b}") for b in range(2)], [st.sem(f"wa{b}") for b in range(2)]
            rstd_pe, rstd_dve, rstd_act = self.rstd(st, acc, total, rstd, after=lambda e: st.wait(e, st.dve, "sq_added7"))
            sq_act, sq_dve = self.sum_squares(st, sq, acc, ready=lambda e: st.wait(e, st.act, "xt1"))
            sc_dve, sc_act, sc_pool = self.scale_split(st, rstd, self.mod[:, 8:16], self.mod[:, 0:8], tmp, "rstd")
            with st.block() as blk:
                @blk.sync
                def _(e):
                    e.dma_start(self.cols[:, :], ins["cols"]).then_inc(s_cols, 16)
                    e.dma_start(self.consts[:, :], ins["consts"]).then_inc(s_cols, 16)
                    with e.Fori(0, NT // 2) as i:
                        for b in range(2):
                            st.wait(e, st.pe, f"turn{b}", i - 1)
                            e.dma_start(xtok[:, b, :], ins["x"][2 * i + b]).then_inc(s_x[b], 16)
                    with e.Fori(0, 24) as i:
                        for b in range(2):
                            st.wait(e, st.pe, f"ada{b}", i - 1)
                            e.dma_start(wa[:, b, :], ins["w_ada"][2 * i + b]).then_inc(s_wa[b], 16)
                    st.wait(e, st.act, "xt1")
                    e.dma_start(self.xt_dram, self.x[:, :, :]).then_inc(s_out, 16)
                    e.wait_ge(s_out, 16)

                @blk.tensor
                def _(e):
                    st.pe.start(e)
                    e.wait_ge(s_cols, 32)
                    with st.pe.loop(NT // 2) as i:
                        for b in range(2):
                            e.wait_ge(s_x[b], 16 * i + 16)
                            st.wait(e, st.act, f"xt{b}", i - 1)
                            for k in range(KT):
                                m = e.transpose(turned[b][:, k * P:(k + 1) * P], xtok[:, b, k * P:(k + 1) * P], self.const("ident"))
                            st.pe(m, f"turn{b}")
                    st.wait(e, st.act, "silu_c")
                    with st.pe.loop(24) as i:
                        for b in range(2):
                            e.wait_ge(s_wa[b], 16 * i + 16)
                            st.wait(e, st.dve, f"mod{b}", i - 1)
                            for k in range(KT):
                                m = e.matmul(pm[b][:, 0:1], wa[:, b, k * P:(k + 1) * P], sc[:, k:k + 1], start=(k == 0), stop=(k == KT - 1))
                            st.pe(m, f"ada{b}")
                    rstd_pe(e)

                @blk.scalar
                def _(e):
                    st.act.start(e)
                    e.wait_ge(s_cols, 32)
                    st.act(e.activation(sc[:, :], self.col("c", 0, KT), ACT.Silu), "silu_c")
                    with st.act.loop(NT // 2) as i:
                        for b in range(2):
                            st.wait(e, st.pe, f"turn{b}", i)
                            st.act(e.activation(self.x[:, :, bass.ds(2 * P * i + P * b, P)],
                                                turned[b][:, :].rearrange("p (k t) -> p k t", t=P), ACT.Copy), f"xt{b}")
                    sq_act(e)
                    rstd_act(e)
                    sc_act(e)

                @blk.vector
                def _(e):
                    st.dve.start(e)
                    e.wait_ge(s_cols, 32)
                    sq_dve(e)
                    with st.dve.loop(24) as i:
                        for b in range(2):
                            st.wait(e, st.pe, f"ada{b}", i)
                            n = 2 * i + b
                            st.dve(e.tensor_tensor(self.mod[:, bass.ds(n, 1)], pm[b][:, 0:1],
                                                   self.cols[:, bass.ds(2 * i + (COLS["b_ada"].start + b), 1)], ALU.add), f"mod{b}")
                    st.dve.settle()
                    for a in (8, 32):
                        st.dve(e.tensor_scalar(self.mod[:, a:a + 8], self.mod[:, a:a + 8], 1.0, None, ALU.add))
                    rstd_dve(e)
                    sc_dve(e)

                @blk.gpsimd
                def _(e):
                    st.pool.start(e)
                    sc_pool(e)

    def mixer_in(self):
        ins, nc = self.ins, self.nc
        self.keep = ExitStack()
        sb = lambda n, s: self.keep.enter_context(nc.sbuf_tensor(n, s, F32))
        self.xbc = sb("xbc", [P, CONV_T, T])
        self.zs = sb("zs", [P, SSD_T, T])
        self.acs_row = sb("acs_row", [HEADS, T])
        self.dt_tok = sb("dt_tok", [P, NCH * HEADS])
        self.acs_tok = sb("acs_tok", [P, NCH * HEADS])
        PAD = 16
        with self.stage("in") as st:
            g = Gemm(st)
            raw = st.sb("raw", [P, 2, PAD + T])
            wrk = st.sb("wrk", [P, 2, PAD + T])
            wpool = st.sb("wpool", [P, POOL_T, P])
            dta_tok = st.sb("dta_tok", [P, NCH * HEADS])
            nega = st.sb("nega", [HEADS, 1])
            s_wp = st.sem("wp")
            turn = st.ps("turn", [P, 2 * HALF])
            mix = [st.ps(f"mix{b}", [P, HALF]) for b in range(2)]
            W = ins["w_in"]
            cw, cb = COLS["conv_w"].start, COLS["conv_b"].start
            N_SILU, N_Z = CONV_T // 2, SSD_T // 2
            BZ, BD = CONV_T, CONV_T + SSD_T
            TAIL = [(0, BD), (1, BD), (0, BD + 2)]
            with st.block() as blk:
                @blk.sync
                def _(e):
                    e.dma_start(wpool[:, :, :], ins["w_pool"]).then_inc(s_wp, 16)
                    with e.Fori(0, N_SILU + N_Z) as i:
                        for b in range(2):
                            g.load(e, i, 0, b, W[2 * i + b])
                    for j, (b, base) in enumerate(TAIL):
                        g.load(e, 0, base, b, W[BD + j])

                @blk.gpsimd
                def _(e):
                    st.pool.start(e)
                    e.sem_inc(g.s_split, 2)
                    with e.Fori(0, N_SILU + N_Z) as i:
                        for b in range(2):
                            g.split(e, i, 0, b)
                    for b, base in TAIL:
                        g.split(e, 0, base, b)

                @blk.tensor
                def _(e):
                    st.pe.start(e)
                    e.sem_inc(g.s_mult, 2)
                    with e.Fori(0, N_SILU + N_Z) as i:
                        for b in range(2):
                            g.mult(e, i, 0, b, self.xh, self.xl)
                    for b, base in TAIL:
                        g.mult(e, 0, base, b, self.xh, self.xl)
                    ident = self.consts[0:HEADS, 0:HEADS]
                    for src, at in ((0, 0), (1, HALF)):
                        st.wait(e, st.dve, "dt" if src == 0 else "dta")
                        for c in range(NCH):
                            m = e.transpose(turn[:, at + c * HEADS:at + (c + 1) * HEADS],
                                            wrk[0:HEADS, src, c * CH:(c + 1) * CH], ident)
                        st.pe(m, f"dt_turned{src}")
                    st.wait(e, st.dve, "dta_tok")
                    m = e.matmul(mix[0][:, 0:NCH * HEADS], self.const("upto"), dta_tok[:, :], start=True, stop=True)
                    st.pe(m, "acs_tok")
                    for c in range(NCH):
                        m = e.matmul(turn[0:HEADS, c * CH:(c + 1) * CH], dta_tok[:, c * HEADS:(c + 1) * HEADS],
                                     self.const("upto"), start=True, stop=True)
                    st.pe(m, "acs_row")
                    e.wait_ge(s_wp, 16)
                    for j in range(POOL_T):
                        st.wait(e, st.dve, f"pool_diff{j}")
                        for h in range(2):
                            if j == 0 and h == 0:
                                st.wait(e, st.act, "acs_tok")
                            if j:
                                st.wait(e, st.dve, f"pool_lo{j - 1}{h}")
                            m = e.matmul(mix[h][:, :], wpool[:, j, :], raw[:, 1 - j, PAD + h * HALF:PAD + (h + 1) * HALF],
                                         start=True, stop=True)
                            st.pe(m, f"pool{j}{h}")

                @blk.scalar
                def _(e):
                    st.act.start(e)
                    with st.act.loop(N_SILU) as i:
                        for b in range(2):
                            g.ready(e, i, 0, b)
                            if b == 0:
                                st.wait(e, st.dve, "zeros")
                            st.wait(e, st.dve, f"conv{b}", i - 1)
                            g.empty(e.activation(raw[:, b, PAD:PAD + T], g.acc[b][:, :], ACT.Copy))
                            st.wait(e, st.dve, f"conv{b}", i)
                            st.act(e.activation(tile_of(self.xbc, i, b), wrk[:, b, 0:T], ACT.Silu), f"xbc{b}")
                    with st.act.loop(N_Z) as i:
                        for b in range(2):
                            g.ready(e, i, BZ, b)
                            g.empty(e.activation(tile_of(self.zs, i, b), g.acc[b][:, :], ACT.Silu))
                    g.ready(e, 0, BD, 0)
                    bias = self.cols[0:HEADS, COLS["dt_bias"]]
                    e1, v = raw[0:HEADS, 1, PAD:PAD + T], wrk[0:HEADS, 1, 0:T]
                    st.act(e.activation(nega[:, :], self.cols[0:HEADS, COLS["a_log"]], ACT.Exp), "exp_a")
                    st.act.settle()
                    g.empty(e.activation(v, g.acc[0][0:HEADS, :], ACT.Identity, bias=bias))
                    g.emptied(e, 0, BD, 0)
                    st.act(e.activation(e1, v, ACT.Abs))
                    st.act.settle()
                    st.act(e.activation(e1, e1, ACT.Exp, scale=-1.0), "dt_e")
                    st.wait(e, st.dve, "dt_u")
                    st.act(e.activation(raw[0:HEADS, 0, PAD:PAD + T], wrk[0:HEADS, 0, 0:T], ACT.Ln), "dt_ln")
                    for j in range(POOL_T):
                        b, base = TAIL[1 + j]
                        g.ready(e, 0, base, b)
                        if j == 0:
                            st.wait(e, st.dve, "dt")
                        g.empty(e.activation(raw[:, 1 - j, PAD:PAD + T], g.acc[b][:, :], ACT.Copy))
                    st.wait(e, st.pe, "acs_tok")
                    st.act(e.activation(self.acs_tok[:, :], mix[0][:, 0:NCH * HEADS], ACT.Copy), "acs_tok")
                    st.wait(e, st.pe, "acs_row")
                    st.act(e.activation(self.acs_row[:, :], turn[0:HEADS, :], ACT.Copy), "acs_row")
                    g.ready(e, 0, BD + 2, 0)
                    for j in range(POOL_T):
                        for h in range(2):
                            st.wait(e, st.pe, f"pool{j}{h}")
                            st.act(e.activation(self.xh[:, j, h * HALF:(h + 1) * HALF], mix[h][:, :], ACT.Copy,
                                                scale=self.col("pool_scale", j)), f"pool_hi{j}{h}")

                @blk.vector
                def _(e):
                    st.dve.start(e)
                    e.sem_inc(g.s_emptied, 2)
                    st.dve(e.memset(raw[:, :, 0:PAD], 0.0), "zeros")
                    with st.dve.loop(N_SILU) as i:
                        for b in range(2):
                            g.emptied(e, i, 0, b)
                            st.wait(e, st.act, f"xbc{b}", i - 1)
                            at = i * (2 * CONV) + (cw + b * CONV)
                            taps = [self.cols[:, bass.ds(at + j, 1)] for j in range(CONV)]
                            bias = self.cols[:, bass.ds(2 * i + (cb + b), 1)]
                            if b == 0:
                                st.dve.settle()
                            a = wrk[:, b, 0:T]
                            st.dve(e.tensor_scalar(a, raw[:, b, PAD:PAD + T], taps[3], bias, ALU.mult, ALU.add))
                            for j in (2, 1, 0):
                                st.dve.settle()
                                s = PAD - 3 + j
                                st.dve(e.scalar_tensor_tensor(a, raw[:, b, s:s + T], taps[j], a, ALU.mult, ALU.add),
                                       f"conv{b}" if j == 0 else None)
                    st.wait(e, st.act, "dt_e")
                    e1, v = raw[0:HEADS, 1, PAD:PAD + T], wrk[0:HEADS, 1, 0:T]
                    u, t, ln = wrk[0:HEADS, 0, 0:T], self.acs_row[:, :], raw[0:HEADS, 0, PAD:PAD + T]
                    st.dve(e.tensor_scalar(u, e1, 1.0, None, ALU.add), "dt_u")
                    st.dve.settle()
                    st.dve(e.scalar_tensor_tensor(t, u, -1.0, e1, ALU.add, ALU.subtract))
                    st.wait(e, st.act, "dt_ln")
                    st.dve(e.reciprocal(u, u))
                    st.dve.settle()
                    st.dve(e.tensor_tensor(t, t, u, ALU.mult))
                    st.dve.settle()
                    st.dve(e.tensor_tensor(ln, ln, t, ALU.subtract))
                    st.dve.settle()
                    st.dve(e.scalar_tensor_tensor(u, v, 0.0, ln, ALU.max, ALU.add), "dt")
                    st.dve(e.tensor_scalar(nega[:, :], nega[:, :], -1.0, None, ALU.mult))
                    st.dve.settle()
                    st.dve(e.tensor_scalar(v, u, nega[:, 0:1], None, ALU.mult), "dta")
                    for src, dst in ((0, self.dt_tok), (1, dta_tok)):
                        st.wait(e, st.pe, f"dt_turned{src}")
                        at = src * HALF
                        st.dve(e.tensor_copy(dst[:, :], turn[:, at:at + NCH * HEADS]), "dta_tok" if src else "dt_tok")
                    W_ = PAD + T
                    for j in range(POOL_T):
                        g.emptied(e, 0, TAIL[1 + j][1], TAIL[1 + j][0])
                        uu, s, r = raw[:, 1 - j, :], wrk[:, 0, :], wrk[:, 1, :]
                        if j == 1:
                            st.dve.settle()
                        st.dve(e.tensor_tensor(s[:, 1:W_], uu[:, 1:W_], uu[:, 0:W_ - 1], ALU.add))
                        st.dve.settle()
                        st.dve(e.tensor_tensor(r[:, 3:W_], s[:, 3:W_], s[:, 1:W_ - 2], ALU.add))
                        if j == 1:
                            st.dve.settle()
                            st.dve(e.tensor_tensor(s[:, 7:W_], r[:, 7:W_], r[:, 3:W_ - 4], ALU.add))
                            st.dve.settle()
                            st.dve(e.tensor_tensor(r[:, 15:W_], s[:, 15:W_], s[:, 7:W_ - 8], ALU.add))
                        st.dve.settle()
                        for half, src in ((0, s), (1, r)):
                            rows = slice(64 * half, 64 * half + 64)
                            first = self.consts[rows, CONSTS["pool_first"].start + 16 * j:CONSTS["pool_first"].start + 16 * j + 16]
                            inv = self.consts[rows, CONSTS["pool_inv"].start + j:CONSTS["pool_inv"].start + j + 1]
                            st.dve(e.tensor_tensor(src[rows, PAD:PAD + 16], src[rows, PAD:PAD + 16], first, ALU.mult))
                            st.dve.settle()
                            st.dve(e.scalar_tensor_tensor(uu[rows, PAD:W_], src[rows, PAD:W_], inv, uu[rows, PAD:W_],
                                                          ALU.mult, ALU.subtract), f"pool_diff{j}" if half else None)
                    for j in range(POOL_T):
                        for h in range(2):
                            st.wait(e, st.act, f"pool_hi{j}{h}")
                            cs = slice(h * HALF, (h + 1) * HALF)
                            st.dve(e.scalar_tensor_tensor(self.xl[:, j, cs], mix[h][:, :], self.col("pool_scale", j),
                                                          self.xh[:, j, cs].bitcast(F32), ALU.mult, ALU.subtract), f"pool_lo{j}{h}")

    def ssd(self):
        ins, xbc = self.ins, self.xbc
        with self.stage("ssd") as st:
            sel = st.sb("sel", [HEADS, HEADS * P])
            stg = st.sb("stg", [P, 10, CH])
            xdt = st.sb("xdt", [P, HEADS * HD])
            xdte = st.sb("xdte", [P, HEADS * HD])
            btok = st.sb("btok", [P, GROUPS * STATE])
            m = st.sb("m", [P, HEADS * CH])
            ce = st.sb("ce", [P, HEADS * CH])
            cbm = st.sb("cbm", [P, GROUPS * CH])
            state = st.sb("state", [P, HEADS * HD])
            dte, cdec = st.sb("dte", [P, HEADS]), st.sb("cdec", [P, HEADS])
            xy = st.ps("xy", [P, 2 * HALF])
            bt = st.ps("bt", [P, HALF])
            cb = st.ps("cb", [P, HALF])
            bc = st.ps("bc", [P, 3 * HALF])
            s_sel, s_fill = st.sem("sel"), st.sem("fill")
            zeros = st.sb("zeros", [P, D])
            heads = lambda a, n: a[:, :].rearrange("p (h n) -> p h n", n=n)
            groups = lambda a, n: a[:, :].rearrange("p (g r n) -> p g r n", r=HPG, n=n)
            per_head = lambda a, n: a.unsqueeze(2).to_broadcast([P, HEADS, n])
            chunk = lambda a, c: a[:, bass.ds(c * HEADS, HEADS)]
            new_states = bc[:, 0:2 * HALF].rearrange("p (b x) -> p b x", x=HALF)[:, :, 0:2 * HPG * HD]
            with st.block() as blk:
                @blk.sync
                def _(e):
                    e.dma_start(sel[:, :], ins["sel"]).then_inc(s_sel, 16)
                    st.wait(e, st.dve, "zeros")
                    with e.Fori(2 * T // P, NBLK) as i:
                        e.dma_start(self.y_dram[bass.ds(i * P, P), :], zeros[:, :]).then_inc(s_fill, 16)
                    e.wait_ge(s_fill, 16 * (NBLK - 2 * T // P))

                @blk.gpsimd
                def _(e):
                    st.pool.start(e)
                    with st.pool.loop(NCH) as c:
                        st.wait(e, st.pe, "cb", c - 1)
                        e.nop(nofuse=True)
                        st.pool(e.tensor_copy(stg[:, :, :], xbc[:, 0:10, bass.ds(c * CH, CH)]), "staged")
                        st.wait(e, st.dve, "min", c)
                        st.pool(e.tensor_tensor(heads(m, CH), heads(m, CH), per_head(chunk(self.acs_tok, c), CH), ALU.subtract), "seg")
                        st.wait(e, st.act, "dte", c)
                        st.wait(e, st.dve, "xdt", c)
                        st.pool(e.tensor_tensor(heads(xdte, HD), heads(xdt, HD), per_head(dte[:, :], HD), ALU.mult), "xdte")

                @blk.tensor
                def _(e):
                    st.pe.start(e)
                    e.wait_ge(s_sel, 16)
                    with st.pe.loop(NCH) as c:
                        st.wait(e, st.pool, "staged", c)
                        st.wait(e, st.act, "y_out", c - 1)
                        for j in range(SSD_T):
                            k = e.transpose(xy[:, j * P:(j + 1) * P], stg[:, j, :], self.const("ident"))
                        st.pe(k, "x_turned")
                        st.wait(e, st.act, "btok", c - 1)
                        for g in range(GROUPS):
                            k = e.transpose(bt[:, g * P:(g + 1) * P], stg[:, SSD_T + g, :], self.const("ident"))
                        st.pe(k, "b_turned")
                        st.wait(e, st.dve, "cbm", c - 1)
                        for g in range(GROUPS):
                            k = e.matmul(cb[:, g * CH:(g + 1) * CH], stg[:, SSD_T + g, :],
                                         xbc[:, 10 + g, bass.ds(c * CH, CH)], start=True, stop=True)
                        st.pe(k, "cb")
                        st.wait(e, st.dve, "state", c - 1)
                        for h in range(HEADS):
                            k = e.matmul(bc[:, h * CH:(h + 1) * CH], sel[:, h * P:(h + 1) * P],
                                         self.acs_row[:, bass.ds(c * CH, CH)], start=True, stop=True)
                        st.pe(k, "bc")
                        st.wait(e, st.dve, "xdt", c)
                        st.wait(e, st.dve, "ce", c)
                        st.wait(e, st.dve, "m", c)
                        for h in range(HEADS):
                            o = xy[64 * (h % 2):64 * (h % 2) + 64, (h // 2) * CH:(h // 2 + 1) * CH]
                            e.matmul(o, xdt[:, h * HD:(h + 1) * HD], m[:, h * CH:(h + 1) * CH], start=True, stop=False)
                            k = e.matmul(o, state[:, h * HD:(h + 1) * HD], ce[:, h * CH:(h + 1) * CH], start=False, stop=True)
                        st.pe(k, "y")
                        st.wait(e, st.pool, "xdte", c)
                        st.wait(e, st.act, "btok", c)
                        w = HPG * HD
                        for g in range(GROUPS):
                            at = (g // 2) * HALF + (g % 2) * w
                            k = e.matmul(bc[:, at:at + w], btok[:, g * P:(g + 1) * P], xdte[:, g * w:(g + 1) * w], start=True, stop=True)
                        st.pe(k, "states")

                @blk.scalar
                def _(e):
                    st.act.start(e)
                    with st.act.loop(NCH) as c:
                        st.wait(e, st.pe, "b_turned", c)
                        st.act(e.activation(btok[:, :], bt[:, :], ACT.Copy), "btok")
                        st.wait(e, st.dve, "dte_arg", c)
                        st.act(e.activation(ce[:, :], bc[:, :], ACT.Exp), "exp_bc")
                        st.act(e.activation(dte[:, :], dte[:, :], ACT.Exp), "dte")
                        st.wait(e, st.dve, "decayed", c - 1)
                        st.act.settle()
                        st.act(e.activation(cdec[:, :], heads(ce, CH)[:, :, CH - 1], ACT.Copy), "cdec")
                        st.wait(e, st.pool, "seg", c)
                        st.act(e.activation(m[:, :], m[:, :], ACT.Exp), "exp_seg")
                        st.wait(e, st.pe, "y", c)
                        st.act(e.activation(xbc[:, SSD_T:2 * SSD_T, bass.ds(c * CH, CH)],
                                            xy[:, 0:SSD_T * P].rearrange("p (j t) -> p j t", t=CH), ACT.Copy), "y_out")

                @blk.vector
                def _(e):
                    st.dve.start(e)
                    st.dve(e.memset(state[:, :], 0.0), "zero")
                    st.dve(e.memset(zeros[:, :], 0.0), "zeros")
                    mask = self.const("upto").unsqueeze(1).to_broadcast([P, GROUPS, CH])
                    with st.dve.loop(NCH) as c:
                        st.wait(e, st.pe, "x_turned", c)
                        st.dve(e.tensor_tensor(heads(xdt, HD), xy[:, 0:HEADS * HD].rearrange("p (h n) -> p h n", n=HD),
                                               per_head(chunk(self.dt_tok, c), HD), ALU.mult), "xdt")
                        st.wait(e, st.pe, "bc", c)
                        st.dve(e.tensor_tensor(heads(m, CH), heads(bc, CH), per_head(chunk(self.acs_tok, c), CH), ALU.min), "min")
                        st.dve(e.tensor_tensor(dte[:, :], heads(bc, CH)[:, :, CH - 1], chunk(self.acs_tok, c), ALU.subtract), "dte_arg")
                        st.dve(e.tensor_tensor(heads(cbm, CH), heads(cb, CH), mask, ALU.mult), "cbm")
                        st.wait(e, st.act, "cdec", c)
                        for g in range(GROUPS):
                            a = ce[:, g * HPG * CH:(g + 1) * HPG * CH].rearrange("p (r n) -> p r n", n=CH)
                            cT = xbc[:, 10 + g, bass.ds(c * CH, CH)].unsqueeze(1).to_broadcast([P, HPG, CH])
                            st.dve(e.tensor_tensor(a, a, cT, ALU.mult), "ce" if g == GROUPS - 1 else None)
                        st.wait(e, st.act, "exp_seg", c)
                        st.dve.settle()
                        st.dve(e.tensor_tensor(groups(m, CH), groups(m, CH),
                                               heads(cbm, CH).unsqueeze(2).to_broadcast([P, GROUPS, HPG, CH]), ALU.mult), "m")
                        st.wait(e, st.pe, "y", c)
                        st.dve(e.tensor_tensor(heads(state, HD), heads(state, HD), per_head(cdec[:, :], HD), ALU.mult), "decayed")
                        st.wait(e, st.pe, "states", c)
                        st.dve.settle()
                        s2 = state[:, :].rearrange("p (b x) -> p b x", b=2)
                        st.dve(e.tensor_tensor(s2, s2, new_states, ALU.add), "state")

    def gate_norm(self):
        xbc, zs = self.xbc, self.zs
        with self.stage("gate") as st:
            same = st.sb("same", [P, 7, P])
            rstd, tmp = st.sb("rstd", [P, T]), st.sb("tmp", [P, 2, T])
            total = [st.ps(f"total{b}", [P, T]) for b in range(2)]
            s_same = st.sem("same")
            PAIRS = [(0, 0), (1, 0), (0, 1), (1, 1), (2, 1), (1, 2), (2, 2)]
            with st.block() as blk:
                @blk.sync
                def _(e):
                    e.dma_start(same[:, :, :], self.ins["same"]).then_inc(s_same, 16)

                @blk.tensor
                def _(e):
                    st.pe.start(e)
                    e.wait_ge(s_same, 16)
                    for j in range(SSD_T):
                        mine = [(n, a) for n, (a, o) in enumerate(PAIRS) if o == j % 3]
                        for h in range(0, T, HALF):
                            for x, (n, a) in enumerate(mine):
                                src = 3 * (j // 3) + a
                                if h == 0:
                                    st.wait(e, st.act, f"sq{src}")
                                    if j >= 2 and x == 0:
                                        st.wait(e, st.dve, f"mean{j - 2}")
                                k = e.matmul(total[j % 2][:, h:h + HALF], same[:, n, :], zs[:, src, h:h + HALF],
                                             start=(x == 0), stop=(x == len(mine) - 1))
                        st.pe(k, f"total{j}")

                @blk.scalar
                def _(e):
                    st.act.start(e)
                    for j in range(SSD_T):
                        st.wait(e, st.dve, f"gated{j}")
                        st.act(e.activation(zs[:, j, :], xbc[:, SSD_T + j, :], ACT.Square), f"sq{j}")
                    for j in range(SSD_T):
                        st.wait(e, st.dve, f"inv{j}")
                        st.act(e.activation(rstd[:, :], rstd[:, :], ACT.Sqrt), f"rstd{j}")
                        st.wait(e, st.dve, f"normed{j}")
                        st.act(e.activation(self.xh[:, POOL_T + j, :], tmp[:, j % 2, :], ACT.Copy), f"hi{j}")

                @blk.gpsimd
                def _(e):
                    st.pool.start(e)
                    for j in range(SSD_T):
                        st.wait(e, st.act, f"hi{j}")
                        st.pool(e.tensor_tensor(self.xl[:, POOL_T + j, :], tmp[:, j % 2, :],
                                                self.xh[:, POOL_T + j, :].bitcast(F32), ALU.subtract), f"lo{j}")

                @blk.vector
                def _(e):
                    st.dve.start(e)
                    for j in range(SSD_T):
                        y = xbc[:, SSD_T + j, :]
                        st.dve(e.scalar_tensor_tensor(y, xbc[:, j, :], self.col("d_skip", j), y, ALU.mult, ALU.add))
                        st.dve.settle()
                        st.dve(e.tensor_tensor(y, y, zs[:, j, :], ALU.mult), f"gated{j}")
                    for j in range(SSD_T):
                        st.wait(e, st.pe, f"total{j}")
                        st.dve.settle()
                        st.dve(e.tensor_scalar(rstd[:, :], total[j % 2][:, :], GROUPS / (SSD_T * P), EPS, ALU.mult, ALU.add), f"mean{j}")
                        st.dve.settle()
                        st.dve(e.reciprocal(rstd[:, :], rstd[:, :]), f"inv{j}")
                        st.wait(e, st.act, f"rstd{j}")
                        if j >= 2:
                            st.wait(e, st.pool, f"lo{j - 2}")
                        st.dve(e.scalar_tensor_tensor(tmp[:, j % 2, :], xbc[:, SSD_T + j, :], self.col("ssd_norm_w", j),
                                                      rstd[:, :], ALU.mult, ALU.mult), f"normed{j}")
        self.keep.close()

    def dense_out(self, name, W, reload=False, gate=None):
        x, acc = self.x, self.acc_sq
        with self.stage(name) as st:
            g = Gemm(st)
            sq = st.sb("sq", [P, 2, T])
            s_x = st.sem("x")
            with st.block() as blk:
                @blk.sync
                def _(e):
                    with e.Fori(0, KT // 2) as i:
                        for b in range(2):
                            g.load(e, i, 0, b, W[2 * i + b])

                @blk.gpsimd
                def _(e):
                    st.pool.start(e)
                    e.sem_inc(g.s_split, 2)
                    with e.Fori(0, KT // 2) as i:
                        for b in range(2):
                            g.split(e, i, 0, b)

                @blk.tensor
                def _(e):
                    st.pe.start(e)
                    e.sem_inc(g.s_mult, 2)
                    with e.Fori(0, KT // 2) as i:
                        for b in range(2):
                            g.mult(e, i, 0, b, self.xh, self.xl)

                @blk.scalar
                def _(e):
                    st.act.start(e)
                    if reload:
                        e.dma_start(x[:, :, :], self.xt_dram).then_inc(s_x, 16)
                    with st.act.loop(KT // 2) as i:
                        for b in range(2):
                            g.emptied(e, i, 0, b)
                            st.wait(e, st.dve, f"added{b}", i - 1)
                            st.act(e.activation(sq[:, b, :], tile_of(x, i, b), ACT.Square), f"sq{b}")

                @blk.vector
                def _(e):
                    st.dve.start(e)
                    e.sem_inc(g.s_emptied, 2)
                    st.dve(e.memset(acc[:, :], 0.0))
                    if reload:
                        e.wait_ge(s_x, 16)
                    with st.dve.loop(KT // 2) as i:
                        for b in range(2):
                            g.ready(e, i, 0, b)
                            xn = tile_of(x, i, b)
                            if gate is None:
                                g.empty(e.tensor_tensor(xn, g.acc[b][:, :], xn, ALU.add))
                            else:
                                s = self.mod[:, bass.ds(2 * i + (gate.start + b), 1)]
                                g.empty(e.scalar_tensor_tensor(xn, g.acc[b][:, :], s, xn, ALU.mult, ALU.add))
                            st.wait(e, st.act, f"sq{b}", i)
                            st.dve.settle()
                            st.dve(e.tensor_tensor(acc[:, :], acc[:, :], sq[:, b, :], ALU.add), f"added{b}")

    def route(self):
        ins, nc, x = self.ins, self.nc, self.x
        self.rkeep = ExitStack()
        sb = lambda n, s, d=F32: self.rkeep.enter_context(nc.sbuf_tensor(n, s, d))
        self.slots = sb("slots", [P, 2 * NT], I32)
        self.gates = sb("gates", [P, 2 * NT])
        self.blocks = sb("blocks", [P, NBLK + 2], I32)
        self.rows = sb("rows", [P, NBLK + 1], I32)
        R = EG + NE
        with self.stage("route") as st:
            rstd, hst = st.sb("rstd", [P, T]), st.sb("hst", [P, 2, KT * P])
            htok = st.sb("htok", [P, 2, D])
            wr = st.sb("wr", [P, KT, R])
            lg = st.sb("lg", [P, NT, R])
            zeros = st.sb("zeros", [P, NBLK + 1])
            total = st.ps("total", [P, T])
            turned = [st.ps(f"turned{b}", [P, D]) for b in range(2)]
            pl = [st.ps(f"logits{b}", [P, HALF]) for b in range(2)]
            s_wr, s_zero, s_scatter, s_rows = (st.sem(n) for n in ("wr", "zero", "scatter", "rows"))
            s_h = [st.sem(f"h{b}") for b in range(2)]
            rstd_pe, rstd_dve, rstd_act = self.rstd(st, self.acc_sq, total, rstd, after=lambda e: None)
            t3 = lambda a, k=KT: a.rearrange("p (k t) -> p k t", k=k)
            table = st.sb("table", [NBLK + 1, P])
            W = {}
            def buf(name, *shape):
                n = int(np.prod(shape))
                if name not in W:
                    W[name] = st.sb(name, [P, n])
                a = W[name][:, 0:n]
                if len(shape) == 2:
                    return a.rearrange("p (a b) -> p a b", b=shape[1])
                if len(shape) == 3:
                    return a.rearrange("p (a b c) -> p a b c", b=shape[1], c=shape[2])
                return a
            both_ = lambda st: buf("both", NT * NE)
            g_exp = lambda st: buf("g_exp", NT, EG)
            e_exp = lambda st: buf("e_exp", NT)
            for n, w in (("both", NT * NE), ("g_exp", NT * EG), ("e_exp", NT)):
                buf(n, w)
            with st.block() as blk:
                @blk.sync
                def _(e):
                    for b in range(2):
                        e.sem_inc(s_h[b], 16)
                    e.dma_start(wr[:, :, :], ins["w_route"]).then_inc(s_wr, 16)
                    st.wait(e, st.dve, "zeros")
                    e.dma_start(self.tok_dram.rearrange("(p n) a -> p (n a)", p=P), zeros[:, :]).then_inc(s_zero, 16)
                    with e.Fori(0, NT // 2) as i:
                        for b in range(2):
                            st.wait(e, st.act, f"htok{b}", i)
                            e.dma_start(self.h_dram[bass.ds(2 * P * i + P * b, P), :], htok[:, b, :]).then_inc(s_h[b], 16)
                    for b in range(2):
                        e.wait_ge(s_h[b], 16 * (NT // 2) + 16)
                    e.wait_ge(s_scatter, 16 * 2 * NT)
                    e.dma_start(table[:, :], self.tok_dram.rearrange("(n p) a -> n (p a)", p=P)).then_inc(s_rows, 16)

                @blk.tensor
                def _(e):
                    st.pe.start(e)
                    rstd_pe(e)
                    e.wait_ge(s_wr, 16)
                    with st.pe.loop(NT // 2) as i:
                        for b in range(2):
                            st.wait(e, st.pool, f"h{b}", i)
                            st.wait(e, st.act, f"htok{b}", i - 1)
                            for k in range(KT):
                                e.transpose(turned[b][:, k * P:(k + 1) * P], hst[:, b, k * P:(k + 1) * P], self.const("ident"))
                            st.wait(e, st.dve, f"logits{b}", i - 1)
                            for k in range(KT):
                                m = e.matmul(pl[b][:, 0:R], hst[:, b, k * P:(k + 1) * P], wr[:, k, :], start=(k == 0), stop=(k == KT - 1))
                            st.pe(m, f"used{b}")
                    st.wait(e, st.dve, "chosen")
                    e.matmul(total[:, 0:NT * NE], self.const("before"), both_(st), start=True, stop=True)
                    m = e.matmul(total[:, HALF:HALF + NT * NE], self.const("ones"), both_(st), start=True, stop=True)
                    st.pe(m, "ranked")
                    e.wait_ge(s_rows, 16)
                    m = e.transpose(pl[0][:, 0:NBLK + 1], table[:, :], self.consts[0:NBLK + 1, 0:NBLK + 1])
                    st.pe(m, "rows")

                @blk.scalar
                def _(e):
                    st.act.start(e)
                    rstd_act(e)
                    with st.act.loop(NT // 2) as i:
                        for b in range(2):
                            st.wait(e, st.pe, f"used{b}", i)
                            e.wait_ge(s_h[b], 16 * i + 16)
                            st.act(e.activation(htok[:, b, :], turned[b][:, :], ACT.Copy), f"htok{b}")
                    st.wait(e, st.dve, "g_arg")
                    st.act(e.activation(g_exp(st), g_exp(st), ACT.Exp), "g_exp")
                    st.wait(e, st.dve, "e_arg")
                    st.act(e.activation(e_exp(st), e_exp(st), ACT.Exp), "e_exp")

                @blk.gpsimd
                def _(e):
                    st.pool.start(e)
                    shift = self.mod[:, 24:32].unsqueeze(2).to_broadcast([P, KT, P])
                    with st.pool.loop(NT // 2) as i:
                        for b in range(2):
                            st.wait(e, st.dve, f"scaled{b}", i)
                            st.pool(e.tensor_tensor(t3(hst[:, b, :]), t3(hst[:, b, :]), shift, ALU.add), f"h{b}")
                    st.wait(e, st.dve, "slots")
                    e.wait_ge(s_zero, 16)
                    e.nop(nofuse=True)
                    tokid = self.const("tokid")
                    for n in range(2 * NT):
                        e.indirect_dma_start(out=self.tok_dram, out_offset=bass.IndirectOffsetOnAxis(ap=self.slots[:, n:n + 1], axis=0),
                                             in_=tokid[:, n % NT:n % NT + 1], in_offset=None).then_inc(s_scatter, 16)

                @blk.vector
                def _(e):
                    dve = st.dve
                    dve.start(e)
                    dve(e.memset(zeros[:, :], 0.0), "zeros")
                    rstd_dve(e)
                    st.wait(e, st.act, "rstd")
                    scale = self.mod[:, 32:40].unsqueeze(2).to_broadcast([P, KT, P])
                    with dve.loop(NT // 2) as i:
                        for b in range(2):
                            ts = bass.ds(2 * P * i + P * b, P)
                            st.wait(e, st.pe, f"used{b}", i - 1)
                            dve(e.tensor_tensor(t3(hst[:, b, :]), x[:, :, ts], rstd[:, ts].unsqueeze(1).to_broadcast([P, KT, P]), ALU.mult))
                            dve.settle()
                            dve(e.tensor_tensor(t3(hst[:, b, :]), t3(hst[:, b, :]), scale, ALU.mult), f"scaled{b}")
                            st.wait(e, st.pe, f"used{b}", i)
                            dve(e.tensor_tensor(tile_of(lg, i, b), pl[b][:, 0:R], self.cols[:, COLS["router_b"]], ALU.add), f"logits{b}")

                    def do(ins, name=None):
                        dve(ins, name)
                        dve.settle()

                    def over(a, *shape):
                        return a.to_broadcast([P, *shape])
                    iota8 = self.const("iota8")

                    def first_largest(v, n, onehot, most):
                        eq, low = buf(f"eq{n}", NT, n), buf("low", NT)
                        do(e.tensor_reduce(most, v, AX.X, ALU.max))
                        do(e.tensor_tensor(eq, v, over(most.unsqueeze(2), NT, n), ALU.is_equal))
                        do(e.scalar_tensor_tensor(eq, eq, -64.0, over(iota8[:, 0:n].unsqueeze(1), NT, n), ALU.mult, ALU.add))
                        do(e.tensor_reduce(low, eq, AX.X, ALU.min))
                        do(e.tensor_tensor(onehot, eq, over(low.unsqueeze(2), NT, n), ALU.is_equal))

                    dve.settle()
                    g_one, g_most = buf("g_one", NT, EG), buf("g_most", NT)
                    first_largest(lg[:, :, 0:EG], EG, g_one, g_most)
                    do(e.tensor_tensor(g_exp(st), lg[:, :, 0:EG], over(g_most.unsqueeze(2), NT, EG), ALU.subtract), "g_arg")
                    el = lg[:, :, EG:].rearrange("p t (g x) -> p t g x", g=EG)
                    prod, within = buf("prod", NT, EG, EPG), buf("within", NT, EPG)
                    g_wide = over(g_one.unsqueeze(3), NT, EG, EPG)
                    do(e.tensor_tensor(prod, el, g_wide, ALU.mult))
                    do(e.tensor_reduce(within, prod.rearrange("p t g x -> p t x g"), AX.X, ALU.add))
                    one, most = [buf(f"one{k}", NT, EPG) for k in range(2)], [buf(f"most{k}", NT) for k in range(2)]
                    first_largest(within, EPG, one[0], most[0])
                    do(e.scalar_tensor_tensor(within, one[0], -BIG, within, ALU.mult, ALU.add))
                    first_largest(within, EPG, one[1], most[1])
                    do(e.tensor_tensor(e_exp(st), most[1], most[0], ALU.subtract), "e_arg")
                    hot = [buf(f"hot{k}", NT, EG, EPG) for k in range(2)]
                    for k in range(2):
                        do(e.tensor_tensor(hot[k], over(one[k].unsqueeze(2), NT, EG, EPG), g_wide, ALU.mult))
                    flat = [buf(f"hot{k}", NT * NE) for k in range(2)]
                    do(e.tensor_tensor(buf("both", NT * NE), flat[0], flat[1], ALU.add), "chosen")
                    psum_, pg, den = buf("g_sum", NT), buf("pg", NT), buf("den", NT)
                    st.wait(e, st.act, "g_exp")
                    do(e.tensor_reduce(psum_, g_exp(st), AX.X, ALU.add))
                    st.wait(e, st.act, "e_exp")
                    do(e.tensor_scalar(den, e_exp(st), 1.0, None, ALU.add))
                    do(e.tensor_tensor(den, den, psum_, ALU.mult))
                    do(e.reciprocal(self.gates[:, 0:NT], den))
                    do(e.tensor_tensor(self.gates[:, NT:], self.gates[:, 0:NT], e_exp(st), ALU.mult))
                    st.wait(e, st.pe, "ranked")
                    rank, tot = buf("rank", NT, NE), buf("tot", NT, NE)
                    upto, cnt = buf("before_tile", NT, NE), buf("cnt", NE)
                    do(e.tensor_copy(tot, total[:, HALF:HALF + NT * NE].rearrange("p (t x) -> p t x", x=NE)))
                    do(e.memset(upto[:, 0, :], 0.0))
                    for t in range(1, NT):
                        do(e.tensor_tensor(upto[:, t, :], upto[:, t - 1, :], tot[:, t - 1, :], ALU.add))
                    do(e.tensor_tensor(cnt, upto[:, NT - 1, :], tot[:, NT - 1, :], ALU.add))
                    do(e.tensor_tensor(rank, total[:, 0:NT * NE].rearrange("p (t x) -> p t x", x=NE), upto, ALU.add))
                    more, nb = buf("more", NE, NT), buf("nb", NE)
                    do(e.tensor_tensor(more, over(cnt.unsqueeze(2), NE, NT), over(self.const("iota8x128").unsqueeze(1), NE, NT), ALU.is_gt))
                    do(e.tensor_reduce(nb, more, AX.X, ALU.add))
                    run = [buf("run0", NE), buf("run1", NE)]
                    do(e.tensor_copy(run[0], nb))
                    for n, w in enumerate((1, 2, 4, 8, 16)):
                        a, o = run[n % 2], run[1 - n % 2]
                        do(e.tensor_copy(o[:, 0:w], a[:, 0:w]))
                        do(e.tensor_tensor(o[:, w:], a[:, w:], a[:, 0:NE - w], ALU.add))
                    end, start = run[1], buf("start", NE)
                    do(e.tensor_tensor(start, end, nb, ALU.subtract))
                    do(e.tensor_scalar(start, start, float(P), None, ALU.mult))
                    do(e.tensor_tensor(rank, rank, over(start.unsqueeze(1), NT, NE), ALU.add))
                    slot = buf("slot", 2, NT)
                    for k in range(2):
                        do(e.tensor_tensor(flat[k], flat[k], buf("rank", NT * NE), ALU.mult))
                        do(e.tensor_reduce(slot[:, k, :], buf(f"hot{k}", NT, NE), AX.X, ALU.add))
                    do(e.tensor_copy(self.slots[:, :], buf("slot", 2 * NT)), "slots")
                    ended, expert = buf("ended", NBLK + 1, NE), buf("expert", NBLK + 1)
                    do(e.tensor_tensor(ended, over(end.unsqueeze(1), NBLK + 1, NE), over(self.const("iotab").unsqueeze(2), NBLK + 1, NE), ALU.is_le))
                    do(e.tensor_reduce(expert, ended, AX.X, ALU.add))
                    do(e.tensor_scalar(expert, expert, float(NE - 1), None, ALU.min))
                    do(e.tensor_copy(self.blocks[:, 0:NBLK + 1], expert))
                    do(e.tensor_copy(self.blocks[:, NBLK + 1:], end[:, NE - 1:NE]))
                    st.wait(e, st.pe, "rows")
                    do(e.tensor_copy(self.rows[:, :], pl[0][:, 0:NBLK + 1]))

    def experts(self):
        ins = self.ins
        U, RING = KT + FF // P, 6
        with self.stage("moe") as st:
            raw = st.sb("raw", [P, U, D])
            hi, lo = self.xh, self.xl
            xt = [a[:, RING, :] for a in (hi, lo)]
            at = [a[:, RING + 1, 0:FF] for a in (hi, lo)]
            xg = st.sb("xg", [P, D])
            idx = st.sb("idx", [P, 1], I32)
            sg, act_ = st.sb("sg", [P, FF]), st.sb("act", [P, FF])
            ysb = st.sb("ysb", [P, D])
            hu, yp, xturn = st.ps("hu", [P, 2 * FF]), st.ps("y", [P, D]), st.ps("xturn", [P, D])
            aturn = st.ps("aturn", [P, FF])
            s_w = [st.sem(f"w{u}") for u in range(U)]
            s_g, s_y = st.sem("gathered"), st.sem("y_out")
            blocks = lambda e: e.value_load(self.blocks[0:1, NBLK + 1:NBLK + 2], min_val=2 * T // P, max_val=NBLK)
            with st.block() as blk:
                @blk.sync
                def _(e):
                    n = blocks(e)
                    with e.Fori(0, NBLK) as i:
                        with e.If(i < n):
                            ex = e.value_load(self.blocks[0:1, bass.ds(i, 1)], min_val=0, max_val=NE - 1)
                            for u in range(U):
                                st.wait(e, st.dve, f"lo{u}", i - 1)
                                src = ins["w13"][ex, u * P:(u + 1) * P, :] if u < KT else ins["w2"][ex, (u - KT) * P:(u - KT + 1) * P, :]
                                e.dma_start(raw[:, u, :], src).then_inc(s_w[u], 16)

                @blk.gpsimd
                def _(e):
                    st.pool.start(e)
                    n = blocks(e)

                    def gather(name, i=None):
                        e.nop(nofuse=True)
                        st.pool(e.tensor_copy(idx[:, :], self.rows[:, 0:1] if i is None else self.rows[:, bass.ds(i + 1, 1)]), name)
                        st.pool.settle()
                        e.nop(nofuse=True)
                        e.indirect_dma_start(out=xg[:, :], out_offset=None, in_=self.h_dram,
                                             in_offset=bass.IndirectOffsetOnAxis(ap=idx[:, 0:1], axis=0)).then_inc(s_g, 16)
                    gather("idx_first")
                    st.wait(e, st.pe, "x_first")
                    with st.pool.loop(NBLK) as i:
                        with e.If(i < n):
                            e.wait_ge(s_g, 16 * i + 16)
                            st.wait(e, st.pe, "x_turned", i - 1)
                            gather("idx", i)

                @blk.tensor
                def _(e):
                    st.pe.start(e)
                    n = blocks(e)

                    def turn_x():
                        for k in range(KT):
                            m = e.transpose(xturn[:, k * P:(k + 1) * P], xg[:, k * P:(k + 1) * P], self.const("ident"))
                        return m

                    def product(i, u, x, k, out):
                        st.wait(e, st.dve, f"lo{u}", i)
                        r = u % RING
                        last = (u == KT - 1) or (u == U - 1)
                        first = u in (0, KT)
                        for h in range(0, D, HALF):
                            for t, (a, w) in enumerate(((x[0], hi), (x[0], lo), (x[1], hi))):
                                m = e.matmul(out[:, h:h + HALF], a[:, k * P:(k + 1) * P], w[:, r, h:h + HALF],
                                             start=first and t == 0, stop=last and t == 2)
                        st.pe(m, f"mm{u}")
                    e.wait_ge(s_g, 16)
                    st.pe(turn_x(), "x_first")
                    st.wait(e, st.dve, "x_lo_first")
                    with st.pe.loop(NBLK) as i:
                        with e.If(i < n):
                            st.wait(e, st.dve, "x_lo", i - 1)
                            for u in range(KT):
                                product(i, u, xt, u, hu)
                            e.wait_ge(s_g, 16 * i + 32)
                            st.pe(turn_x(), "x_turned")
                            st.wait(e, st.dve, "act", i)
                            for k in range(FF // P):
                                m = e.transpose(aturn[:, k * P:(k + 1) * P], act_[:, k * P:(k + 1) * P], self.const("ident"))
                            st.pe(m, "a_turned")
                            st.wait(e, st.dve, "a_lo", i)
                            st.wait(e, st.act, "y0", i - 1)
                            st.wait(e, st.dve, "y1", i - 1)
                            for u in range(KT, U):
                                product(i, u, at, u - KT, yp)

                @blk.scalar
                def _(e):
                    st.act.start(e)
                    n = blocks(e)
                    e.sem_inc(s_y, 16)

                    def high(i, u):
                        e.wait_ge(s_w[u], 16 * i + 16)
                        prev, j = (u - RING, i) if u >= RING else (u + RING, i - 1)
                        st.wait(e, st.pe, f"mm{prev}", j)
                        st.act(e.activation(hi[:, u % RING, :], raw[:, u, :], ACT.Copy), f"hi{u}")
                    st.wait(e, st.pe, "x_first")
                    st.act(e.activation(xt[0], xturn[:, :], ACT.Copy), "x_hi_first")
                    with st.act.loop(NBLK) as i:
                        with e.If(i < n):
                            for u in range(10):
                                high(i, u)
                            st.wait(e, st.pe, "mm7", i)
                            st.act(e.activation(sg[:, :], hu[:, 0:FF], ACT.Silu), "silu")
                            st.wait(e, st.pe, "x_turned", i)
                            st.act(e.activation(xt[0], xturn[:, :], ACT.Copy), "x_hi")
                            st.wait(e, st.pe, "a_turned", i)
                            st.act(e.activation(at[0], aturn[:, :], ACT.Copy), "a_hi")
                            for u in range(10, U):
                                high(i, u)
                            st.wait(e, st.pe, f"mm{U - 1}", i)
                            e.wait_ge(s_y, 16 * i + 16)
                            st.act(e.activation(ysb[:, 0:HALF], yp[:, 0:HALF], ACT.Copy), "y0")
                            st.wait(e, st.dve, "y1", i)
                            st.act.settle()
                            e.dma_start(self.y_dram[bass.ds(i * P, P), :], ysb[:, :]).then_inc(s_y, 16)
                    e.wait_ge(s_y, 16 * n + 16)
                    e.nop(nofuse=True)

                @blk.vector
                def _(e):
                    st.dve.start(e)
                    n = blocks(e)

                    def low(i, u):
                        st.wait(e, st.act, f"hi{u}", i)
                        r = u % RING
                        st.dve(e.tensor_tensor(lo[:, r, :], raw[:, u, :], hi[:, r, :].bitcast(F32), ALU.subtract), f"lo{u}")
                    st.wait(e, st.act, "x_hi_first")
                    st.dve(e.tensor_tensor(xt[1], xturn[:, :], xt[0].bitcast(F32), ALU.subtract), "x_lo_first")
                    with st.dve.loop(NBLK) as i:
                        with e.If(i < n):
                            for u in range(10):
                                low(i, u)
                            st.wait(e, st.act, "silu", i)
                            st.dve(e.tensor_tensor(act_[:, :], sg[:, :], hu[:, FF:2 * FF], ALU.mult), "act")
                            st.wait(e, st.act, "x_hi", i)
                            st.dve(e.tensor_tensor(xt[1], xturn[:, :], xt[0].bitcast(F32), ALU.subtract), "x_lo")
                            st.wait(e, st.act, "a_hi", i)
                            st.dve(e.tensor_tensor(at[1], aturn[:, :], at[0].bitcast(F32), ALU.subtract), "a_lo")
                            for u in range(10, U):
                                low(i, u)
                            st.wait(e, st.pe, f"mm{U - 1}", i)
                            e.wait_ge(s_y, 16 * i + 16)
                            st.dve(e.tensor_copy(ysb[:, HALF:], yp[:, HALF:]), "y1")

    def combine(self):
        x = self.x
        with self.stage("comb") as st:
            ys = [st.sb(f"y{k}", [P, 2, D]) for k in range(2)]
            idx = st.sb("idx", [P, 4], I32)
            sq, tmp = st.sb("sq", [P, 2, KT * P]), st.sb("tmp", [P, KT * P])
            turned = [st.ps(f"turned{b}", [P, D]) for b in range(2)]
            s_g = [st.sem(f"g{b}") for b in range(2)]
            t3 = lambda a: a.rearrange("p (k t) -> p k t", k=KT)
            gate = self.mod[:, 40:48].unsqueeze(2).to_broadcast([P, KT, P])
            with st.block() as blk:
                @blk.gpsimd
                def _(e):
                    st.pool.start(e)
                    with st.pool.loop(NT // 2) as i:
                        for b in range(2):
                            st.wait(e, st.pe, f"turned{b}", i - 1)
                            e.nop(nofuse=True)
                            for k in range(2):
                                st.pool(e.tensor_copy(idx[:, 2 * b + k:2 * b + k + 1], self.slots[:, bass.ds(2 * i + (b + k * NT), 1)]))
                            st.pool.settle()
                            e.nop(nofuse=True)
                            for k in range(2):
                                e.indirect_dma_start(out=ys[k][:, b, :], out_offset=None, in_=self.y_dram,
                                                     in_offset=bass.IndirectOffsetOnAxis(ap=idx[:, 2 * b + k:2 * b + k + 1], axis=0)).then_inc(s_g[b], 16)

                @blk.tensor
                def _(e):
                    st.pe.start(e)
                    with st.pe.loop(NT // 2) as i:
                        for b in range(2):
                            st.wait(e, st.dve, f"mixed{b}", i)
                            st.wait(e, st.dve, f"gated{b}", i - 1)
                            for k in range(KT):
                                m = e.transpose(turned[b][:, k * P:(k + 1) * P], ys[0][:, b, k * P:(k + 1) * P], self.const("ident"))
                            st.pe(m, f"turned{b}")

                @blk.scalar
                def _(e):
                    st.act.start(e)
                    with st.act.loop(NT // 2) as i:
                        for b in range(2):
                            ts = bass.ds(2 * P * i + P * b, P)
                            st.wait(e, st.dve, f"x{b}", i)
                            st.wait(e, st.dve, f"sum{b}", i - 1)
                            st.act(e.activation(t3(sq[:, b, :]), x[:, :, ts], ACT.Square), f"sq{b}")

                @blk.vector
                def _(e):
                    st.dve.start(e)
                    with st.dve.loop(NT // 2) as i:
                        for b in range(2):
                            ts = bass.ds(2 * P * i + P * b, P)
                            g = [self.gates[:, bass.ds(2 * i + (b + k * NT), 1)] for k in range(2)]
                            y0, y1 = (y[:, b, :] for y in ys)
                            e.wait_ge(s_g[b], 32 * i + 32)
                            st.dve(e.tensor_scalar(y0, y0, g[0], None, ALU.mult))
                            st.dve.settle()
                            st.dve(e.scalar_tensor_tensor(y0, y1, g[1], y0, ALU.mult, ALU.add), f"mixed{b}")
                            st.wait(e, st.pe, f"turned{b}", i)
                            st.dve(e.tensor_tensor(t3(tmp[:, :]), t3(turned[b][:, :]), gate, ALU.mult), f"gated{b}")
                            st.dve.settle()
                            st.dve(e.tensor_tensor(x[:, :, ts], x[:, :, ts], t3(tmp[:, :]), ALU.add), f"x{b}")
                            st.wait(e, st.act, f"sq{b}", i)
                            st.dve(e.tensor_reduce(self.acc_sq[:, ts], sq[:, b, :].rearrange("p (k t) -> p t k", k=KT), AX.X, ALU.add), f"sum{b}")
        self.rkeep.close()

    def attention_in(self):
        self.keep = ExitStack()
        with self.stage("renorm") as st:
            rstd, tmp, sq = st.sb("rstd", [P, T]), st.sb("tmp", [P, 4, T]), st.sb("sq", [P, 2, T])
            total = st.ps("total", [P, T])
            pe1, dve1, act1 = self.rstd(st, self.acc_sq, total, rstd, "rstd_a", after=lambda e: None)
            sq_act, sq_dve = self.sum_squares(st, sq, self.acc_sq, ready=lambda e: st.wait(e, st.dve, "normed"))
            pe2, dve2, act2 = self.rstd(st, self.acc_sq, total, rstd, "rstd_b", after=lambda e: st.wait(e, st.dve, "sq_added7"))
            sc_dve, sc_act, sc_pool = self.scale_split(st, rstd, self.col("norm_mix", 0, KT), None, tmp, "rstd_b")
            with st.block() as blk:
                @blk.tensor
                def _(e):
                    st.pe.start(e)
                    pe1(e)
                    pe2(e)

                @blk.scalar
                def _(e):
                    st.act.start(e)
                    act1(e)
                    sq_act(e)
                    act2(e)
                    sc_act(e)

                @blk.gpsimd
                def _(e):
                    st.pool.start(e)
                    sc_pool(e)

                @blk.vector
                def _(e):
                    st.dve.start(e)
                    dve1(e)
                    st.wait(e, st.act, "rstd_a")
                    for k in range(KT):
                        st.dve(e.scalar_tensor_tensor(self.x[:, k, :], self.x[:, k, :], self.col("final_norm_w", k), rstd[:, :],
                                                      ALU.mult, ALU.mult), "normed" if k == KT - 1 else None)
                    sq_dve(e)
                    st.dve.settle()
                    dve2(e)
                    sc_dve(e)
        QKV = (Q_HEADS + 2 * KV_HEADS) * HD // P
        self.qkv = self.keep.enter_context(self.nc.sbuf_tensor("qkv", [P, QKV, T], F32))
        with self.stage("qkv") as st:
            g = Gemm(st)
            with st.block() as blk:
                @blk.sync
                def _(e):
                    with e.Fori(0, QKV // 2) as i:
                        for b in range(2):
                            g.load(e, i, 0, b, self.ins["w_qkv"][2 * i + b])

                @blk.gpsimd
                def _(e):
                    e.sem_inc(g.s_split, 2)
                    with e.Fori(0, QKV // 2) as i:
                        for b in range(2):
                            g.split(e, i, 0, b)

                @blk.tensor
                def _(e):
                    e.sem_inc(g.s_mult, 2)
                    with e.Fori(0, QKV // 2) as i:
                        for b in range(2):
                            g.mult(e, i, 0, b, self.xh, self.xl)

                @blk.scalar
                def _(e):
                    e.sem_inc(g.s_emptied, 2)
                    with e.Fori(0, QKV // 2) as i:
                        for b in range(2):
                            g.ready(e, i, 0, b)
                            g.empty(e.activation(tile_of(self.qkv, i, b), g.acc[b][:, :], ACT.Copy))

    def attention(self):
        qkv, QT, G4 = self.qkv, Q_HEADS * HD // P, Q_HEADS // KV_HEADS
        K0, V0 = QT, QT + 2
        with self.stage("att") as st:
            bias = st.sb("bias", [P, Q_HEADS, 2 * P])
            dist = st.sb("dist", [P, 2, 2 * P])
            qs, ks, vs = st.sb("qs", [P, QT, P]), st.sb("ks", [P, 2, 2 * P]), st.sb("vs", [P, 2, P])
            vtok = st.sb("vtok", [P, NT, KV_HEADS * HD])
            p = st.sb("p", [P, 2, G4 * 2 * P])
            pt = st.sb("pt", [P, 2, G4 * 2 * P])
            mx, sums = st.sb("mx", [P, 2, G4]), st.sb("sums", [P, Q_HEADS])
            esink = st.sb("esink", [P, Q_HEADS])
            osb = st.sb("osb", [P, Q_HEADS * HD])
            sc = [st.ps(f"scores{b}", [P, G4 * 2 * P]) for b in range(2)]
            tp = st.ps("turned", [P, 2 * HALF])
            op = st.ps("o", [P, Q_HEADS * HD])
            s_dist = st.sem("dist")
            mask_slopes = [2.0 ** (-8.0 * (h + 1) / Q_HEADS) for h in range(Q_HEADS)]

            def sync(e):
                e.dma_start(dist[:, :, :], self.ins["dist"]).then_inc(s_dist, 16)

            def cols(n, first, lead=0):
                return slice(0, P) if first else bass.ds(n * P, P)

            def pool_body(e, n, first, tag):
                keys = slice(P, 2 * P) if first else slice(0, 2 * P)
                src = slice(0, P) if first else bass.ds(n * P - P, 2 * P)
                e.nop(nofuse=True)
                st.pool(e.tensor_copy(vs[:, :, :], qkv[:, V0:V0 + 2, cols(n, first)]), tag + "vs")
                st.pool(e.tensor_copy(ks[:, :, keys], qkv[:, K0:K0 + 2, src]))
                st.pool(e.tensor_copy(qs[:, :, :], qkv[:, 0:QT, cols(n, first)]), tag + "qs")

            def wide(first):
                return slice(P, 2 * P) if first else slice(0, 2 * P)

            def pe_scores(e, n, j, tag, first, idx, nprev):
                b = j % 2
                nprev(e, j)
                half, jj = 64 * (j % 2), j // 2
                for h in range(G4):
                    m = e.matmul(sc[b][:, h * 2 * P:(h + 1) * 2 * P][:, wide(first)], qs[half:half + 64, G4 * jj + h, :],
                                 ks[half:half + 64, jj, wide(first)], start=True, stop=True)
                st.pe(m, tag + f"scores{j}")

            def pe_body(e, n, first, tag):
                i = None if first else n - 1
                im1 = None if first else n - 2

                def before(e, j):
                    if j >= 2:
                        st.wait(e, st.dve, tag + f"scored{j - 2}", i)
                    elif not first:
                        st.wait(e, st.dve, "first_scored%d" % (j + 2))
                        st.wait(e, st.dve, tag + f"scored{j + 2}", im1)
                st.wait(e, st.pool, tag + "vs", i)
                if not first:
                    st.wait(e, st.dve, "first_o_lo")
                    st.wait(e, st.dve, tag + "o_lo", im1)
                for k in range(2):
                    m = e.transpose(tp[:, k * P:(k + 1) * P], vs[:, k, :], self.const("ident"))
                st.pe(m, tag + "v_turned")
                st.wait(e, st.pool, tag + "qs", i)
                pe_scores(e, n, 0, tag, first, i, before)
                for j in range(KV_HEADS):
                    b = j % 2
                    if j + 1 < KV_HEADS:
                        pe_scores(e, n, j + 1, tag, first, i, before)
                    st.wait(e, st.act, tag + f"exp{j}", i)
                    if j == 0:
                        st.wait(e, st.act, tag + "vtok", i)
                    else:
                        st.wait(e, st.act, tag + f"pt_a{j - 1}", i)
                        st.wait(e, st.dve, tag + f"pt_b{j - 1}", i)
                    blocks = [(h, w) for h in range(G4) for w in ((1,) if first else (0, 1))]
                    for h, w in blocks:
                        m = e.transpose(tp[:, (2 * h + w) * P:(2 * h + w + 1) * P],
                                        p[:, b, (2 * h + w) * P:(2 * h + w + 1) * P], self.const("ident"))
                    st.pe(m, tag + f"p_turned{j}")
                    st.wait(e, st.act, tag + f"pt_a{j}", i)
                    st.wait(e, st.dve, tag + f"pt_b{j}", i)
                    if j == 0 and not first:
                        st.wait(e, st.dve, "first_o")
                        st.wait(e, st.dve, tag + "o", im1)
                    for h in range(G4):
                        o = op[:, (G4 * j + h) * HD:(G4 * j + h + 1) * HD]
                        for w in ((1,) if first else (0, 1)):
                            v = vtok[:, 0, j * HD:(j + 1) * HD] if first else \
                                vtok[:, bass.ds(n - 1 + w, 1), j * HD:(j + 1) * HD].rearrange("p a d -> p (a d)")
                            m = e.matmul(o, pt[:, b, (2 * h + w) * P:(2 * h + w + 1) * P], v, start=(first or w == 0), stop=(w == 1))
                    st.pe(m, tag + f"pv{j}")
                st.wait(e, st.dve, tag + "o", i)
                for k in range(QT):
                    m = e.transpose(tp[:, k * P:(k + 1) * P], osb[:, k * P:(k + 1) * P], self.const("ident"))
                st.pe(m, tag + "o_turned")

            def halves(a, b_, first, part):
                v = a.rearrange("p (h w q) -> p h w q", h=G4, w=2)[:, 2 * part:2 * part + 2]
                return v[:, :, 1, :] if first else v

            def act_body(e, n, first, tag):
                i = None if first else n - 1
                im1 = None if first else n - 2
                st.wait(e, st.pe, tag + "v_turned", i)
                dst = vtok[:, 0, :] if first else vtok[:, bass.ds(n, 1), :].rearrange("p a d -> p (a d)")
                st.act(e.activation(dst, tp[:, 0:2 * P], ACT.Copy), tag + "vtok")

                def exps(j):
                    b = j % 2
                    st.wait(e, st.dve, tag + f"neg{j}", i)
                    for h in range(G4):
                        a = p[:, b, h * 2 * P:(h + 1) * 2 * P][:, wide(first)]
                        st.act(e.activation(a, a, ACT.Exp, bias=mx[:, b, h:h + 1], accum_out=sums[:, G4 * j + h:G4 * j + h + 1]), tag + f"exp{j}")

                def pt_a(j):
                    b = j % 2
                    st.wait(e, st.pe, tag + f"p_turned{j}", i)
                    st.act(e.activation(halves(pt[:, b, :], 0, first, 0), halves(tp[:, :], 0, first, 0), ACT.Copy), tag + f"pt_a{j}")
                for j in range(KV_HEADS):
                    exps(j)
                    if j:
                        pt_a(j - 1)
                pt_a(KV_HEADS - 1)
                st.wait(e, st.dve, tag + "sink", i)
                st.act(e.activation(esink[:, :], esink[:, :], ACT.Exp), tag + "esink")
                st.wait(e, st.pe, tag + "o_turned", i)
                t3 = tp[:, :].rearrange("p (k t) -> p k t", k=KT)
                st.act(e.activation(self.xh[:, :, cols(n, first)], t3, ACT.Copy), tag + "o_hi")

            def dve_body(e, n, first, tag):
                i = None if first else n - 1

                def score(j):
                    b = j % 2
                    st.wait(e, st.pe, tag + f"scores{j}", i)
                    if j >= 2:
                        st.wait(e, st.pe, tag + f"p_turned{j - 2}", i)
                    v = lambda a: a.rearrange("p (h k) -> p h k", h=G4)[:, :, wide(first)]
                    st.dve(e.scalar_tensor_tensor(v(p[:, b, :]), v(sc[b][:, :]), HD ** -0.5,
                                                  bias[:, G4 * j:G4 * j + G4, wide(first)], ALU.mult, ALU.add), tag + f"scored{j}")
                    st.dve.settle()
                    if j >= 2:
                        st.wait(e, st.act, tag + f"exp{j - 2}", i)
                    elif not first:
                        st.wait(e, st.act, tag + f"exp{j + 2}", n - 2)
                    st.dve(e.tensor_reduce(mx[:, b, :], v(p[:, b, :]), AX.X, ALU.max))
                    st.dve.settle()
                    sink = self.cols[:, COLS["sinks"].start + G4 * j:COLS["sinks"].start + G4 * (j + 1)]
                    st.dve(e.tensor_tensor(mx[:, b, :], mx[:, b, :], sink, ALU.max))
                    st.dve.settle()
                    st.dve(e.tensor_scalar(mx[:, b, :], mx[:, b, :], -1.0, None, ALU.mult), tag + f"neg{j}")
                    st.dve.settle()
                    st.dve(e.tensor_tensor(esink[:, G4 * j:G4 * (j + 1)], mx[:, b, :], sink, ALU.add), tag + "sink")

                def pt_b(j):
                    b = j % 2
                    st.wait(e, st.pe, tag + f"p_turned{j}", i)
                    if j >= 2:
                        st.wait(e, st.pe, tag + f"pv{j - 2}", i)
                    st.dve(e.tensor_copy(halves(pt[:, b, :], 0, first, 1), halves(tp[:, :], 0, first, 1)), tag + f"pt_b{j}")
                score(0)
                for j in range(KV_HEADS):
                    if j + 1 < KV_HEADS:
                        score(j + 1)
                    pt_b(j)
                st.wait(e, st.act, tag + "esink", i)
                st.dve(e.tensor_tensor(sums[:, :], sums[:, :], esink[:, :], ALU.add))
                st.dve.settle()
                st.dve(e.reciprocal(sums[:, :], sums[:, :]))
                st.dve.settle()
                st.wait(e, st.pe, tag + f"pv{KV_HEADS - 1}", i)
                src = op[:, :].rearrange("p (s r h d) -> p s h r d", s=2, r=2, h=G4)
                den = sums[:, :].rearrange("p (s r h) -> p s h r", s=2, r=2, h=G4)
                dst = osb[:, :].rearrange("p (s h r d) -> p s h r d", s=2, h=G4, r=2)
                for s in range(2):
                    st.dve(e.tensor_tensor(dst[:, s], src[:, s], den[:, s].unsqueeze(3).to_broadcast([P, G4, 2, HD]), ALU.mult), tag + "o")
                st.wait(e, st.act, tag + "o_hi", i)
                t3 = tp[:, :].rearrange("p (k t) -> p k t", k=KT)
                st.dve(e.tensor_tensor(self.xl[:, :, cols(n, first)], t3, self.xh[:, :, cols(n, first)].bitcast(F32), ALU.subtract), tag + "o_lo")

            with st.block() as blk:
                blk.sync(sync)

                @blk.gpsimd
                def _(e):
                    st.pool.start(e)
                    pool_body(e, 0, True, "first_")
                    with st.pool.loop(NT - 1) as m:
                        st.wait(e, st.pe, "first_scores3")
                        st.wait(e, st.pe, "scores3", m - 1)
                        pool_body(e, m + 1, False, "")

                @blk.tensor
                def _(e):
                    st.pe.start(e)
                    pe_body(e, 0, True, "first_")
                    with st.pe.loop(NT - 1) as m:
                        pe_body(e, m + 1, False, "")

                @blk.scalar
                def _(e):
                    st.act.start(e)
                    act_body(e, 0, True, "first_")
                    with st.act.loop(NT - 1) as m:
                        act_body(e, m + 1, False, "")

                @blk.vector
                def _(e):
                    st.dve.start(e)
                    e.wait_ge(s_dist, 16)
                    for h in range(Q_HEADS):
                        st.dve(e.scalar_tensor_tensor(bias[:, h, :], dist[:, 0, :], mask_slopes[h], dist[:, 1, :], ALU.mult, ALU.add))
                    st.dve.settle()
                    dve_body(e, 0, True, "first_")
                    with st.dve.loop(NT - 1) as m:
                        dve_body(e, m + 1, False, "")
        self.keep.close()

    def feed_forward(self):
        x = self.x
        with self.stage("ffnorm") as st:
            rstd, tmp = st.sb("rstd", [P, T]), st.sb("tmp", [P, 4, T])
            total = st.ps("total", [P, T])
            pe1, dve1, act1 = self.rstd(st, self.acc_sq, total, rstd, after=lambda e: None)
            sc_dve, sc_act, sc_pool = self.scale_split(st, rstd, self.col("norm_ffn", 0, KT), None, tmp, "rstd")
            with st.block() as blk:
                @blk.tensor
                def _(e):
                    st.pe.start(e)
                    pe1(e)

                @blk.scalar
                def _(e):
                    st.act.start(e)
                    act1(e)
                    sc_act(e)

                @blk.gpsimd
                def _(e):
                    st.pool.start(e)
                    sc_pool(e)

                @blk.vector
                def _(e):
                    st.dve.start(e)
                    dve1(e)
                    sc_dve(e)
        with self.stage("ff") as st:
            g = Gemm(st)
            ah, al = st.sb("ah", [P, max(FF_PARTS), T], F32R), st.sb("al", [P, max(FF_PARTS), T], F32R)
            a, sq = st.sb("a", [P, T]), st.sb("sq", [P, T])
            parts, base, wide = [], 0, 0
            for n, w in enumerate(FF_PARTS):
                parts.append((n, w, wide, base, base + 2 * w))
                base += 2 * w + KT
                wide += w
            up, down = self.ins["w_up"], [self.ins[f"w_down{n}"] for n in range(len(FF_PARTS))]
            with st.block() as blk:
                @blk.sync
                def _(e):
                    for n, w, at, b_up, b_down in parts:
                        with e.Fori(0, w) as i:
                            for b in range(2):
                                g.load(e, i, b_up, b, up[2 * i + (2 * at + b)])
                        with e.Fori(0, KT // 2) as i:
                            for b in range(2):
                                g.load(e, i, b_down, b, down[n][2 * i + b], kt=w)

                @blk.gpsimd
                def _(e):
                    e.sem_inc(g.s_split, 2)
                    for n, w, at, b_up, b_down in parts:
                        with e.Fori(0, w) as i:
                            for b in range(2):
                                g.split(e, i, b_up, b)
                        with e.Fori(0, KT // 2) as i:
                            for b in range(2):
                                g.split(e, i, b_down, b, kt=w)

                @blk.tensor
                def _(e):
                    e.sem_inc(g.s_mult, 2)
                    for n, w, at, b_up, b_down in parts:
                        with e.Fori(0, w) as i:
                            for b in range(2):
                                g.mult(e, i, b_up, b, self.xh, self.xl)
                        st.wait(e, st.dve, f"a_lo{n}")
                        with e.Fori(0, KT // 2) as i:
                            for b in range(2):
                                g.mult(e, i, b_down, b, ah, al, kt=w)

                @blk.scalar
                def _(e):
                    st.act.start(e)
                    for n, w, at, b_up, b_down in parts:
                        e.wait_ge(g.s_mult, b_up + 2)
                        with st.act.loop(w) as i:
                            g.ready(e, i, b_up, 0)
                            g.emptied(e, i - 1, b_up, 1)
                            g.empty(e.activation(sq[:, :], g.acc[0][:, :], ACT.Silu))
                            g.emptied(e, i, b_up, 1)
                            st.act(e.activation(tile_of(ah, i, 0, 1), a[:, :], ACT.Copy), f"hi{n}")
                    with st.act.loop(KT // 2) as i:
                        for b in range(2):
                            g.emptied(e, i, parts[-1][4], b)
                            st.wait(e, st.dve, "sum1" if b == 0 else "sum0", i - 1 if b == 0 else i)
                            st.act(e.activation(sq[:, :], tile_of(x, i, b), ACT.Square), f"sq{b}")

                @blk.vector
                def _(e):
                    st.dve.start(e)
                    e.sem_inc(g.s_emptied, 2)
                    st.dve(e.memset(self.acc_sq[:, :], 0.0))
                    for n, w, at, b_up, b_down in parts:
                        with st.dve.loop(w) as i:
                            g.emptied(e, i, b_up, 0)
                            g.ready(e, i, b_up, 1)
                            st.dve.settle()
                            g.empty(e.tensor_tensor(a[:, :], sq[:, :], g.acc[1][:, :], ALU.mult))
                            st.wait(e, st.act, f"hi{n}", i)
                            g.emptied(e, i, b_up, 1)
                            st.dve(e.tensor_tensor(tile_of(al, i, 0, 1), a[:, :], tile_of(ah, i, 0, 1).bitcast(F32), ALU.subtract), f"a_lo{n}")
                        last = n == len(parts) - 1
                        with st.dve.loop(KT // 2) as i:
                            for b in range(2):
                                g.ready(e, i, b_down, b)
                                xn = tile_of(x, i, b)
                                g.empty(e.tensor_tensor(xn, g.acc[b][:, :], xn, ALU.add))
                                if last:
                                    st.wait(e, st.act, f"sq{b}", i)
                                    st.dve.settle()
                                    st.dve(e.tensor_tensor(self.acc_sq[:, :], self.acc_sq[:, :], sq[:, :], ALU.add), f"sum{b}")

    def finish(self):
        x = self.x
        with self.stage("out") as st:
            rstd, ost, otok = st.sb("rstd", [P, T]), st.sb("ost", [P, 2, KT * P]), st.sb("otok", [P, 2, D])
            total = st.ps("total", [P, T])
            turned = [st.ps(f"turned{b}", [P, D]) for b in range(2)]
            s_o = [st.sem(f"o{b}") for b in range(2)]
            pe1, dve1, act1 = self.rstd(st, self.acc_sq, total, rstd, after=lambda e: None)
            t3 = lambda a: a.rearrange("p (k t) -> p k t", k=KT)
            with st.block() as blk:
                @blk.sync
                def _(e):
                    for b in range(2):
                        e.sem_inc(s_o[b], 16)
                    with e.Fori(0, NT // 2) as i:
                        for b in range(2):
                            st.wait(e, st.act, f"otok{b}", i)
                            e.dma_start(self.out[bass.ds(2 * P * i + P * b, P), :], otok[:, b, :]).then_inc(s_o[b], 16)
                    for b in range(2):
                        e.wait_ge(s_o[b], 16 * (NT // 2) + 16)

                @blk.tensor
                def _(e):
                    st.pe.start(e)
                    pe1(e)
                    with st.pe.loop(NT // 2) as i:
                        for b in range(2):
                            st.wait(e, st.dve, f"scaled{b}", i)
                            st.wait(e, st.act, f"otok{b}", i - 1)
                            for k in range(KT):
                                m = e.transpose(turned[b][:, k * P:(k + 1) * P], ost[:, b, k * P:(k + 1) * P], self.const("ident"))
                            st.pe(m, f"turned{b}")

                @blk.scalar
                def _(e):
                    st.act.start(e)
                    act1(e)
                    with st.act.loop(NT // 2) as i:
                        for b in range(2):
                            st.wait(e, st.pe, f"turned{b}", i)
                            e.wait_ge(s_o[b], 16 * i + 16)
                            st.act(e.activation(otok[:, b, :], turned[b][:, :], ACT.Copy), f"otok{b}")

                @blk.vector
                def _(e):
                    st.dve.start(e)
                    dve1(e)
                    st.wait(e, st.act, "rstd")
                    w = self.col("final_norm", 0, KT).unsqueeze(2).to_broadcast([P, KT, P])
                    with st.dve.loop(NT // 2) as i:
                        for b in range(2):
                            ts = bass.ds(2 * P * i + P * b, P)
                            st.wait(e, st.pe, f"turned{b}", i - 1)
                            st.dve(e.tensor_tensor(t3(ost[:, b, :]), x[:, :, ts], rstd[:, ts].unsqueeze(1).to_broadcast([P, KT, P]), ALU.mult))
                            st.dve.settle()
                            st.dve(e.tensor_tensor(t3(ost[:, b, :]), t3(ost[:, b, :]), w, ALU.mult), f"scaled{b}")


def tiles(w, kt=None):
    K, N = w.shape
    return np.ascontiguousarray(w.reshape(K // P, P, N // P, P).transpose(2, 1, 0, 3)).reshape(N // P, P, K)


def layout(a):
    def per_tile(v):
        return v.reshape(-1, P).T
    f = np.float32
    first = a["w_in"][0]
    u, z, xbc, dt = np.split(first, [256, 1024, 2816], axis=1)
    pad = np.zeros((D, P - HEADS), f)
    heads = np.arange(Q_HEADS).reshape(2, 2, 4).transpose(0, 2, 1).reshape(-1)
    qcols = (heads[:, None] * HD + np.arange(HD)).reshape(-1)
    wqkv = a["swa_w_in_2"][0]
    wqkv = np.concatenate([wqkv[:, :Q_HEADS * HD][:, qcols], wqkv[:, Q_HEADS * HD:]], axis=1)
    gu = a["ffn_w_gate_up_2"][0]
    gu = gu.reshape(D, 2, FFT, P).transpose(0, 2, 1, 3).reshape(D, -1)
    cols = np.zeros((P, NCOLS), f)
    cols[:, COLS["b_ada"]] = per_tile(a["b_ada"][0])
    cols[:, COLS["c"]] = per_tile(a["c"][0])
    cols[:, COLS["conv_w"]] = a["conv_w"][0].reshape(CONV, CONV_T, P).transpose(2, 1, 0).reshape(P, -1)
    cols[:, COLS["conv_b"]] = per_tile(a["conv_b"][0])
    cols[:, COLS["d_skip"]] = per_tile(np.repeat(a["d_skip"][0], HD))
    cols[:, COLS["pool_scale"]] = per_tile(a["pool_scale"][0])
    cols[:, COLS["ssd_norm_w"]] = per_tile(a["ssd_norm_w"][0])
    cols[:, COLS["final_norm_w"]] = per_tile(a["final_norm_w"])
    cols[:, COLS["norm_mix"]] = per_tile(a["norm_mix_2"][0])
    cols[:, COLS["norm_ffn"]] = per_tile(a["norm_ffn_2"][0])
    cols[:, COLS["final_norm"]] = per_tile(a["final_norm_2"])
    cols[:, COLS["router_b"]] = np.concatenate([a["b_group"][0], a["b_router"][0]])[None]
    cols[:, COLS["sinks"]] = a["swa_sinks_2"][0][None]
    cols[:HEADS, COLS["dt_bias"]] = a["dt_bias"][0][:, None]
    cols[:HEADS, COLS["a_log"]] = a["a_log"][0][:, None]
    k = np.arange(P)
    consts = np.zeros((P, NCONST), f)
    consts[:, CONSTS["ident"]] = np.eye(P)
    consts[:, CONSTS["ones"]] = 1
    consts[:, CONSTS["upto"]] = k[:, None] <= k[None]
    consts[:, CONSTS["before"]] = k[:, None] < k[None]
    window = np.array([[2, 4], [8, 16]])[:, k // 64].T
    consts[:, CONSTS["pool_first"]] = (window[:, :, None] / np.minimum(np.arange(1, 17), window[:, :, None])).reshape(P, 32)
    consts[:, CONSTS["pool_inv"]] = 1.0 / window
    consts[:, CONSTS["iota8"]] = np.arange(8)
    consts[:, CONSTS["iota8x128"]] = np.arange(8) * P
    consts[:, CONSTS["iotab"]] = np.arange(NBLK + 1)
    consts[:, CONSTS["tokid"]] = k[:, None] + P * np.arange(NT)
    sel = np.zeros((HEADS, HEADS, P), f)
    sel[np.arange(HEADS), np.arange(HEADS)] = 1
    f3 = np.arange(3 * P).reshape(3, P) // (SSD_T * P // GROUPS)
    same = np.stack([f3[i][:, None] == f3[o][None] for i, o in ((0, 0), (1, 0), (0, 1), (1, 1), (2, 1), (1, 2), (2, 2))], 1)
    d = P + k[:, None] - np.arange(2 * P)[None]
    ok = (d >= 0) & (d < P)
    wpool = np.zeros((P, POOL_T, P), f)
    for g in range(4):
        wpool[64 * (g % 2):64 * (g % 2) + 64, g // 2, 64 * (g % 2):64 * (g % 2) + 64] = a["w_pool"][0, g]
    down = a["ffn_w_down_2"][0]
    at = np.cumsum((0,) + FF_PARTS) * P
    return {
        "cols": cols, "consts": consts, "sel": sel.reshape(HEADS, -1), "same": same.astype(f),
        "dist": np.stack([np.where(ok, -d, 0), np.where(ok, 0, -BIG)], 1).astype(f),
        "x": np.ascontiguousarray(a["x"][0]).reshape(NT, P, D),
        "w_ada": tiles(a["w_ada"][0]),
        "w_in": tiles(np.concatenate([xbc, z, dt, pad, u], axis=1)),
        "w_pool": wpool,
        "w_out": tiles(a["w_out"][0]),
        "w_route": np.ascontiguousarray(np.concatenate([a["w_group"][0], a["w_router"][0]], 1).reshape(KT, P, EG + NE).transpose(1, 0, 2)),
        "w13": np.ascontiguousarray(a["w13"][0]), "w2": np.ascontiguousarray(a["w2"][0]),
        "w_qkv": tiles(wqkv),
        "swa_w_out": tiles(a["swa_w_out_2"][0][qcols]),
        "w_up": tiles(gu),
        **{f"w_down{n}": tiles(down[at[n]:at[n + 1]]) for n in range(len(FF_PARTS))},
    }


def program(nc, shapes, counts):
    ins = {k: nc.dram_tensor(f"in_{k}", s, F32, kind="ExternalInput").ap() for k, s in shapes.items()}
    out = nc.dram_tensor("out", (T, D), F32, kind="ExternalOutput").ap()
    marks = {}
    Kernel(nc, ins, out, counts, marks).build()
    return marks


def kernel(**inputs):
    import concourse.bacc as bacc
    from concourse.bass_utils import run_bass_kernel_spmd
    arrays = layout({k: np.asarray(v) for k, v in inputs.items()})
    shapes = {k: v.shape for k, v in arrays.items()}
    counts = {}
    for _ in range(3):
        nc = bacc.Bacc("TRN2", target_bir_lowering=False, num_devices=1)
        counts = program(nc, shapes, counts)
    r = run_bass_kernel_spmd(nc, [{f"in_{k}": v for k, v in arrays.items()}], core_ids=[0])
    return r.results[0]["out"].reshape(1, T, D)
```

```python
from contextlib import ExitStack, contextmanager

import concourse.bass as bass
from concourse import mybir
import numpy as np

ALU = mybir.AluOpType
ACT = mybir.ActivationFunctionType
AX = mybir.AxisListType
F32 = mybir.dt.float32
F32R = mybir.dt.float32r
I32 = mybir.dt.int32

P = 128
T = 1024
D = 1024
KT = D // P
NT = T // P
HALF = 512
POOL_T, SSD_T, CONV_T = 2, 6, 14
CONV = 4
HEADS, HD, GROUPS, STATE = 12, 64, 4, 128
HPG = HEADS // GROUPS
CH = 128
NCH = T // CH
EG, EPG = 4, 8
NE = EG * EPG
FF = 512
NBLK = 2 * T // P + NE - 1
Q_HEADS, KV_HEADS = 16, 4
FFT = 2816 // P
FF_PARTS = (8, 8, 6)
EPS = 1e-6
BIG = 3.0e38
CREDIT = 400

COLS = {}
_at = 0
for _n, _w in (("b_ada", 48), ("c", 8), ("conv_w", CONV_T * CONV), ("conv_b", CONV_T), ("d_skip", SSD_T),
               ("pool_scale", POOL_T), ("ssd_norm_w", SSD_T), ("final_norm_w", KT), ("norm_mix", KT),
               ("norm_ffn", KT), ("final_norm", KT), ("router_b", EG + NE), ("sinks", Q_HEADS),
               ("dt_bias", 1), ("a_log", 1)):
    COLS[_n] = slice(_at, _at + _w)
    _at += _w
NCOLS = _at
CONSTS = {}
_at = 0
for _n, _w in (("ident", P), ("ones", P), ("upto", P), ("before", P), ("pool_first", 32), ("pool_inv", 2),
               ("iota8", 8), ("iota8x128", 8), ("iotab", NBLK + 1), ("tokid", NT)):
    CONSTS[_n] = slice(_at, _at + _w)
    _at += _w
NCONST = _at


class Lane:

    def __init__(self, stage, key):
        self.stage, self.key = stage, key
        self.sem = stage.sem("n_" + key)
        self.count, self.i, self.per, self.base, self.loops = CREDIT, None, 0, 0, 0

    def start(self, eng):
        self.e = eng
        eng.sem_inc(self.sem, CREDIT)
        return eng

    def at(self):
        return self.count if self.i is None else self.i * self.per + self.count

    def __call__(self, ins, name=None):
        ins.then_inc(self.sem, 1)
        self.count += 1
        if name:
            self.stage.marks[self.stage.name, self.key, name] = (self.count, self.per, self.trips if self.i is not None else 0)
        return ins

    def settle(self):
        self.e.wait_ge(self.sem, self.at())

    @contextmanager
    def loop(self, trips):
        key = (self.stage.name, self.key, "loop", self.loops)
        self.loops += 1
        start = self.count
        self.per = self.stage.counts.get(key, 1)
        self.trips = trips
        with self.e.Fori(0, trips) as i:
            self.i = i
            yield i
            self.i = None
        self.stage.marks[key] = self.count - start
        self.count = start + trips * self.per
        self.per = 0


class Stage:

    def __init__(self, nc, name, counts, marks):
        self.nc, self.name, self.counts, self.marks = nc, name, counts, marks
        self.ctx = ExitStack()

    def __enter__(self):
        self.pe, self.act, self.dve, self.pool = (Lane(self, k) for k in ("pe", "act", "dve", "pool"))
        return self

    def __exit__(self, *a):
        self.ctx.close()

    def sb(self, name, shape, dt=F32):
        return self.ctx.enter_context(self.nc.sbuf_tensor(f"{self.name}_{name}", shape, dt))

    def ps(self, name, shape, dt=F32):
        return self.ctx.enter_context(self.nc.psum_tensor(f"{self.name}_{name}", shape, dt))

    def sem(self, name):
        return self.ctx.enter_context(self.nc.semaphore(f"{self.name}_{name}"))

    def block(self):
        return self.nc.Block()

    def wait(self, eng, lane, name, i=None):
        count, per, trips = self.counts.get((self.name, lane.key, name), (CREDIT + 1, 0, 0))
        if trips and i is None:
            i = trips - 1
        eng.wait_ge(lane.sem, count + per * i if trips and per else count)


class Gemm:

    def __init__(self, st, kt=KT):
        self.st = st
        self.raw = st.sb("w_raw", [P, 2, kt * P])
        self.hi = st.sb("w_hi", [P, 2, kt * P], F32R)
        self.lo = st.sb("w_lo", [P, 2, kt * P], F32R)
        self.acc = [st.ps(f"acc{b}", [P, T]) for b in range(2)]
        self.s_loaded = [st.sem(f"w_loaded{b}") for b in range(2)]
        self.s_hi, self.s_split, self.s_mult, self.s_emptied = (
            st.sem(n) for n in ("w_hi", "w_split", "w_mult", "w_emptied"))

    def load(self, sp, i, base, b, src, kt=KT):
        sp.wait_ge(self.s_split, 2 * i + (base + b + 1))
        sp.dma_start(self.raw[:, b, 0:kt * P], src).then_inc(self.s_loaded[b], 16)

    def split(self, pool, i, base, b, kt=KT):
        raw, hi, lo = (x[:, b, 0:kt * P] for x in (self.raw, self.hi, self.lo))
        pool.wait_ge(self.s_loaded[b], 16 * i + 16 * (base // 2 + 1))
        pool.wait_ge(self.s_mult, 2 * i + (base + b + 1))
        pool.nop(nofuse=True)
        pool.tensor_copy(hi, raw).then_inc(self.s_hi, 1)
        pool.wait_ge(self.s_hi, 2 * i + (base + b + 1))
        pool.tensor_tensor(lo, raw, hi.bitcast(F32), ALU.subtract).then_inc(self.s_split, 1)

    def mult(self, pe, i, base, b, xh, xl, kt=KT):
        pe.wait_ge(self.s_split, 2 * i + (base + b + 3))
        pe.wait_ge(self.s_emptied, 2 * i + (base + b + 1))
        for h in range(0, T, HALF):
            for k in range(kt):
                for t, (w, x) in enumerate(((self.hi, xh), (self.hi, xl), (self.lo, xh))):
                    m = pe.matmul(self.acc[b][:, h:h + HALF], w[:, b, k * P:(k + 1) * P], x[:, k, h:h + HALF],
                                  start=(k == 0 and t == 0), stop=(k == kt - 1 and t == 2))
        m.then_inc(self.s_mult, 1)

    def ready(self, eng, i, base, b):
        eng.wait_ge(self.s_mult, 2 * i + (base + b + 3))

    def empty(self, ins):
        return ins.then_inc(self.s_emptied, 1)

    def emptied(self, eng, i, base, b):
        eng.wait_ge(self.s_emptied, 2 * i + (base + b + 3))


def tile_of(x, i, b=0, step=2):
    return x[:, bass.ds(step * i + b, 1), :].rearrange("p a t -> p (a t)")


class Kernel:
    def __init__(self, nc, ins, out, counts, marks):
        self.nc, self.ins, self.out, self.counts, self.marks = nc, ins, out, counts, marks

    def stage(self, name):
        return Stage(self.nc, name, self.counts, self.marks)

    def build(self, upto=None):
        nc = self.nc
        with ExitStack() as ctx:
            sb = lambda n, s, d=F32: ctx.enter_context(nc.sbuf_tensor(n, s, d))
            self.cols = sb("cols", [P, NCOLS])
            self.consts = sb("consts", [P, NCONST])
            self.mod = sb("mod", [P, 48])
            self.xh = sb("xh", [P, KT, T], F32R)
            self.xl = sb("xl", [P, KT, T], F32R)
            self.xt_dram = nc.dram_tensor("xt_scratch", (P, KT, T), F32).ap()
            self.h_dram = nc.dram_tensor("h_scratch", (T, D), F32).ap()
            self.y_dram = nc.dram_tensor("y_scratch", ((NBLK + 1) * P, D), F32).ap()
            self.tok_dram = nc.dram_tensor("token_of_slot", ((NBLK + 2) * P, 1), F32).ap()
            with nc.sbuf_tensor("x_first", [P, KT, T], F32) as self.x:
                self.prepare()
            self.mixer_in()
            self.ssd()
            self.gate_norm()
            self.x = sb("x_res", [P, KT, T])
            self.acc_sq = sb("acc_sq", [P, T])
            self.dense_out("mixout", self.ins["w_out"], reload=True, gate=slice(16, 24))
            self.route()
            self.experts()
            self.combine()
            self.attention_in()
            self.attention()
            self.dense_out("attout", self.ins["swa_w_out"])
            self.feed_forward()
            self.finish()

    def col(self, name, k=0, n=1):
        a = COLS[name].start + k
        return self.cols[:, a:a + n]

    def const(self, name, rows=P):
        return self.consts[0:rows, CONSTS[name]]

    def rstd(self, st, sq_sum, total, rstd, name="rstd", after=None):
        def pe(e):
            after(e)
            for h in range(0, T, HALF):
                m = e.matmul(total[:, h:h + HALF], self.const("ones"), sq_sum[:, h:h + HALF], start=True, stop=True)
            st.pe(m, name + "_sum")

        def dve(e):
            st.wait(e, st.pe, name + "_sum")
            st.dve(e.tensor_scalar(rstd[:, :], total[:, :], 1.0 / D, EPS, ALU.mult, ALU.add))
            st.dve.settle()
            st.dve(e.reciprocal(rstd[:, :], rstd[:, :]), name + "_inv")

        def act(e):
            st.wait(e, st.dve, name + "_inv")
            st.act(e.activation(rstd[:, :], rstd[:, :], ACT.Sqrt), name)
        return pe, dve, act

    def scale_split(self, st, rstd, scale, shift, tmp, rstd_name):
        lanes = {0: st.dve, 1: st.dve if shift is not None else st.pool}

        def lo(e, k):
            st.wait(e, st.act, f"hi{k}")
            hi, out, t = self.xh[:, k, :].bitcast(F32), self.xl[:, k, :], tmp[:, k % 4, :]
            if shift is None:
                ins = e.tensor_tensor(out, t, hi, ALU.subtract)
            else:
                ins = e.scalar_tensor_tensor(out, t, shift[:, k:k + 1], hi, ALU.add, ALU.subtract)
            lanes[k % 2](ins, f"lo{k}")

        def dve(e):
            for k in range(KT + 1):
                if k < KT:
                    if k >= 4:
                        st.wait(e, lanes[k % 2], f"lo{k - 4}")
                    elif k == 0:
                        st.wait(e, st.act, rstd_name)
                    st.dve(e.scalar_tensor_tensor(tmp[:, k % 4, :], self.x[:, k, :], scale[:, k:k + 1], rstd[:, :],
                                                  ALU.mult, ALU.mult), f"scaled{k}")
                if k >= 1 and lanes[(k - 1) % 2] is st.dve:
                    lo(e, k - 1)

        def act(e):
            for k in range(KT):
                st.wait(e, st.dve, f"scaled{k}")
                if shift is None:
                    st.act(e.activation(self.xh[:, k, :], tmp[:, k % 4, :], ACT.Copy), f"hi{k}")
                else:
                    st.act(e.activation(self.xh[:, k, :], tmp[:, k % 4, :], ACT.Identity, bias=shift[:, k:k + 1]), f"hi{k}")

        def pool(e):
            for k in range(1, KT, 2) if shift is None else ():
                lo(e, k)
        return dve, act, pool

    def sum_squares(self, st, sq, acc, ready=None):
        def act(e):
            ready(e)
            for k in range(KT):
                if k >= 2:
                    st.wait(e, st.dve, f"sq_added{k - 2}")
                st.act(e.activation(sq[:, k % 2, :], self.x[:, k, :], ACT.Square), f"sq{k}")

        def dve(e):
            for k in range(KT):
                st.wait(e, st.act, f"sq{k}")
                if k == 0:
                    st.dve(e.tensor_copy(acc[:, :], sq[:, 0, :]), "sq_added0")
                else:
                    st.dve.settle()
                    st.dve(e.tensor_tensor(acc[:, :], acc[:, :], sq[:, k % 2, :], ALU.add), f"sq_added{k}")
        return act, dve

    def prepare(self):
        ins, ones = self.ins, self.const("ones")
        with self.stage("prep") as st:
            xtok = st.sb("xtok", [P, 2, D])
            wa = st.sb("wa", [P, 2, KT * P])
            sc = st.sb("silu_c", [P, KT])
            sq, acc, rstd, tmp = st.sb("sq", [P, 2, T]), st.sb("acc", [P, T]), st.sb("rstd", [P, T]), st.sb("tmp", [P, 4, T])
            turned = [st.ps(f"turned{b}", [P, D]) for b in range(2)]
            pm = [st.ps(f"mod{b}", [P, HALF]) for b in range(2)]
            total = st.ps("total", [P, T])
            s_cols, s_out = st.sem("cols"), st.sem("xt_out")
            s_x, s_wa = [st.sem(f"x{b}") for b in range(2)], [st.sem(f"wa{b}") for b in range(2)]
            rstd_pe, rstd_dve, rstd_act = self.rstd(st, acc, total, rstd, after=lambda e: st.wait(e, st.dve, "sq_added7"))
            sq_act, sq_dve = self.sum_squares(st, sq, acc, ready=lambda e: st.wait(e, st.act, "xt1"))
            sc_dve, sc_act, sc_pool = self.scale_split(st, rstd, self.mod[:, 8:16], self.mod[:, 0:8], tmp, "rstd")
            with st.block() as blk:
                @blk.sync
                def _(e):
                    e.dma_start(self.cols[:, :], ins["cols"]).then_inc(s_cols, 16)
                    e.dma_start(self.consts[:, :], ins["consts"]).then_inc(s_cols, 16)
                    with e.Fori(0, NT // 2) as i:
                        for b in range(2):
                            st.wait(e, st.pe, f"turn{b}", i - 1)
                            e.dma_start(xtok[:, b, :], ins["x"][2 * i + b]).then_inc(s_x[b], 16)
                    with e.Fori(0, 24) as i:
                        for b in range(2):
                            st.wait(e, st.pe, f"ada{b}", i - 1)
                            e.dma_start(wa[:, b, :], ins["w_ada"][2 * i + b]).then_inc(s_wa[b], 16)
                    st.wait(e, st.act, "xt1")
                    e.dma_start(self.xt_dram, self.x[:, :, :]).then_inc(s_out, 16)
                    e.wait_ge(s_out, 16)

                @blk.tensor
                def _(e):
                    st.pe.start(e)
                    e.wait_ge(s_cols, 32)
                    with st.pe.loop(NT // 2) as i:
                        for b in range(2):
                            e.wait_ge(s_x[b], 16 * i + 16)
                            st.wait(e, st.act, f"xt{b}", i - 1)
                            for k in range(KT):
                                m = e.transpose(turned[b][:, k * P:(k + 1) * P], xtok[:, b, k * P:(k + 1) * P], self.const("ident"))
                            st.pe(m, f"turn{b}")
                    st.wait(e, st.act, "silu_c")
                    with st.pe.loop(24) as i:
                        for b in range(2):
                            e.wait_ge(s_wa[b], 16 * i + 16)
                            st.wait(e, st.dve, f"mod{b}", i - 1)
                            for k in range(KT):
                                m = e.matmul(pm[b][:, 0:1], wa[:, b, k * P:(k + 1) * P], sc[:, k:k + 1], start=(k == 0), stop=(k == KT - 1))
                            st.pe(m, f"ada{b}")
                    rstd_pe(e)

                @blk.scalar
                def _(e):
                    st.act.start(e)
                    e.wait_ge(s_cols, 32)
                    st.act(e.activation(sc[:, :], self.col("c", 0, KT), ACT.Silu), "silu_c")
                    with st.act.loop(NT // 2) as i:
                        for b in range(2):
                            st.wait(e, st.pe, f"turn{b}", i)
                            st.act(e.activation(self.x[:, :, bass.ds(2 * P * i + P * b, P)],
                                                turned[b][:, :].rearrange("p (k t) -> p k t", t=P), ACT.Copy), f"xt{b}")
                    sq_act(e)
                    rstd_act(e)
                    sc_act(e)

                @blk.vector
                def _(e):
                    st.dve.start(e)
                    e.wait_ge(s_cols, 32)
                    sq_dve(e)
                    with st.dve.loop(24) as i:
                        for b in range(2):
                            st.wait(e, st.pe, f"ada{b}", i)
                            n = 2 * i + b
                            st.dve(e.tensor_tensor(self.mod[:, bass.ds(n, 1)], pm[b][:, 0:1],
                                                   self.cols[:, bass.ds(2 * i + (COLS["b_ada"].start + b), 1)], ALU.add), f"mod{b}")
                    st.dve.settle()
                    for a in (8, 32):
                        st.dve(e.tensor_scalar(self.mod[:, a:a + 8], self.mod[:, a:a + 8], 1.0, None, ALU.add))
                    rstd_dve(e)
                    sc_dve(e)

                @blk.gpsimd
                def _(e):
                    st.pool.start(e)
                    sc_pool(e)

    def mixer_in(self):
        ins, nc = self.ins, self.nc
        self.keep = ExitStack()
        sb = lambda n, s: self.keep.enter_context(nc.sbuf_tensor(n, s, F32))
        self.xbc = sb("xbc", [P, CONV_T, T])
        self.zs = sb("zs", [P, SSD_T, T])
        self.acs_row = sb("acs_row", [HEADS, T])
        self.dt_tok = sb("dt_tok", [P, NCH * HEADS])
        self.acs_tok = sb("acs_tok", [P, NCH * HEADS])
        PAD = 16
        with self.stage("in") as st:
            g = Gemm(st)
            raw = st.sb("raw", [P, 2, PAD + T])
            wrk = st.sb("wrk", [P, 2, PAD + T])
            wpool = st.sb("wpool", [P, POOL_T, P])
            dta_tok = st.sb("dta_tok", [P, NCH * HEADS])
            nega = st.sb("nega", [HEADS, 1])
            s_wp = st.sem("wp")
            turn = st.ps("turn", [P, 2 * HALF])
            mix = [st.ps(f"mix{b}", [P, HALF]) for b in range(2)]
            W = ins["w_in"]
            cw, cb = COLS["conv_w"].start, COLS["conv_b"].start
            N_SILU, N_Z = CONV_T // 2, SSD_T // 2
            BZ, BD = CONV_T, CONV_T + SSD_T
            TAIL = [(0, BD), (1, BD), (0, BD + 2)]
            with st.block() as blk:
                @blk.sync
                def _(e):
                    e.dma_start(wpool[:, :, :], ins["w_pool"]).then_inc(s_wp, 16)
                    with e.Fori(0, N_SILU + N_Z) as i:
                        for b in range(2):
                            g.load(e, i, 0, b, W[2 * i + b])
                    for j, (b, base) in enumerate(TAIL):
                        g.load(e, 0, base, b, W[BD + j])

                @blk.gpsimd
                def _(e):
                    st.pool.start(e)
                    e.sem_inc(g.s_split, 2)
                    with e.Fori(0, N_SILU + N_Z) as i:
                        for b in range(2):
                            g.split(e, i, 0, b)
                    for b, base in TAIL:
                        g.split(e, 0, base, b)

                @blk.tensor
                def _(e):
                    st.pe.start(e)
                    e.sem_inc(g.s_mult, 2)
                    with e.Fori(0, N_SILU + N_Z) as i:
                        for b in range(2):
                            g.mult(e, i, 0, b, self.xh, self.xl)
                    for b, base in TAIL:
                        g.mult(e, 0, base, b, self.xh, self.xl)
                    ident = self.consts[0:HEADS, 0:HEADS]
                    for src, at in ((0, 0), (1, HALF)):
                        st.wait(e, st.dve, "dt" if src == 0 else "dta")
                        for c in range(NCH):
                            m = e.transpose(turn[:, at + c * HEADS:at + (c + 1) * HEADS],
                                            wrk[0:HEADS, src, c * CH:(c + 1) * CH], ident)
                        st.pe(m, f"dt_turned{src}")
                    st.wait(e, st.dve, "dta_tok")
                    m = e.matmul(mix[0][:, 0:NCH * HEADS], self.const("upto"), dta_tok[:, :], start=True, stop=True)
                    st.pe(m, "acs_tok")
                    for c in range(NCH):
                        m = e.matmul(turn[0:HEADS, c * CH:(c + 1) * CH], dta_tok[:, c * HEADS:(c + 1) * HEADS],
                                     self.const("upto"), start=True, stop=True)
                    st.pe(m, "acs_row")
                    e.wait_ge(s_wp, 16)
                    for j in range(POOL_T):
                        st.wait(e, st.dve, f"pool_diff{j}")
                        for h in range(2):
                            if j == 0 and h == 0:
                                st.wait(e, st.act, "acs_tok")
                            if j:
                                st.wait(e, st.dve, f"pool_lo{j - 1}{h}")
                            m = e.matmul(mix[h][:, :], wpool[:, j, :], raw[:, 1 - j, PAD + h * HALF:PAD + (h + 1) * HALF],
                                         start=True, stop=True)
                            st.pe(m, f"pool{j}{h}")

                @blk.scalar
                def _(e):
                    st.act.start(e)
                    e.preload_act_table(ACT.Silu)
                    with st.act.loop(N_SILU) as i:
                        for b in range(2):
                            g.ready(e, i, 0, b)
                            if b == 0:
                                st.wait(e, st.dve, "zeros")
                            st.wait(e, st.dve, f"conv{b}", i - 1)
                            g.empty(e.activation(raw[:, b, PAD:PAD + T], g.acc[b][:, :], ACT.Copy))
                            st.wait(e, st.dve, f"conv{b}", i)
                            st.act(e.activation(tile_of(self.xbc, i, b), wrk[:, b, 0:T], ACT.Silu), f"xbc{b}")
                    with st.act.loop(N_Z) as i:
                        for b in range(2):
                            g.ready(e, i, BZ, b)
                            g.empty(e.activation(tile_of(self.zs, i, b), g.acc[b][:, :], ACT.Silu))
                    g.ready(e, 0, BD, 0)
                    bias = self.cols[0:HEADS, COLS["dt_bias"]]
                    e1, v = raw[0:HEADS, 1, PAD:PAD + T], wrk[0:HEADS, 1, 0:T]
                    st.act(e.activation(nega[:, :], self.cols[0:HEADS, COLS["a_log"]], ACT.Exp), "exp_a")
                    st.act.settle()
                    g.empty(e.activation(v, g.acc[0][0:HEADS, :], ACT.Identity, bias=bias))
                    g.emptied(e, 0, BD, 0)
                    st.act(e.activation(e1, v, ACT.Abs))
                    st.act.settle()
                    st.act(e.activation(e1, e1, ACT.Exp, scale=-1.0), "dt_e")
                    st.wait(e, st.dve, "dt_u")
                    st.act(e.activation(raw[0:HEADS, 0, PAD:PAD + T], wrk[0:HEADS, 0, 0:T], ACT.Ln), "dt_ln")
                    for j in range(POOL_T):
                        b, base = TAIL[1 + j]
                        g.ready(e, 0, base, b)
                        if j == 0:
                            st.wait(e, st.dve, "dt")
                        g.empty(e.activation(raw[:, 1 - j, PAD:PAD + T], g.acc[b][:, :], ACT.Copy))
                    st.wait(e, st.pe, "acs_tok")
                    st.act(e.activation(self.acs_tok[:, :], mix[0][:, 0:NCH * HEADS], ACT.Copy), "acs_tok")
                    st.wait(e, st.pe, "acs_row")
                    st.act(e.activation(self.acs_row[:, :], turn[0:HEADS, :], ACT.Copy), "acs_row")
                    g.ready(e, 0, BD + 2, 0)
                    for j in range(POOL_T):
                        for h in range(2):
                            st.wait(e, st.pe, f"pool{j}{h}")
                            st.act(e.activation(self.xh[:, j, h * HALF:(h + 1) * HALF], mix[h][:, :], ACT.Copy,
                                                scale=self.col("pool_scale", j)), f"pool_hi{j}{h}")

                @blk.vector
                def _(e):
                    st.dve.start(e)
                    e.sem_inc(g.s_emptied, 2)
                    st.dve(e.memset(raw[:, :, 0:PAD], 0.0), "zeros")
                    with st.dve.loop(N_SILU) as i:
                        for b in range(2):
                            g.emptied(e, i, 0, b)
                            st.wait(e, st.act, f"xbc{b}", i - 1)
                            at = i * (2 * CONV) + (cw + b * CONV)
                            taps = [self.cols[:, bass.ds(at + j, 1)] for j in range(CONV)]
                            bias = self.cols[:, bass.ds(2 * i + (cb + b), 1)]
                            if b == 0:
                                st.dve.settle()
                            a = wrk[:, b, 0:T]
                            st.dve(e.tensor_scalar(a, raw[:, b, PAD:PAD + T], taps[3], bias, ALU.mult, ALU.add))
                            for j in (2, 1, 0):
                                st.dve.settle()
                                s = PAD - 3 + j
                                st.dve(e.scalar_tensor_tensor(a, raw[:, b, s:s + T], taps[j], a, ALU.mult, ALU.add),
                                       f"conv{b}" if j == 0 else None)
                    st.wait(e, st.act, "dt_e")
                    e1, v = raw[0:HEADS, 1, PAD:PAD + T], wrk[0:HEADS, 1, 0:T]
                    u, t, ln = wrk[0:HEADS, 0, 0:T], self.acs_row[:, :], raw[0:HEADS, 0, PAD:PAD + T]
                    st.dve(e.tensor_scalar(u, e1, 1.0, None, ALU.add), "dt_u")
                    st.dve.settle()
                    st.dve(e.scalar_tensor_tensor(t, u, -1.0, e1, ALU.add, ALU.subtract))
                    st.wait(e, st.act, "dt_ln")
                    st.dve(e.reciprocal(u, u))
                    st.dve.settle()
                    st.dve(e.tensor_tensor(t, t, u, ALU.mult))
                    st.dve.settle()
                    st.dve(e.tensor_tensor(ln, ln, t, ALU.subtract))
                    st.dve.settle()
                    st.dve(e.scalar_tensor_tensor(u, v, 0.0, ln, ALU.max, ALU.add), "dt")
                    st.dve(e.tensor_scalar(nega[:, :], nega[:, :], -1.0, None, ALU.mult))
                    st.dve.settle()
                    st.dve(e.tensor_scalar(v, u, nega[:, 0:1], None, ALU.mult), "dta")
                    for src, dst in ((0, self.dt_tok), (1, dta_tok)):
                        st.wait(e, st.pe, f"dt_turned{src}")
                        at = src * HALF
                        st.dve(e.tensor_copy(dst[:, :], turn[:, at:at + NCH * HEADS]), "dta_tok" if src else "dt_tok")
                    W_ = PAD + T
                    for j in range(POOL_T):
                        g.emptied(e, 0, TAIL[1 + j][1], TAIL[1 + j][0])
                        uu, s, r = raw[:, 1 - j, :], wrk[:, 0, :], wrk[:, 1, :]
                        if j == 1:
                            st.dve.settle()
                        st.dve(e.tensor_tensor(s[:, 1:W_], uu[:, 1:W_], uu[:, 0:W_ - 1], ALU.add))
                        st.dve.settle()
                        st.dve(e.tensor_tensor(r[:, 3:W_], s[:, 3:W_], s[:, 1:W_ - 2], ALU.add))
                        if j == 1:
                            st.dve.settle()
                            st.dve(e.tensor_tensor(s[:, 7:W_], r[:, 7:W_], r[:, 3:W_ - 4], ALU.add))
                            st.dve.settle()
                            st.dve(e.tensor_tensor(r[:, 15:W_], s[:, 15:W_], s[:, 7:W_ - 8], ALU.add))
                        st.dve.settle()
                        for half, src in ((0, s), (1, r)):
                            rows = slice(64 * half, 64 * half + 64)
                            first = self.consts[rows, CONSTS["pool_first"].start + 16 * j:CONSTS["pool_first"].start + 16 * j + 16]
                            inv = self.consts[rows, CONSTS["pool_inv"].start + j:CONSTS["pool_inv"].start + j + 1]
                            st.dve(e.tensor_tensor(src[rows, PAD:PAD + 16], src[rows, PAD:PAD + 16], first, ALU.mult))
                            st.dve.settle()
                            st.dve(e.scalar_tensor_tensor(uu[rows, PAD:W_], src[rows, PAD:W_], inv, uu[rows, PAD:W_],
                                                          ALU.mult, ALU.subtract), f"pool_diff{j}" if half else None)
                    for j in range(POOL_T):
                        for h in range(2):
                            st.wait(e, st.act, f"pool_hi{j}{h}")
                            cs = slice(h * HALF, (h + 1) * HALF)
                            st.dve(e.scalar_tensor_tensor(self.xl[:, j, cs], mix[h][:, :], self.col("pool_scale", j),
                                                          self.xh[:, j, cs].bitcast(F32), ALU.mult, ALU.subtract), f"pool_lo{j}{h}")

    def ssd(self):
        ins, xbc = self.ins, self.xbc
        with self.stage("ssd") as st:
            sel = st.sb("sel", [HEADS, HEADS * P])
            stg = st.sb("stg", [P, 10, CH])
            xdt = st.sb("xdt", [P, HEADS * HD])
            xdte = st.sb("xdte", [P, HEADS * HD])
            btok = st.sb("btok", [P, GROUPS * STATE])
            m = st.sb("m", [P, HEADS * CH])
            ce = st.sb("ce", [P, HEADS * CH])
            cbm = st.sb("cbm", [P, GROUPS * CH])
            state = st.sb("state", [P, HEADS * HD])
            dte, cdec = st.sb("dte", [P, HEADS]), st.sb("cdec", [P, HEADS])
            xy = st.ps("xy", [P, 2 * HALF])
            bt = st.ps("bt", [P, HALF])
            cb = st.ps("cb", [P, HALF])
            bc = st.ps("bc", [P, 3 * HALF])
            s_sel, s_fill = st.sem("sel"), st.sem("fill")
            zeros = st.sb("zeros", [P, D])
            heads = lambda a, n: a[:, :].rearrange("p (h n) -> p h n", n=n)
            groups = lambda a, n: a[:, :].rearrange("p (g r n) -> p g r n", r=HPG, n=n)
            per_head = lambda a, n: a.unsqueeze(2).to_broadcast([P, HEADS, n])
            chunk = lambda a, c: a[:, bass.ds(c * HEADS, HEADS)]
            new_states = bc[:, 0:2 * HALF].rearrange("p (b x) -> p b x", x=HALF)[:, :, 0:2 * HPG * HD]
            with st.block() as blk:
                @blk.sync
                def _(e):
                    e.dma_start(sel[:, :], ins["sel"]).then_inc(s_sel, 16)
                    st.wait(e, st.dve, "zeros")
                    with e.Fori(2 * T // P, NBLK) as i:
                        e.dma_start(self.y_dram[bass.ds(i * P + P, P), :], zeros[:, :]).then_inc(s_fill, 16)
                    e.wait_ge(s_fill, 16 * (NBLK - 2 * T // P))

                @blk.gpsimd
                def _(e):
                    st.pool.start(e)
                    with st.pool.loop(NCH) as c:
                        st.wait(e, st.pe, "cb", c - 1)
                        e.nop(nofuse=True)
                        st.pool(e.tensor_copy(stg[:, :, :], xbc[:, 0:10, bass.ds(c * CH, CH)]), "staged")
                        st.wait(e, st.dve, "min", c)
                        st.pool(e.tensor_tensor(heads(m, CH), heads(m, CH), per_head(chunk(self.acs_tok, c), CH), ALU.subtract), "seg")
                        st.wait(e, st.act, "dte", c)
                        st.wait(e, st.dve, "xdt", c)
                        st.pool(e.tensor_tensor(heads(xdte, HD), heads(xdt, HD), per_head(dte[:, :], HD), ALU.mult), "xdte")

                @blk.tensor
                def _(e):
                    st.pe.start(e)
                    e.wait_ge(s_sel, 16)
                    with st.pe.loop(NCH) as c:
                        st.wait(e, st.pool, "staged", c)
                        st.wait(e, st.act, "y_out", c - 1)
                        for j in range(SSD_T):
                            k = e.transpose(xy[:, j * P:(j + 1) * P], stg[:, j, :], self.const("ident"))
                        st.pe(k, "x_turned")
                        st.wait(e, st.act, "btok", c - 1)
                        for g in range(GROUPS):
                            k = e.transpose(bt[:, g * P:(g + 1) * P], stg[:, SSD_T + g, :], self.const("ident"))
                        st.pe(k, "b_turned")
                        st.wait(e, st.dve, "cbm", c - 1)
                        for g in range(GROUPS):
                            k = e.matmul(cb[:, g * CH:(g + 1) * CH], stg[:, SSD_T + g, :],
                                         xbc[:, 10 + g, bass.ds(c * CH, CH)], start=True, stop=True)
                        st.pe(k, "cb")
                        st.wait(e, st.dve, "state", c - 1)
                        for h in range(HEADS):
                            k = e.matmul(bc[:, h * CH:(h + 1) * CH], sel[:, h * P:(h + 1) * P],
                                         self.acs_row[:, bass.ds(c * CH, CH)], start=True, stop=True)
                        st.pe(k, "bc")
                        st.wait(e, st.dve, "xdt", c)
                        st.wait(e, st.dve, "ce", c)
                        st.wait(e, st.dve, "m", c)
                        for h in range(HEADS):
                            o = xy[64 * (h % 2):64 * (h % 2) + 64, (h // 2) * CH:(h // 2 + 1) * CH]
                            e.matmul(o, xdt[:, h * HD:(h + 1) * HD], m[:, h * CH:(h + 1) * CH], start=True, stop=False)
                            k = e.matmul(o, state[:, h * HD:(h + 1) * HD], ce[:, h * CH:(h + 1) * CH], start=False, stop=True)
                        st.pe(k, "y")
                        st.wait(e, st.pool, "xdte", c)
                        st.wait(e, st.act, "btok", c)
                        w = HPG * HD
                        for g in range(GROUPS):
                            at = (g // 2) * HALF + (g % 2) * w
                            k = e.matmul(bc[:, at:at + w], btok[:, g * P:(g + 1) * P], xdte[:, g * w:(g + 1) * w], start=True, stop=True)
                        st.pe(k, "states")

                @blk.scalar
                def _(e):
                    st.act.start(e)
                    with st.act.loop(NCH) as c:
                        st.wait(e, st.pe, "b_turned", c)
                        st.act(e.activation(btok[:, :], bt[:, :], ACT.Copy), "btok")
                        st.wait(e, st.dve, "dte_arg", c)
                        st.act(e.activation(ce[:, :], bc[:, :], ACT.Exp), "exp_bc")
                        st.act(e.activation(dte[:, :], dte[:, :], ACT.Exp), "dte")
                        st.wait(e, st.dve, "decayed", c - 1)
                        st.act.settle()
                        st.act(e.activation(cdec[:, :], heads(ce, CH)[:, :, CH - 1], ACT.Copy), "cdec")
                        st.wait(e, st.pool, "seg", c)
                        st.act(e.activation(m[:, :], m[:, :], ACT.Exp), "exp_seg")
                        st.wait(e, st.pe, "y", c)
                        st.act(e.activation(xbc[:, SSD_T:2 * SSD_T, bass.ds(c * CH, CH)],
                                            xy[:, 0:SSD_T * P].rearrange("p (j t) -> p j t", t=CH), ACT.Copy), "y_out")

                @blk.vector
                def _(e):
                    st.dve.start(e)
                    st.dve(e.memset(state[:, :], 0.0), "zero")
                    st.dve(e.memset(zeros[:, :], 0.0), "zeros")
                    mask = self.const("upto").unsqueeze(1).to_broadcast([P, GROUPS, CH])
                    with st.dve.loop(NCH) as c:
                        st.wait(e, st.pe, "x_turned", c)
                        st.dve(e.tensor_tensor(heads(xdt, HD), xy[:, 0:HEADS * HD].rearrange("p (h n) -> p h n", n=HD),
                                               per_head(chunk(self.dt_tok, c), HD), ALU.mult), "xdt")
                        st.wait(e, st.pe, "bc", c)
                        st.dve(e.tensor_tensor(heads(m, CH), heads(bc, CH), per_head(chunk(self.acs_tok, c), CH), ALU.min), "min")
                        st.dve(e.tensor_tensor(dte[:, :], heads(bc, CH)[:, :, CH - 1], chunk(self.acs_tok, c), ALU.subtract), "dte_arg")
                        st.dve(e.tensor_tensor(heads(cbm, CH), heads(cb, CH), mask, ALU.mult), "cbm")
                        st.wait(e, st.act, "cdec", c)
                        for g in range(GROUPS):
                            a = ce[:, g * HPG * CH:(g + 1) * HPG * CH].rearrange("p (r n) -> p r n", n=CH)
                            cT = xbc[:, 10 + g, bass.ds(c * CH, CH)].unsqueeze(1).to_broadcast([P, HPG, CH])
                            st.dve(e.tensor_tensor(a, a, cT, ALU.mult), "ce" if g == GROUPS - 1 else None)
                        st.wait(e, st.act, "exp_seg", c)
                        st.dve.settle()
                        st.dve(e.tensor_tensor(groups(m, CH), groups(m, CH),
                                               heads(cbm, CH).unsqueeze(2).to_broadcast([P, GROUPS, HPG, CH]), ALU.mult), "m")
                        st.wait(e, st.pe, "y", c)
                        st.dve(e.tensor_tensor(heads(state, HD), heads(state, HD), per_head(cdec[:, :], HD), ALU.mult), "decayed")
                        st.wait(e, st.pe, "states", c)
                        st.dve.settle()
                        s2 = state[:, :].rearrange("p (b x) -> p b x", b=2)
                        st.dve(e.tensor_tensor(s2, s2, new_states, ALU.add), "state")

    def gate_norm(self):
        xbc, zs = self.xbc, self.zs
        with self.stage("gate") as st:
            same = st.sb("same", [P, 7, P])
            rstd, tmp = st.sb("rstd", [P, T]), st.sb("tmp", [P, 2, T])
            total = [st.ps(f"total{b}", [P, T]) for b in range(2)]
            s_same = st.sem("same")
            PAIRS = [(0, 0), (1, 0), (0, 1), (1, 1), (2, 1), (1, 2), (2, 2)]
            with st.block() as blk:
                @blk.sync
                def _(e):
                    e.dma_start(same[:, :, :], self.ins["same"]).then_inc(s_same, 16)

                @blk.tensor
                def _(e):
                    st.pe.start(e)
                    e.wait_ge(s_same, 16)
                    for j in range(SSD_T):
                        mine = [(n, a) for n, (a, o) in enumerate(PAIRS) if o == j % 3]
                        for h in range(0, T, HALF):
                            for x, (n, a) in enumerate(mine):
                                src = 3 * (j // 3) + a
                                if h == 0:
                                    st.wait(e, st.act, f"sq{src}")
                                    if j >= 2 and x == 0:
                                        st.wait(e, st.dve, f"mean{j - 2}")
                                k = e.matmul(total[j % 2][:, h:h + HALF], same[:, n, :], zs[:, src, h:h + HALF],
                                             start=(x == 0), stop=(x == len(mine) - 1))
                        st.pe(k, f"total{j}")

                @blk.scalar
                def _(e):
                    st.act.start(e)
                    for j in range(SSD_T):
                        st.wait(e, st.dve, f"gated{j}")
                        st.act(e.activation(zs[:, j, :], xbc[:, SSD_T + j, :], ACT.Square), f"sq{j}")
                    for j in range(SSD_T):
                        st.wait(e, st.dve, f"inv{j}")
                        st.act(e.activation(rstd[:, :], rstd[:, :], ACT.Sqrt), f"rstd{j}")
                        st.wait(e, st.dve, f"normed{j}")
                        st.act(e.activation(self.xh[:, POOL_T + j, :], tmp[:, j % 2, :], ACT.Copy), f"hi{j}")

                @blk.gpsimd
                def _(e):
                    st.pool.start(e)
                    for j in range(SSD_T):
                        st.wait(e, st.act, f"hi{j}")
                        st.pool(e.tensor_tensor(self.xl[:, POOL_T + j, :], tmp[:, j % 2, :],
                                                self.xh[:, POOL_T + j, :].bitcast(F32), ALU.subtract), f"lo{j}")

                @blk.vector
                def _(e):
                    st.dve.start(e)
                    for j in range(SSD_T):
                        y = xbc[:, SSD_T + j, :]
                        st.dve(e.scalar_tensor_tensor(y, xbc[:, j, :], self.col("d_skip", j), y, ALU.mult, ALU.add))
                        st.dve.settle()
                        st.dve(e.tensor_tensor(y, y, zs[:, j, :], ALU.mult), f"gated{j}")
                    for j in range(SSD_T):
                        st.wait(e, st.pe, f"total{j}")
                        st.dve.settle()
                        st.dve(e.tensor_scalar(rstd[:, :], total[j % 2][:, :], GROUPS / (SSD_T * P), EPS, ALU.mult, ALU.add), f"mean{j}")
                        st.dve.settle()
                        st.dve(e.reciprocal(rstd[:, :], rstd[:, :]), f"inv{j}")
                        st.wait(e, st.act, f"rstd{j}")
                        if j >= 2:
                            st.wait(e, st.pool, f"lo{j - 2}")
                        st.dve(e.scalar_tensor_tensor(tmp[:, j % 2, :], xbc[:, SSD_T + j, :], self.col("ssd_norm_w", j),
                                                      rstd[:, :], ALU.mult, ALU.mult), f"normed{j}")
        self.keep.close()

    def dense_out(self, name, W, reload=False, gate=None):
        x, acc = self.x, self.acc_sq
        with self.stage(name) as st:
            g = Gemm(st)
            sq = st.sb("sq", [P, 2, T])
            s_x = st.sem("x")
            with st.block() as blk:
                @blk.sync
                def _(e):
                    with e.Fori(0, KT // 2) as i:
                        for b in range(2):
                            g.load(e, i, 0, b, W[2 * i + b])

                @blk.gpsimd
                def _(e):
                    st.pool.start(e)
                    e.sem_inc(g.s_split, 2)
                    with e.Fori(0, KT // 2) as i:
                        for b in range(2):
                            g.split(e, i, 0, b)

                @blk.tensor
                def _(e):
                    st.pe.start(e)
                    e.sem_inc(g.s_mult, 2)
                    with e.Fori(0, KT // 2) as i:
                        for b in range(2):
                            g.mult(e, i, 0, b, self.xh, self.xl)

                @blk.scalar
                def _(e):
                    st.act.start(e)
                    if reload:
                        e.dma_start(x[:, :, :], self.xt_dram).then_inc(s_x, 16)
                    with st.act.loop(KT // 2) as i:
                        for b in range(2):
                            g.emptied(e, i, 0, b)
                            st.wait(e, st.dve, f"added{b}", i - 1)
                            st.act(e.activation(sq[:, b, :], tile_of(x, i, b), ACT.Square), f"sq{b}")

                @blk.vector
                def _(e):
                    st.dve.start(e)
                    e.sem_inc(g.s_emptied, 2)
                    st.dve(e.memset(acc[:, :], 0.0))
                    if reload:
                        e.wait_ge(s_x, 16)
                    with st.dve.loop(KT // 2) as i:
                        for b in range(2):
                            g.ready(e, i, 0, b)
                            xn = tile_of(x, i, b)
                            if gate is None:
                                g.empty(e.tensor_tensor(xn, g.acc[b][:, :], xn, ALU.add))
                            else:
                                s = self.mod[:, bass.ds(2 * i + (gate.start + b), 1)]
                                g.empty(e.scalar_tensor_tensor(xn, g.acc[b][:, :], s, xn, ALU.mult, ALU.add))
                            st.wait(e, st.act, f"sq{b}", i)
                            st.dve.settle()
                            st.dve(e.tensor_tensor(acc[:, :], acc[:, :], sq[:, b, :], ALU.add), f"added{b}")

    def route(self):
        ins, nc, x = self.ins, self.nc, self.x
        self.rkeep = ExitStack()
        sb = lambda n, s, d=F32: self.rkeep.enter_context(nc.sbuf_tensor(n, s, d))
        self.slots = sb("slots", [P, 2 * NT], I32)
        self.gates = sb("gates", [P, 2 * NT])
        self.blocks = sb("blocks", [P, NBLK + 2], I32)
        self.rows = sb("rows", [P, NBLK + 2], I32)
        R = EG + NE
        with self.stage("route") as st:
            rstd, hst = st.sb("rstd", [P, T]), st.sb("hst", [P, 2, KT * P])
            htok = st.sb("htok", [P, 2, D])
            wr = st.sb("wr", [P, KT, R])
            lg = st.sb("lg", [P, NT, R])
            zeros = st.sb("zeros", [P, NBLK + 2])
            total = st.ps("total", [P, T])
            turned = [st.ps(f"turned{b}", [P, D]) for b in range(2)]
            pl = [st.ps(f"logits{b}", [P, HALF]) for b in range(2)]
            s_wr, s_zero, s_scatter, s_rows = (st.sem(n) for n in ("wr", "zero", "scatter", "rows"))
            s_h = [st.sem(f"h{b}") for b in range(2)]
            rstd_pe, rstd_dve, rstd_act = self.rstd(st, self.acc_sq, total, rstd, after=lambda e: None)
            t3 = lambda a, k=KT: a.rearrange("p (k t) -> p k t", k=k)
            table = st.sb("table", [NBLK + 2, P])
            W = {}
            def buf(name, *shape):
                n = int(np.prod(shape))
                if name not in W:
                    W[name] = st.sb(name, [P, n])
                a = W[name][:, 0:n]
                if len(shape) == 2:
                    return a.rearrange("p (a b) -> p a b", b=shape[1])
                if len(shape) == 3:
                    return a.rearrange("p (a b c) -> p a b c", b=shape[1], c=shape[2])
                return a
            both_ = lambda st: buf("both", NT * NE)
            g_exp = lambda st: buf("g_exp", NT, EG)
            e_exp = lambda st: buf("e_exp", NT)
            for n, w in (("both", NT * NE), ("g_exp", NT * EG), ("e_exp", NT)):
                buf(n, w)
            with st.block() as blk:
                @blk.sync
                def _(e):
                    for b in range(2):
                        e.sem_inc(s_h[b], 16)
                    e.dma_start(wr[:, :, :], ins["w_route"]).then_inc(s_wr, 16)
                    st.wait(e, st.dve, "zeros")
                    e.dma_start(self.tok_dram.rearrange("(p n) a -> p (n a)", p=P), zeros[:, :]).then_inc(s_zero, 16)
                    with e.Fori(0, NT // 2) as i:
                        for b in range(2):
                            st.wait(e, st.act, f"htok{b}", i)
                            e.dma_start(self.h_dram[bass.ds(2 * P * i + P * b, P), :], htok[:, b, :]).then_inc(s_h[b], 16)
                    for b in range(2):
                        e.wait_ge(s_h[b], 16 * (NT // 2) + 16)
                    e.wait_ge(s_scatter, 16 * 2 * NT)
                    e.dma_start(table[:, :], self.tok_dram.rearrange("(n p) a -> n (p a)", p=P)).then_inc(s_rows, 16)

                @blk.tensor
                def _(e):
                    st.pe.start(e)
                    rstd_pe(e)
                    e.wait_ge(s_wr, 16)
                    with st.pe.loop(NT // 2) as i:
                        for b in range(2):
                            st.wait(e, st.pool, f"h{b}", i)
                            st.wait(e, st.act, f"htok{b}", i - 1)
                            for k in range(KT):
                                e.transpose(turned[b][:, k * P:(k + 1) * P], hst[:, b, k * P:(k + 1) * P], self.const("ident"))
                            st.wait(e, st.dve, f"logits{b}", i - 1)
                            for k in range(KT):
                                m = e.matmul(pl[b][:, 0:R], hst[:, b, k * P:(k + 1) * P], wr[:, k, :], start=(k == 0), stop=(k == KT - 1))
                            st.pe(m, f"used{b}")
                    st.wait(e, st.dve, "chosen")
                    e.matmul(total[:, 0:NT * NE], self.const("before"), both_(st), start=True, stop=True)
                    m = e.matmul(total[:, HALF:HALF + NT * NE], self.const("ones"), both_(st), start=True, stop=True)
                    st.pe(m, "ranked")
                    e.wait_ge(s_rows, 16)
                    m = e.transpose(pl[0][:, 0:NBLK + 2], table[:, :], self.consts[0:NBLK + 2, 0:NBLK + 2])
                    st.pe(m, "rows")

                @blk.scalar
                def _(e):
                    st.act.start(e)
                    rstd_act(e)
                    with st.act.loop(NT // 2) as i:
                        for b in range(2):
                            st.wait(e, st.pe, f"used{b}", i)
                            e.wait_ge(s_h[b], 16 * i + 16)
                            st.act(e.activation(htok[:, b, :], turned[b][:, :], ACT.Copy), f"htok{b}")
                    st.wait(e, st.dve, "g_arg")
                    st.act(e.activation(g_exp(st), g_exp(st), ACT.Exp), "g_exp")
                    st.wait(e, st.dve, "e_arg")
                    st.act(e.activation(e_exp(st), e_exp(st), ACT.Exp), "e_exp")

                @blk.gpsimd
                def _(e):
                    st.pool.start(e)
                    shift = self.mod[:, 24:32].unsqueeze(2).to_broadcast([P, KT, P])
                    with st.pool.loop(NT // 2) as i:
                        for b in range(2):
                            st.wait(e, st.dve, f"scaled{b}", i)
                            st.pool(e.tensor_tensor(t3(hst[:, b, :]), t3(hst[:, b, :]), shift, ALU.add), f"h{b}")
                    st.wait(e, st.dve, "slots")
                    e.wait_ge(s_zero, 16)
                    e.nop(nofuse=True)
                    tokid = self.const("tokid")
                    for n in range(2 * NT):
                        e.indirect_dma_start(out=self.tok_dram, out_offset=bass.IndirectOffsetOnAxis(ap=self.slots[:, n:n + 1], axis=0),
                                             in_=tokid[:, n % NT:n % NT + 1], in_offset=None).then_inc(s_scatter, 16)

                @blk.vector
                def _(e):
                    dve = st.dve
                    dve.start(e)
                    dve(e.memset(zeros[:, :], 0.0), "zeros")
                    rstd_dve(e)
                    st.wait(e, st.act, "rstd")
                    scale = self.mod[:, 32:40].unsqueeze(2).to_broadcast([P, KT, P])
                    with dve.loop(NT // 2) as i:
                        for b in range(2):
                            ts = bass.ds(2 * P * i + P * b, P)
                            st.wait(e, st.pe, f"used{b}", i - 1)
                            dve(e.tensor_tensor(t3(hst[:, b, :]), x[:, :, ts], rstd[:, ts].unsqueeze(1).to_broadcast([P, KT, P]), ALU.mult))
                            dve.settle()
                            dve(e.tensor_tensor(t3(hst[:, b, :]), t3(hst[:, b, :]), scale, ALU.mult), f"scaled{b}")
                            st.wait(e, st.pe, f"used{b}", i)
                            dve(e.tensor_tensor(tile_of(lg, i, b), pl[b][:, 0:R], self.cols[:, COLS["router_b"]], ALU.add), f"logits{b}")

                    def do(ins, name=None):
                        dve(ins, name)
                        dve.settle()

                    def over(a, *shape):
                        return a.to_broadcast([P, *shape])
                    iota8 = self.const("iota8")

                    def first_largest(v, n, onehot, most):
                        eq, low = buf(f"eq{n}", NT, n), buf("low", NT)
                        do(e.tensor_reduce(most, v, AX.X, ALU.max))
                        do(e.tensor_tensor(eq, v, over(most.unsqueeze(2), NT, n), ALU.is_equal))
                        do(e.scalar_tensor_tensor(eq, eq, -64.0, over(iota8[:, 0:n].unsqueeze(1), NT, n), ALU.mult, ALU.add))
                        do(e.tensor_reduce(low, eq, AX.X, ALU.min))
                        do(e.tensor_tensor(onehot, eq, over(low.unsqueeze(2), NT, n), ALU.is_equal))

                    dve.settle()
                    g_one, g_most = buf("g_one", NT, EG), buf("g_most", NT)
                    first_largest(lg[:, :, 0:EG], EG, g_one, g_most)
                    do(e.tensor_tensor(g_exp(st), lg[:, :, 0:EG], over(g_most.unsqueeze(2), NT, EG), ALU.subtract), "g_arg")
                    el = lg[:, :, EG:].rearrange("p t (g x) -> p t g x", g=EG)
                    prod, within = buf("prod", NT, EG, EPG), buf("within", NT, EPG)
                    g_wide = over(g_one.unsqueeze(3), NT, EG, EPG)
                    do(e.tensor_tensor(prod, el, g_wide, ALU.mult))
                    do(e.tensor_reduce(within, prod.rearrange("p t g x -> p t x g"), AX.X, ALU.add))
                    one, most = [buf(f"one{k}", NT, EPG) for k in range(2)], [buf(f"most{k}", NT) for k in range(2)]
                    first_largest(within, EPG, one[0], most[0])
                    do(e.scalar_tensor_tensor(within, one[0], -BIG, within, ALU.mult, ALU.add))
                    first_largest(within, EPG, one[1], most[1])
                    do(e.tensor_tensor(e_exp(st), most[1], most[0], ALU.subtract), "e_arg")
                    hot = [buf(f"hot{k}", NT, EG, EPG) for k in range(2)]
                    for k in range(2):
                        do(e.tensor_tensor(hot[k], over(one[k].unsqueeze(2), NT, EG, EPG), g_wide, ALU.mult))
                    flat = [buf(f"hot{k}", NT * NE) for k in range(2)]
                    do(e.tensor_tensor(buf("both", NT * NE), flat[0], flat[1], ALU.add), "chosen")
                    psum_, pg, den = buf("g_sum", NT), buf("pg", NT), buf("den", NT)
                    st.wait(e, st.act, "g_exp")
                    do(e.tensor_reduce(psum_, g_exp(st), AX.X, ALU.add))
                    st.wait(e, st.act, "e_exp")
                    do(e.tensor_scalar(den, e_exp(st), 1.0, None, ALU.add))
                    do(e.tensor_tensor(den, den, psum_, ALU.mult))
                    do(e.reciprocal(self.gates[:, 0:NT], den))
                    do(e.tensor_tensor(self.gates[:, NT:], self.gates[:, 0:NT], e_exp(st), ALU.mult))
                    st.wait(e, st.pe, "ranked")
                    rank, tot = buf("rank", NT, NE), buf("tot", NT, NE)
                    upto, cnt = buf("before_tile", NT, NE), buf("cnt", NE)
                    do(e.tensor_copy(tot, total[:, HALF:HALF + NT * NE].rearrange("p (t x) -> p t x", x=NE)))
                    do(e.memset(upto[:, 0, :], 0.0))
                    for t in range(1, NT):
                        do(e.tensor_tensor(upto[:, t, :], upto[:, t - 1, :], tot[:, t - 1, :], ALU.add))
                    do(e.tensor_tensor(cnt, upto[:, NT - 1, :], tot[:, NT - 1, :], ALU.add))
                    do(e.tensor_tensor(rank, total[:, 0:NT * NE].rearrange("p (t x) -> p t x", x=NE), upto, ALU.add))
                    more, nb = buf("more", NE, NT), buf("nb", NE)
                    do(e.tensor_tensor(more, over(cnt.unsqueeze(2), NE, NT), over(self.const("iota8x128").unsqueeze(1), NE, NT), ALU.is_gt))
                    do(e.tensor_reduce(nb, more, AX.X, ALU.add))
                    run = [buf("run0", NE), buf("run1", NE)]
                    do(e.tensor_copy(run[0], nb))
                    for n, w in enumerate((1, 2, 4, 8, 16)):
                        a, o = run[n % 2], run[1 - n % 2]
                        do(e.tensor_copy(o[:, 0:w], a[:, 0:w]))
                        do(e.tensor_tensor(o[:, w:], a[:, w:], a[:, 0:NE - w], ALU.add))
                    end, start = run[1], buf("start", NE)
                    do(e.tensor_tensor(start, end, nb, ALU.subtract))
                    do(e.tensor_scalar(start, start, float(P), float(P), ALU.mult, ALU.add))
                    do(e.tensor_tensor(rank, rank, over(start.unsqueeze(1), NT, NE), ALU.add))
                    slot = buf("slot", 2, NT)
                    for k in range(2):
                        do(e.tensor_tensor(flat[k], flat[k], buf("rank", NT * NE), ALU.mult))
                        do(e.tensor_reduce(slot[:, k, :], buf(f"hot{k}", NT, NE), AX.X, ALU.add))
                    do(e.tensor_copy(self.slots[:, :], buf("slot", 2 * NT)), "slots")
                    ended, expert = buf("ended", NBLK + 1, NE), buf("expert", NBLK + 1)
                    do(e.tensor_tensor(ended, over(end.unsqueeze(1), NBLK + 1, NE), over(self.const("iotab").unsqueeze(2), NBLK + 1, NE), ALU.is_le))
                    do(e.tensor_reduce(expert, ended, AX.X, ALU.add))
                    do(e.tensor_scalar(expert, expert, float(NE - 1), None, ALU.min))
                    do(e.tensor_copy(self.blocks[:, 0:NBLK + 1], expert))
                    do(e.tensor_copy(self.blocks[:, NBLK + 1:], end[:, NE - 1:NE]))
                    st.wait(e, st.pe, "rows")
                    do(e.tensor_copy(self.rows[:, :], pl[0][:, 0:NBLK + 2]))

    def experts(self):
        ins = self.ins
        U, RING = KT + FF // P, 6
        with self.stage("moe") as st:
            raw = st.sb("raw", [P, U, D])
            hi, lo = self.xh, self.xl
            xt = [a[:, RING, :] for a in (hi, lo)]
            at = [a[:, RING + 1, 0:FF] for a in (hi, lo)]
            xg = st.sb("xg", [P, D])
            idx = st.sb("idx", [P, 1], I32)
            sg, act_ = st.sb("sg", [P, FF]), st.sb("act", [P, FF])
            ysb = st.sb("ysb", [P, D])
            hu, yp, xturn = st.ps("hu", [P, 2 * FF]), st.ps("y", [P, D]), st.ps("xturn", [P, D])
            aturn = st.ps("aturn", [P, FF])
            s_w = [st.sem(f"w{u}") for u in range(U)]
            s_g, s_y, s_last = st.sem("gathered"), st.sem("y_out"), st.sem("last_rows")
            blocks = lambda e: e.value_load(self.blocks[0:1, NBLK + 1:NBLK + 2], min_val=2 * T // P, max_val=NBLK)
            with st.block() as blk:
                @blk.sync
                def _(e):
                    n = blocks(e)
                    with e.Fori(0, NBLK) as i:
                        with e.If(i < n):
                            ex = e.value_load(self.blocks[0:1, bass.ds(i, 1)], min_val=0, max_val=NE - 1)
                            for u in range(U):
                                st.wait(e, st.dve, f"lo{u}", i - 1)
                                src = ins["w13"][ex, u * P:(u + 1) * P, :] if u < KT else ins["w2"][ex, (u - KT) * P:(u - KT + 1) * P, :]
                                e.dma_start(raw[:, u, :], src).then_inc(s_w[u], 16)

                @blk.gpsimd
                def _(e):
                    st.pool.start(e)
                    n = blocks(e)

                    def gather(name, i=None):
                        e.nop(nofuse=True)
                        st.pool(e.tensor_copy(idx[:, :], self.rows[:, 1:2] if i is None else self.rows[:, bass.ds(i + 2, 1)]), name)
                        st.pool.settle()
                        e.nop(nofuse=True)
                        e.indirect_dma_start(out=xg[:, :], out_offset=None, in_=self.h_dram,
                                             in_offset=bass.IndirectOffsetOnAxis(ap=idx[:, 0:1], axis=0)).then_inc(s_g, 16)
                    gather("idx_first")
                    st.wait(e, st.pe, "x_first")
                    with st.pool.loop(NBLK) as i:
                        with e.If(i < n):
                            e.wait_ge(s_g, 16 * i + 16)
                            st.wait(e, st.pe, "x_turned", i - 1)
                            gather("idx", i)

                @blk.tensor
                def _(e):
                    st.pe.start(e)
                    n = blocks(e)

                    def turn_x():
                        for k in range(KT):
                            m = e.transpose(xturn[:, k * P:(k + 1) * P], xg[:, k * P:(k + 1) * P], self.const("ident"))
                        return m

                    def product(i, u, x, k, out):
                        st.wait(e, st.dve, f"lo{u}", i)
                        r = u % RING
                        last = (u == KT - 1) or (u == U - 1)
                        first = u in (0, KT)
                        for h in range(0, D, HALF):
                            for t, (a, w) in enumerate(((x[0], hi), (x[0], lo), (x[1], hi))):
                                m = e.matmul(out[:, h:h + HALF], a[:, k * P:(k + 1) * P], w[:, r, h:h + HALF],
                                             start=first and t == 0, stop=last and t == 2)
                        st.pe(m, f"mm{u}")
                    for k in range(D // P):
                        m = e.transpose(yp[:, k * P:(k + 1) * P], self.const("ident"), self.const("ident"))
                    st.pe(m, "y_none")
                    e.wait_ge(s_g, 16)
                    st.pe(turn_x(), "x_first")
                    st.wait(e, st.dve, "x_lo_first")
                    with st.pe.loop(NBLK) as i:
                        with e.If(i < n):
                            st.wait(e, st.dve, "x_lo", i - 1)
                            for u in range(KT):
                                product(i, u, xt, u, hu)
                            e.wait_ge(s_g, 16 * i + 32)
                            st.pe(turn_x(), "x_turned")
                            st.wait(e, st.dve, "act", i)
                            for k in range(FF // P):
                                m = e.transpose(aturn[:, k * P:(k + 1) * P], act_[:, k * P:(k + 1) * P], self.const("ident"))
                            st.pe(m, "a_turned")
                            st.wait(e, st.dve, "a_lo", i)
                            st.wait(e, st.act, "y0", i)
                            st.wait(e, st.dve, "y1", i)
                            for u in range(KT, U):
                                product(i, u, at, u - KT, yp)

                @blk.scalar
                def _(e):
                    st.act.start(e)
                    n = blocks(e)
                    e.sem_inc(s_y, 16)

                    def high(i, u):
                        e.wait_ge(s_w[u], 16 * i + 16)
                        prev, j = (u - RING, i) if u >= RING else (u + RING, i - 1)
                        st.wait(e, st.pe, f"mm{prev}", j)
                        st.act(e.activation(hi[:, u % RING, :], raw[:, u, :], ACT.Copy), f"hi{u}")

                    def rows_out(i):
                        e.wait_ge(s_y, 16 * i + 16)
                        return e.activation(ysb[:, 0:HALF], yp[:, 0:HALF], ACT.Copy)

                    def send(i):
                        e.dma_start(self.y_dram[bass.ds(i * P, P), :], ysb[:, :]).then_inc(s_y, 16)
                    e.preload_act_table(ACT.Silu)
                    st.wait(e, st.pe, "x_first")
                    st.act(e.activation(xt[0], xturn[:, :], ACT.Copy), "x_hi_first")
                    st.wait(e, st.pe, "y_none")
                    with st.act.loop(NBLK) as i:
                        with e.If(i < n):
                            for u in range(10):
                                high(i, u)
                                if u == 2:
                                    st.wait(e, st.pe, f"mm{U - 1}", i - 1)
                                    st.act(rows_out(i), "y0")
                                if u == 3:
                                    st.wait(e, st.act, "y0", i)
                                    st.wait(e, st.dve, "y1", i)
                                    send(i)
                            st.wait(e, st.pe, "mm7", i)
                            st.act(e.activation(sg[:, :], hu[:, 0:FF], ACT.Silu), "silu")
                            st.wait(e, st.pe, "a_turned", i)
                            st.act(e.activation(at[0], aturn[:, :], ACT.Copy), "a_hi")
                            st.wait(e, st.pe, "x_turned", i)
                            st.act(e.activation(xt[0], xturn[:, :], ACT.Copy), "x_hi")
                            for u in range(10, U):
                                high(i, u)
                    st.wait(e, st.pe, f"mm{U - 1}", n - 1)
                    rows_out(n).then_inc(s_last, 1)
                    e.wait_ge(s_last, 2)
                    send(n)
                    e.wait_ge(s_y, 16 * n + 32)
                    e.nop(nofuse=True)

                @blk.vector
                def _(e):
                    st.dve.start(e)
                    n = blocks(e)

                    def low(i, u):
                        st.wait(e, st.act, f"hi{u}", i)
                        r = u % RING
                        st.dve(e.tensor_tensor(lo[:, r, :], raw[:, u, :], hi[:, r, :].bitcast(F32), ALU.subtract), f"lo{u}")
                    st.wait(e, st.act, "x_hi_first")
                    st.dve(e.tensor_tensor(xt[1], xturn[:, :], xt[0].bitcast(F32), ALU.subtract), "x_lo_first")
                    st.wait(e, st.pe, "y_none")
                    with st.dve.loop(NBLK) as i:
                        with e.If(i < n):
                            for u in range(10):
                                low(i, u)
                                if u == 2:
                                    st.wait(e, st.pe, f"mm{U - 1}", i - 1)
                                    e.wait_ge(s_y, 16 * i + 16)
                                    st.dve(e.tensor_copy(ysb[:, HALF:], yp[:, HALF:]), "y1")
                            st.wait(e, st.act, "silu", i)
                            st.dve(e.tensor_tensor(act_[:, :], sg[:, :], hu[:, FF:2 * FF], ALU.mult), "act")
                            st.wait(e, st.act, "a_hi", i)
                            st.dve(e.tensor_tensor(at[1], aturn[:, :], at[0].bitcast(F32), ALU.subtract), "a_lo")
                            st.wait(e, st.act, "x_hi", i)
                            st.dve(e.tensor_tensor(xt[1], xturn[:, :], xt[0].bitcast(F32), ALU.subtract), "x_lo")
                            for u in range(10, U):
                                low(i, u)
                    st.wait(e, st.pe, f"mm{U - 1}", n - 1)
                    e.wait_ge(s_y, 16 * n + 16)
                    e.tensor_copy(ysb[:, HALF:], yp[:, HALF:]).then_inc(s_last, 1)

    def combine(self):
        x = self.x
        with self.stage("comb") as st:
            ys = [st.sb(f"y{k}", [P, 2, D]) for k in range(2)]
            idx = st.sb("idx", [P, 4], I32)
            sq, tmp = st.sb("sq", [P, 2, KT * P]), st.sb("tmp", [P, KT * P])
            turned = [st.ps(f"turned{b}", [P, D]) for b in range(2)]
            s_g = [st.sem(f"g{b}") for b in range(2)]
            t3 = lambda a: a.rearrange("p (k t) -> p k t", k=KT)
            gate = self.mod[:, 40:48].unsqueeze(2).to_broadcast([P, KT, P])
            with st.block() as blk:
                @blk.gpsimd
                def _(e):
                    st.pool.start(e)
                    with st.pool.loop(NT // 2) as i:
                        for b in range(2):
                            st.wait(e, st.pe, f"turned{b}", i - 1)
                            e.nop(nofuse=True)
                            for k in range(2):
                                st.pool(e.tensor_copy(idx[:, 2 * b + k:2 * b + k + 1], self.slots[:, bass.ds(2 * i + (b + k * NT), 1)]))
                            st.pool.settle()
                            e.nop(nofuse=True)
                            for k in range(2):
                                e.indirect_dma_start(out=ys[k][:, b, :], out_offset=None, in_=self.y_dram,
                                                     in_offset=bass.IndirectOffsetOnAxis(ap=idx[:, 2 * b + k:2 * b + k + 1], axis=0)).then_inc(s_g[b], 16)

                @blk.tensor
                def _(e):
                    st.pe.start(e)
                    with st.pe.loop(NT // 2) as i:
                        for b in range(2):
                            st.wait(e, st.dve, f"mixed{b}", i)
                            st.wait(e, st.dve, f"gated{b}", i - 1)
                            for k in range(KT):
                                m = e.transpose(turned[b][:, k * P:(k + 1) * P], ys[0][:, b, k * P:(k + 1) * P], self.const("ident"))
                            st.pe(m, f"turned{b}")

                @blk.scalar
                def _(e):
                    st.act.start(e)
                    with st.act.loop(NT // 2) as i:
                        for b in range(2):
                            ts = bass.ds(2 * P * i + P * b, P)
                            st.wait(e, st.dve, f"x{b}", i)
                            st.wait(e, st.dve, f"sum{b}", i - 1)
                            st.act(e.activation(t3(sq[:, b, :]), x[:, :, ts], ACT.Square), f"sq{b}")

                @blk.vector
                def _(e):
                    st.dve.start(e)
                    with st.dve.loop(NT // 2) as i:
                        for b in range(2):
                            ts = bass.ds(2 * P * i + P * b, P)
                            g = [self.gates[:, bass.ds(2 * i + (b + k * NT), 1)] for k in range(2)]
                            y0, y1 = (y[:, b, :] for y in ys)
                            e.wait_ge(s_g[b], 32 * i + 32)
                            st.dve(e.tensor_scalar(y0, y0, g[0], None, ALU.mult))
                            st.dve.settle()
                            st.dve(e.scalar_tensor_tensor(y0, y1, g[1], y0, ALU.mult, ALU.add), f"mixed{b}")
                            st.wait(e, st.pe, f"turned{b}", i)
                            st.dve(e.tensor_tensor(t3(tmp[:, :]), t3(turned[b][:, :]), gate, ALU.mult), f"gated{b}")
                            st.dve.settle()
                            st.dve(e.tensor_tensor(x[:, :, ts], x[:, :, ts], t3(tmp[:, :]), ALU.add), f"x{b}")
                            st.wait(e, st.act, f"sq{b}", i)
                            st.dve(e.tensor_reduce(self.acc_sq[:, ts], sq[:, b, :].rearrange("p (k t) -> p t k", k=KT), AX.X, ALU.add), f"sum{b}")
        self.rkeep.close()

    def attention_in(self):
        self.keep = ExitStack()
        with self.stage("renorm") as st:
            rstd, tmp, sq = st.sb("rstd", [P, T]), st.sb("tmp", [P, 4, T]), st.sb("sq", [P, 2, T])
            total = st.ps("total", [P, T])
            pe1, dve1, act1 = self.rstd(st, self.acc_sq, total, rstd, "rstd_a", after=lambda e: None)
            sq_act, sq_dve = self.sum_squares(st, sq, self.acc_sq, ready=lambda e: st.wait(e, st.dve, "normed"))
            pe2, dve2, act2 = self.rstd(st, self.acc_sq, total, rstd, "rstd_b", after=lambda e: st.wait(e, st.dve, "sq_added7"))
            sc_dve, sc_act, sc_pool = self.scale_split(st, rstd, self.col("norm_mix", 0, KT), None, tmp, "rstd_b")
            with st.block() as blk:
                @blk.tensor
                def _(e):
                    st.pe.start(e)
                    pe1(e)
                    pe2(e)

                @blk.scalar
                def _(e):
                    st.act.start(e)
                    act1(e)
                    sq_act(e)
                    act2(e)
                    sc_act(e)

                @blk.gpsimd
                def _(e):
                    st.pool.start(e)
                    sc_pool(e)

                @blk.vector
                def _(e):
                    st.dve.start(e)
                    dve1(e)
                    st.wait(e, st.act, "rstd_a")
                    for k in range(KT):
                        st.dve(e.scalar_tensor_tensor(self.x[:, k, :], self.x[:, k, :], self.col("final_norm_w", k), rstd[:, :],
                                                      ALU.mult, ALU.mult), "normed" if k == KT - 1 else None)
                    sq_dve(e)
                    st.dve.settle()
                    dve2(e)
                    sc_dve(e)
        QKV = (Q_HEADS + 2 * KV_HEADS) * HD // P
        self.qkv = self.keep.enter_context(self.nc.sbuf_tensor("qkv", [P, QKV, T], F32))
        with self.stage("qkv") as st:
            g = Gemm(st)
            with st.block() as blk:
                @blk.sync
                def _(e):
                    with e.Fori(0, QKV // 2) as i:
                        for b in range(2):
                            g.load(e, i, 0, b, self.ins["w_qkv"][2 * i + b])

                @blk.gpsimd
                def _(e):
                    e.sem_inc(g.s_split, 2)
                    with e.Fori(0, QKV // 2) as i:
                        for b in range(2):
                            g.split(e, i, 0, b)

                @blk.tensor
                def _(e):
                    e.sem_inc(g.s_mult, 2)
                    with e.Fori(0, QKV // 2) as i:
                        for b in range(2):
                            g.mult(e, i, 0, b, self.xh, self.xl)

                @blk.scalar
                def _(e):
                    e.sem_inc(g.s_emptied, 2)
                    with e.Fori(0, QKV // 2) as i:
                        for b in range(2):
                            g.ready(e, i, 0, b)
                            g.empty(e.activation(tile_of(self.qkv, i, b), g.acc[b][:, :], ACT.Copy))

    def attention(self):
        qkv, QT, G4 = self.qkv, Q_HEADS * HD // P, Q_HEADS // KV_HEADS
        K0, V0 = QT, QT + 2
        LEAD = 2 * KV_HEADS
        with self.stage("att") as st:
            bias = st.sb("bias", [P, Q_HEADS, 2 * P])
            dist = st.sb("dist", [P, 2, 2 * P])
            qs, vs = st.sb("qs", [P, QT, P]), st.sb("vs", [P, 2, KV_HEADS * HD])
            vtok = qkv[:, V0:V0 + 2, :].rearrange("p k (t d) -> p (k t) d", d=KV_HEADS * HD)
            p = st.sb("p", [P, KV_HEADS, G4 * 2 * P])
            pt = st.sb("pt", [P, 2, 2 * HALF])
            diag = st.sb("diag", [P, KV_HEADS, G4 * P])
            small = lambda name: st.sb(name, [P, KV_HEADS, G4])
            ks = dist
            mx, neg, sums, esink, rden = (small(n) for n in ("mx", "neg", "sums", "esink", "rden"))
            nsink = self.cols[:, COLS["sinks"]].rearrange("p (j h) -> p j h", h=G4)
            sc = [st.ps(f"scores{b}", [P, G4 * 2 * P]) for b in range(2)]
            tp = st.ps("turned", [P, 2 * HALF])
            op = [st.ps(f"o{b}", [P, HALF]) for b in range(2)]
            s_dist, s_setup, s_vturned, s_vtok = (st.sem(n) for n in ("dist", "setup", "v_turned", "vtok"))
            owner = {"pe": ("scores", "turned", "pv"), "act": ("exp", "pt_prev", "o_hi"),
                     "dve": ("scored", "maxed", "neg", "shift", "den", "rden", "pt_cur", "o_lo"),
                     "pool": ("diag", "q_staged", "v_staged")}
            sem = {n: st.sem("s_" + n) for names in owner.values() for n in names}
            mask_slopes = [2.0 ** (-8.0 * (h + 1) / Q_HEADS) for h in range(Q_HEADS)]

            def start(e, eng):
                for n in owner[eng]:
                    e.sem_inc(sem[n], LEAD)

            def done(ins, name):
                ins.then_inc(sem[name], 1)

            def wait(e, name, g):
                e.wait_ge(sem[name], g + (LEAD + 1))

            def cols(n):
                return slice(0, P) if isinstance(n, int) and n == 0 else bass.ds(n * P, P)

            def is_first(n):
                return isinstance(n, int) and n == 0

            def keys(n):
                return slice(P, 2 * P) if is_first(n) else slice(0, 2 * P)

            def blocks(e, body):
                body(0, False)
                with e.Fori(0, NT - 2) as m:
                    body(m + 1, False)
                body(NT - 1, True)

            def ahead(n, j, k, last, f):
                if not (last and j + k >= KV_HEADS):
                    f(n + (j + k) // KV_HEADS, (j + k) % KV_HEADS)

            heads = lambda a: a.rearrange("p (h k) -> p h k", h=G4)
            half = lambda j: slice(64 * (j % 2), 64 * (j % 2) + 64)
            with st.block() as blk:
                @blk.sync
                def _(e):
                    e.dma_start(dist[:, :, :], self.ins["dist"]).then_inc(s_dist, 16)

                @blk.gpsimd
                def _(e):
                    start(e, "pool")

                    def stage_q(n, jj):
                        wait(e, "scores", 4 * n + (2 * jj - 3))
                        e.nop(nofuse=True)
                        k = slice(0, P) if is_first(n) else bass.ds((n - 1) * P, 2 * P)
                        e.tensor_copy(ks[:, jj, keys(n)], qkv[:, K0 + jj, k])
                        done(e.tensor_copy(qs[:, G4 * jj:G4 * (jj + 1), :], qkv[:, G4 * jj:G4 * (jj + 1), cols(n)]), "q_staged")

                    def stage_v(n, jj):
                        wait(e, "pv", 4 * n + (2 * jj - 3))
                        e.nop(nofuse=True)
                        c = slice(jj * P, (jj + 1) * P)
                        if is_first(n):
                            done(e.tensor_copy(vs[:, 1, c], vtok[:, 0, c]), "v_staged")
                        else:
                            done(e.tensor_copy(vs[:, :, c], vtok[:, bass.ds(n - 1, 2), c]), "v_staged")

                    def make_diag(n, j):
                        wait(e, "rden", 4 * n + j)
                        e.nop(nofuse=True)
                        done(e.tensor_tensor(heads(diag[:, j, :]), self.const("ident").unsqueeze(1).to_broadcast([P, G4, P]),
                                             rden[:, j, :].unsqueeze(2).to_broadcast([P, G4, P]), ALU.mult), "diag")

                    def body(n, last):
                        for j in range(KV_HEADS):
                            if j == 0 and not last:
                                stage_q(n + 1, 0)
                            ahead(n, j, 2, last, make_diag)
                            if j == 0:
                                stage_v(n, 1)
                            elif j == 1 and not last:
                                stage_q(n + 1, 1)
                            elif j == 3 and not last:
                                stage_v(n + 1, 0)
                    e.wait_ge(s_setup, Q_HEADS + 1)
                    stage_q(0, 0)
                    stage_q(0, 1)
                    e.wait_ge(s_vtok, 2)
                    stage_v(0, 0)
                    make_diag(0, 0)
                    make_diag(0, 1)
                    blocks(e, body)

                @blk.tensor
                def _(e):
                    start(e, "pe")

                    def scores(n, j):
                        b, jj = j % 2, j // 2
                        wait(e, "q_staged", 2 * n + jj)
                        wait(e, "scored", 4 * n + (j - 2))
                        for h in range(G4):
                            m = e.matmul(heads(sc[b][:, :])[:, h, keys(n)], qs[half(j), G4 * jj + h, :],
                                         ks[half(j), jj, keys(n)], start=True, stop=True)
                        done(m, "scores")

                    def body(n, last):
                        for j in range(KV_HEADS):
                            b, jj, g = j % 2, j // 2, 4 * n + j
                            ws = (1,) if is_first(n) else (0, 1)
                            wait(e, "diag", g)
                            wait(e, "pt_prev", g - 1)
                            wait(e, "pt_cur", g - 1)
                            for w in ws:
                                for h in range(G4):
                                    m = e.matmul(tp[:, w * HALF + h * P:w * HALF + (h + 1) * P],
                                                 p[:, j, (2 * h + w) * P:(2 * h + w + 1) * P],
                                                 diag[:, j, h * P:(h + 1) * P], start=True, stop=True)
                            done(m, "turned")
                            ahead(n, j, 3, last, scores)
                            wait(e, "pt_prev", g)
                            wait(e, "pt_cur", g)
                            wait(e, "v_staged", 2 * n + jj)
                            wait(e, "o_lo", g - 2)
                            for w in ws:
                                m = e.matmul(op[b][:, :], vs[:, w, jj * P:(jj + 1) * P], pt[:, b, w * HALF:(w + 1) * HALF],
                                             start=(w == ws[0]), stop=(w == 1))
                            done(m, "pv")
                    for s in range(2):
                        for t in range(NT // 2):
                            for k in range(2):
                                m = e.transpose(sc[s][:, (2 * t + k) * P:(2 * t + k + 1) * P],
                                                qkv[:, V0 + k, (NT // 2 * s + t) * P:(NT // 2 * s + t + 1) * P], self.const("ident"))
                        m.then_inc(s_vturned, 1)
                    e.wait_ge(s_vtok, 2)
                    for j in range(3):
                        scores(0, j)
                    blocks(e, body)

                @blk.scalar
                def _(e):
                    start(e, "act")

                    def exps(n, j):
                        wait(e, "shift", 4 * n + j)
                        e.activation(esink[:, j, :], esink[:, j, :], ACT.Exp)
                        for h in range(G4):
                            a = heads(p[:, j, :])[:, h, keys(n)]
                            m = e.activation(a, a, ACT.Exp, bias=neg[:, j, h:h + 1], accum_out=sums[:, j, h:h + 1])
                        done(m, "exp")

                    def body(n, last):
                        for j in range(KV_HEADS):
                            b, jj, g = j % 2, j // 2, 4 * n + j
                            if is_first(n):
                                e.sem_inc(sem["pt_prev"], 1)
                            else:
                                wait(e, "turned", g)
                                wait(e, "pv", g - 2)
                                done(e.activation(pt[:, b, 0:HALF], tp[:, 0:HALF], ACT.Copy), "pt_prev")
                            ahead(n, j, 2, last, exps)
                            wait(e, "pv", g)
                            done(e.activation(self.xh[half(j), G4 * jj:G4 * (jj + 1), cols(n)], heads(op[b][half(j), :]), ACT.Copy), "o_hi")
                    e.wait_ge(s_vturned, 2)
                    for s in range(2):
                        e.activation(vtok[:, NT // 2 * s:NT // 2 * (s + 1), :].rearrange("p t d -> p (t d)"), sc[s][:, :],
                                     ACT.Copy).then_inc(s_vtok, 1)
                    exps(0, 0)
                    exps(0, 1)
                    blocks(e, body)

                @blk.vector
                def _(e):
                    start(e, "dve")

                    def score(n, j):
                        g = 4 * n + j
                        wait(e, "scores", g)
                        wait(e, "turned", g - 4)
                        v = heads(p[:, j, :])[:, :, keys(n)]
                        done(e.scalar_tensor_tensor(v, heads(sc[j % 2][:, :])[:, :, keys(n)], HD ** -0.5,
                                                    bias[:, G4 * j:G4 * j + G4, keys(n)], ALU.mult, ALU.add), "scored")
                        wait(e, "scored", g)
                        done(e.tensor_reduce(mx[:, j, :], v, AX.X, ALU.max), "maxed")
                        wait(e, "maxed", g)
                        done(e.scalar_tensor_tensor(neg[:, j, :], mx[:, j, :], -1.0, nsink[:, j, :], ALU.mult, ALU.min), "neg")
                        wait(e, "neg", g)
                        done(e.tensor_tensor(esink[:, j, :], neg[:, j, :], nsink[:, j, :], ALU.subtract), "shift")

                    def inverse(n, j):
                        g = 4 * n + j
                        wait(e, "exp", g)
                        done(e.tensor_tensor(sums[:, j, :], sums[:, j, :], esink[:, j, :], ALU.add), "den")
                        wait(e, "den", g)
                        done(e.reciprocal(rden[:, j, :], sums[:, j, :]), "rden")

                    def body(n, last):
                        for j in range(KV_HEADS):
                            b, jj, g = j % 2, j // 2, 4 * n + j
                            wait(e, "turned", g)
                            wait(e, "pv", g - 2)
                            done(e.tensor_copy(pt[:, b, HALF:], tp[:, HALF:]), "pt_cur")
                            ahead(n, j, 3, last, score)
                            ahead(n, j, 2, last, inverse)
                            wait(e, "o_hi", g)
                            x = slice(G4 * jj, G4 * (jj + 1))
                            done(e.tensor_tensor(self.xl[half(j), x, cols(n)], heads(op[b][half(j), :]),
                                                 self.xh[half(j), x, cols(n)].bitcast(F32), ALU.subtract), "o_lo")
                    e.wait_ge(s_dist, 16)
                    for h in range(Q_HEADS):
                        e.scalar_tensor_tensor(bias[:, h, :], dist[:, 0, :], mask_slopes[h], dist[:, 1, :], ALU.mult, ALU.add).then_inc(s_setup, 1)
                    e.tensor_scalar(nsink, nsink, -1.0, None, ALU.mult).then_inc(s_setup, 1)
                    e.wait_ge(s_setup, Q_HEADS + 1)
                    for j in range(3):
                        score(0, j)
                    inverse(0, 0)
                    inverse(0, 1)
                    blocks(e, body)
        self.keep.close()

    def feed_forward(self):
        x = self.x
        with self.stage("ffnorm") as st:
            rstd, tmp = st.sb("rstd", [P, T]), st.sb("tmp", [P, 4, T])
            total = st.ps("total", [P, T])
            pe1, dve1, act1 = self.rstd(st, self.acc_sq, total, rstd, after=lambda e: None)
            sc_dve, sc_act, sc_pool = self.scale_split(st, rstd, self.col("norm_ffn", 0, KT), None, tmp, "rstd")
            with st.block() as blk:
                @blk.tensor
                def _(e):
                    st.pe.start(e)
                    pe1(e)

                @blk.scalar
                def _(e):
                    st.act.start(e)
                    act1(e)
                    sc_act(e)

                @blk.gpsimd
                def _(e):
                    st.pool.start(e)
                    sc_pool(e)

                @blk.vector
                def _(e):
                    st.dve.start(e)
                    dve1(e)
                    sc_dve(e)
        with self.stage("ff") as st:
            g = Gemm(st)
            ah, al = st.sb("ah", [P, max(FF_PARTS), T], F32R), st.sb("al", [P, max(FF_PARTS), T], F32R)
            a, sq = st.sb("a", [P, T]), st.sb("sq", [P, T])
            parts, base, wide = [], 0, 0
            for n, w in enumerate(FF_PARTS):
                parts.append((n, w, wide, base, base + 2 * w))
                base += 2 * w + KT
                wide += w
            up, down = self.ins["w_up"], [self.ins[f"w_down{n}"] for n in range(len(FF_PARTS))]
            with st.block() as blk:
                @blk.sync
                def _(e):
                    for n, w, at, b_up, b_down in parts:
                        with e.Fori(0, w) as i:
                            for b in range(2):
                                g.load(e, i, b_up, b, up[2 * i + (2 * at + b)])
                        with e.Fori(0, KT // 2) as i:
                            for b in range(2):
                                g.load(e, i, b_down, b, down[n][2 * i + b], kt=w)

                @blk.gpsimd
                def _(e):
                    e.sem_inc(g.s_split, 2)
                    for n, w, at, b_up, b_down in parts:
                        with e.Fori(0, w) as i:
                            for b in range(2):
                                g.split(e, i, b_up, b)
                        with e.Fori(0, KT // 2) as i:
                            for b in range(2):
                                g.split(e, i, b_down, b, kt=w)

                @blk.tensor
                def _(e):
                    e.sem_inc(g.s_mult, 2)
                    for n, w, at, b_up, b_down in parts:
                        with e.Fori(0, w) as i:
                            for b in range(2):
                                g.mult(e, i, b_up, b, self.xh, self.xl)
                        st.wait(e, st.dve, f"a_lo{n}")
                        with e.Fori(0, KT // 2) as i:
                            for b in range(2):
                                g.mult(e, i, b_down, b, ah, al, kt=w)

                @blk.scalar
                def _(e):
                    st.act.start(e)
                    e.preload_act_table(ACT.Silu)
                    for n, w, at, b_up, b_down in parts:
                        e.wait_ge(g.s_mult, b_up + 2)
                        with st.act.loop(w) as i:
                            g.ready(e, i, b_up, 0)
                            g.emptied(e, i - 1, b_up, 1)
                            g.empty(e.activation(sq[:, :], g.acc[0][:, :], ACT.Silu))
                            g.emptied(e, i, b_up, 1)
                            st.act(e.activation(tile_of(ah, i, 0, 1), a[:, :], ACT.Copy), f"hi{n}")
                    with st.act.loop(KT // 2) as i:
                        for b in range(2):
                            g.emptied(e, i, parts[-1][4], b)
                            st.wait(e, st.dve, "sum1" if b == 0 else "sum0", i - 1 if b == 0 else i)
                            st.act(e.activation(sq[:, :], tile_of(x, i, b), ACT.Square), f"sq{b}")

                @blk.vector
                def _(e):
                    st.dve.start(e)
                    e.sem_inc(g.s_emptied, 2)
                    st.dve(e.memset(self.acc_sq[:, :], 0.0))
                    for n, w, at, b_up, b_down in parts:
                        with st.dve.loop(w) as i:
                            g.emptied(e, i, b_up, 0)
                            g.ready(e, i, b_up, 1)
                            st.dve.settle()
                            g.empty(e.tensor_tensor(a[:, :], sq[:, :], g.acc[1][:, :], ALU.mult))
                            st.wait(e, st.act, f"hi{n}", i)
                            g.emptied(e, i, b_up, 1)
                            st.dve(e.tensor_tensor(tile_of(al, i, 0, 1), a[:, :], tile_of(ah, i, 0, 1).bitcast(F32), ALU.subtract), f"a_lo{n}")
                        last = n == len(parts) - 1
                        with st.dve.loop(KT // 2) as i:
                            for b in range(2):
                                g.ready(e, i, b_down, b)
                                xn = tile_of(x, i, b)
                                g.empty(e.tensor_tensor(xn, g.acc[b][:, :], xn, ALU.add))
                                if last:
                                    st.wait(e, st.act, f"sq{b}", i)
                                    st.dve.settle()
                                    st.dve(e.tensor_tensor(self.acc_sq[:, :], self.acc_sq[:, :], sq[:, :], ALU.add), f"sum{b}")

    def finish(self):
        x = self.x
        with self.stage("out") as st:
            rstd, ost, otok = st.sb("rstd", [P, T]), st.sb("ost", [P, 2, KT * P]), st.sb("otok", [P, 2, D])
            total = st.ps("total", [P, T])
            turned = [st.ps(f"turned{b}", [P, D]) for b in range(2)]
            s_o = [st.sem(f"o{b}") for b in range(2)]
            pe1, dve1, act1 = self.rstd(st, self.acc_sq, total, rstd, after=lambda e: None)
            t3 = lambda a: a.rearrange("p (k t) -> p k t", k=KT)
            with st.block() as blk:
                @blk.sync
                def _(e):
                    for b in range(2):
                        e.sem_inc(s_o[b], 16)
                    with e.Fori(0, NT // 2) as i:
                        for b in range(2):
                            st.wait(e, st.act, f"otok{b}", i)
                            e.dma_start(self.out[bass.ds(2 * P * i + P * b, P), :], otok[:, b, :]).then_inc(s_o[b], 16)
                    for b in range(2):
                        e.wait_ge(s_o[b], 16 * (NT // 2) + 16)

                @blk.tensor
                def _(e):
                    st.pe.start(e)
                    pe1(e)
                    with st.pe.loop(NT // 2) as i:
                        for b in range(2):
                            st.wait(e, st.dve, f"scaled{b}", i)
                            st.wait(e, st.act, f"otok{b}", i - 1)
                            for k in range(KT):
                                m = e.transpose(turned[b][:, k * P:(k + 1) * P], ost[:, b, k * P:(k + 1) * P], self.const("ident"))
                            st.pe(m, f"turned{b}")

                @blk.scalar
                def _(e):
                    st.act.start(e)
                    act1(e)
                    with st.act.loop(NT // 2) as i:
                        for b in range(2):
                            st.wait(e, st.pe, f"turned{b}", i)
                            e.wait_ge(s_o[b], 16 * i + 16)
                            st.act(e.activation(otok[:, b, :], turned[b][:, :], ACT.Copy), f"otok{b}")

                @blk.vector
                def _(e):
                    st.dve.start(e)
                    dve1(e)
                    st.wait(e, st.act, "rstd")
                    w = self.col("final_norm", 0, KT).unsqueeze(2).to_broadcast([P, KT, P])
                    with st.dve.loop(NT // 2) as i:
                        for b in range(2):
                            ts = bass.ds(2 * P * i + P * b, P)
                            st.wait(e, st.pe, f"turned{b}", i - 1)
                            st.dve(e.tensor_tensor(t3(ost[:, b, :]), x[:, :, ts], rstd[:, ts].unsqueeze(1).to_broadcast([P, KT, P]), ALU.mult))
                            st.dve.settle()
                            st.dve(e.tensor_tensor(t3(ost[:, b, :]), t3(ost[:, b, :]), w, ALU.mult), f"scaled{b}")


def tiles(w, kt=None):
    K, N = w.shape
    return np.ascontiguousarray(w.reshape(K // P, P, N // P, P).transpose(2, 1, 0, 3)).reshape(N // P, P, K)


def layout(a):
    def per_tile(v):
        return v.reshape(-1, P).T
    f = np.float32
    first = a["w_in"][0]
    u, z, xbc, dt = np.split(first, [256, 1024, 2816], axis=1)
    pad = np.zeros((D, P - HEADS), f)
    heads = np.arange(Q_HEADS).reshape(2, 2, 4).transpose(0, 2, 1).reshape(-1)
    qcols = (heads[:, None] * HD + np.arange(HD)).reshape(-1)
    wqkv = a["swa_w_in_2"][0]
    wqkv = np.concatenate([wqkv[:, :Q_HEADS * HD][:, qcols], wqkv[:, Q_HEADS * HD:]], axis=1)
    gu = a["ffn_w_gate_up_2"][0]
    gu = gu.reshape(D, 2, FFT, P).transpose(0, 2, 1, 3).reshape(D, -1)
    cols = np.zeros((P, NCOLS), f)
    cols[:, COLS["b_ada"]] = per_tile(a["b_ada"][0])
    cols[:, COLS["c"]] = per_tile(a["c"][0])
    cols[:, COLS["conv_w"]] = a["conv_w"][0].reshape(CONV, CONV_T, P).transpose(2, 1, 0).reshape(P, -1)
    cols[:, COLS["conv_b"]] = per_tile(a["conv_b"][0])
    cols[:, COLS["d_skip"]] = per_tile(np.repeat(a["d_skip"][0], HD))
    cols[:, COLS["pool_scale"]] = per_tile(a["pool_scale"][0])
    cols[:, COLS["ssd_norm_w"]] = per_tile(a["ssd_norm_w"][0])
    cols[:, COLS["final_norm_w"]] = per_tile(a["final_norm_w"])
    cols[:, COLS["norm_mix"]] = per_tile(a["norm_mix_2"][0])
    cols[:, COLS["norm_ffn"]] = per_tile(a["norm_ffn_2"][0])
    cols[:, COLS["final_norm"]] = per_tile(a["final_norm_2"])
    cols[:, COLS["router_b"]] = np.concatenate([a["b_group"][0], a["b_router"][0]])[None]
    cols[:, COLS["sinks"]] = a["swa_sinks_2"][0][None]
    cols[:HEADS, COLS["dt_bias"]] = a["dt_bias"][0][:, None]
    cols[:HEADS, COLS["a_log"]] = a["a_log"][0][:, None]
    k = np.arange(P)
    consts = np.zeros((P, NCONST), f)
    consts[:, CONSTS["ident"]] = np.eye(P)
    consts[:, CONSTS["ones"]] = 1
    consts[:, CONSTS["upto"]] = k[:, None] <= k[None]
    consts[:, CONSTS["before"]] = k[:, None] < k[None]
    window = np.array([[2, 4], [8, 16]])[:, k // 64].T
    consts[:, CONSTS["pool_first"]] = (window[:, :, None] / np.minimum(np.arange(1, 17), window[:, :, None])).reshape(P, 32)
    consts[:, CONSTS["pool_inv"]] = 1.0 / window
    consts[:, CONSTS["iota8"]] = np.arange(8)
    consts[:, CONSTS["iota8x128"]] = np.arange(8) * P
    consts[:, CONSTS["iotab"]] = np.arange(NBLK + 1)
    consts[:, CONSTS["tokid"]] = k[:, None] + P * np.arange(NT)
    sel = np.zeros((HEADS, HEADS, P), f)
    sel[np.arange(HEADS), np.arange(HEADS)] = 1
    f3 = np.arange(3 * P).reshape(3, P) // (SSD_T * P // GROUPS)
    same = np.stack([f3[i][:, None] == f3[o][None] for i, o in ((0, 0), (1, 0), (0, 1), (1, 1), (2, 1), (1, 2), (2, 2))], 1)
    d = P + k[:, None] - np.arange(2 * P)[None]
    ok = (d >= 0) & (d < P)
    wpool = np.zeros((P, POOL_T, P), f)
    for g in range(4):
        wpool[64 * (g % 2):64 * (g % 2) + 64, g // 2, 64 * (g % 2):64 * (g % 2) + 64] = a["w_pool"][0, g]
    down = a["ffn_w_down_2"][0]
    at = np.cumsum((0,) + FF_PARTS) * P
    return {
        "cols": cols, "consts": consts, "sel": sel.reshape(HEADS, -1), "same": same.astype(f),
        "dist": np.stack([np.where(ok, -d, 0), np.where(ok, 0, -BIG)], 1).astype(f),
        "x": np.ascontiguousarray(a["x"][0]).reshape(NT, P, D),
        "w_ada": tiles(a["w_ada"][0]),
        "w_in": tiles(np.concatenate([xbc, z, dt, pad, u], axis=1)),
        "w_pool": wpool,
        "w_out": tiles(a["w_out"][0]),
        "w_route": np.ascontiguousarray(np.concatenate([a["w_group"][0], a["w_router"][0]], 1).reshape(KT, P, EG + NE).transpose(1, 0, 2)),
        "w13": np.ascontiguousarray(a["w13"][0]), "w2": np.ascontiguousarray(a["w2"][0]),
        "w_qkv": tiles(wqkv),
        "swa_w_out": tiles(a["swa_w_out_2"][0][qcols]),
        "w_up": tiles(gu),
        **{f"w_down{n}": tiles(down[at[n]:at[n + 1]]) for n in range(len(FF_PARTS))},
    }


def program(nc, shapes, counts):
    ins = {k: nc.dram_tensor(f"in_{k}", s, F32, kind="ExternalInput").ap() for k, s in shapes.items()}
    out = nc.dram_tensor("out", (T, D), F32, kind="ExternalOutput").ap()
    marks = {}
    Kernel(nc, ins, out, counts, marks).build()
    return marks


def kernel(**inputs):
    import concourse.bacc as bacc
    from concourse.bass_utils import run_bass_kernel_spmd
    arrays = layout({k: np.asarray(v) for k, v in inputs.items()})
    shapes = {k: v.shape for k, v in arrays.items()}
    counts = {}
    for _ in range(3):
        nc = bacc.Bacc("TRN2", target_bir_lowering=False, num_devices=1)
        counts = program(nc, shapes, counts)
    r = run_bass_kernel_spmd(nc, [{f"in_{k}": v for k, v in arrays.items()}], core_ids=[0])
    return r.results[0]["out"].reshape(1, T, D)
```

```python
from contextlib import ExitStack, contextmanager

import concourse.bass as bass
from concourse import mybir
import numpy as np

ALU = mybir.AluOpType
ACT = mybir.ActivationFunctionType
AX = mybir.AxisListType
F32 = mybir.dt.float32
F32R = mybir.dt.float32r
I32 = mybir.dt.int32

P = 128
T = 1024
D = 1024
KT = D // P
NT = T // P
HALF = 512
POOL_T, SSD_T, CONV_T = 2, 6, 14
CONV = 4
HEADS, HD, GROUPS, STATE = 12, 64, 4, 128
HPG = HEADS // GROUPS
CH = 128
NCH = T // CH
EG, EPG = 4, 8
NE = EG * EPG
FF = 512
NBLK = 2 * T // P + NE - 1
Q_HEADS, KV_HEADS = 16, 4
FFT = 2816 // P
FF_PARTS = (8, 8, 6)
EPS = 1e-6
BIG = 3.0e38
MOD_FIRST = 6
CREDIT = 400

COLS = {}
_at = 0
for _n, _w in (("b_ada", 48), ("conv_w", CONV_T * CONV), ("conv_b", CONV_T), ("d_skip", SSD_T),
               ("pool_scale", POOL_T), ("ssd_norm_w", SSD_T), ("final_norm_w", KT), ("norm_mix", KT),
               ("norm_ffn", KT), ("final_norm", KT), ("router_b", EG + NE), ("sinks", Q_HEADS),
               ("dt_bias", 1), ("a_log", 1)):
    COLS[_n] = slice(_at, _at + _w)
    _at += _w
NCOLS = _at
CONSTS = {}
_at = 0
for _n, _w in (("ident", P), ("ones", P), ("upto", P), ("before", P), ("pool_first", 32), ("pool_inv", 2),
               ("iota8", 8), ("iota8x128", 8), ("iotab", NBLK + 1), ("tokid", NT)):
    CONSTS[_n] = slice(_at, _at + _w)
    _at += _w
NCONST = _at


class Lane:

    def __init__(self, stage, key):
        self.stage, self.key = stage, key
        self.sem = stage.sem("n_" + key)
        self.count, self.i, self.per, self.base, self.loops = CREDIT, None, 0, 0, 0

    def start(self, eng):
        self.e = eng
        eng.sem_inc(self.sem, CREDIT)
        return eng

    def at(self):
        return self.count if self.i is None else self.i * self.per + self.count

    def __call__(self, ins, name=None):
        ins.then_inc(self.sem, 1)
        self.count += 1
        if name:
            self.stage.marks[self.stage.name, self.key, name] = (self.count, self.per, self.trips if self.i is not None else 0)
        return ins

    def settle(self):
        self.e.wait_ge(self.sem, self.at())

    @contextmanager
    def loop(self, trips):
        key = (self.stage.name, self.key, "loop", self.loops)
        self.loops += 1
        start = self.count
        self.per = self.stage.counts.get(key, 1)
        self.trips = trips
        with self.e.Fori(0, trips) as i:
            self.i = i
            yield i
            self.i = None
        self.stage.marks[key] = self.count - start
        self.count = start + trips * self.per
        self.per = 0


class Stage:

    def __init__(self, nc, name, counts, marks):
        self.nc, self.name, self.counts, self.marks = nc, name, counts, marks
        self.ctx, self.sems, self.open = ExitStack(), [], False

    def __enter__(self):
        if self.open:
            return self
        self.open = True
        self.pe, self.act, self.dve, self.pool = (Lane(self, k) for k in ("pe", "act", "dve", "pool"))
        return self

    def __exit__(self, *a):
        self.ctx.close()

    def sb(self, name, shape, dt=F32):
        return self.ctx.enter_context(self.nc.sbuf_tensor(f"{self.name}_{name}", shape, dt))

    def ps(self, name, shape, dt=F32):
        return self.ctx.enter_context(self.nc.psum_tensor(f"{self.name}_{name}", shape, dt))

    def sem(self, name):
        self.sems.append(self.ctx.enter_context(self.nc.semaphore(f"{self.name}_{name}")))
        return self.sems[-1]

    def block(self):
        return self.nc.Block()

    def wait(self, eng, lane, name, i=None):
        count, per, trips = self.counts.get((self.name, lane.key, name), (CREDIT + 1, 0, 0))
        if trips and i is None:
            i = trips - 1
        eng.wait_ge(lane.sem, count + per * i if trips and per else count)


class Steps:

    def __init__(self, st, lead, owner):
        self.lead, self.owner = lead, owner
        self.sem = {n: st.sem("s_" + n) for names in owner.values() for n in names}

    def start(self, e, eng):
        for n in self.owner[eng]:
            e.sem_inc(self.sem[n], self.lead)

    def done(self, ins, name):
        ins.then_inc(self.sem[name], 1)

    def skip(self, e, name):
        e.sem_inc(self.sem[name], 1)

    def wait(self, e, name, step):
        e.wait_ge(self.sem[name], step + (self.lead + 1))


class Gemm:

    def __init__(self, st, kt=KT, psum=True):
        self.st = st
        self.raw = st.sb("w_raw", [P, 2, kt * P])
        self.hi = st.sb("w_hi", [P, 2, kt * P], F32R)
        self.lo = st.sb("w_lo", [P, 2, kt * P], F32R)
        if psum:
            self.banks()
        self.s_loaded = [st.sem(f"w_loaded{b}") for b in range(2)]
        self.s_first, self.s_hi, self.s_split, self.s_mult, self.s_emptied = (
            st.sem(n) for n in ("w_first_hi", "w_hi", "w_split", "w_mult", "w_emptied"))

    def banks(self):
        self.acc = [self.st.ps(f"acc{b}", [P, T]) for b in range(2)]

    def load(self, sp, i, base, b, src, kt=KT):
        sp.wait_ge(self.s_split, 2 * i + (base + b + 1))
        sp.dma_start(self.raw[:, b, 0:kt * P], src).then_inc(self.s_loaded[b], 16)

    def split(self, pool, i, base, b, kt=KT):
        raw, hi, lo = (x[:, b, 0:kt * P] for x in (self.raw, self.hi, self.lo))
        pool.wait_ge(self.s_loaded[b], 16 * i + 16 * (base // 2 + 1))
        pool.wait_ge(self.s_mult, 2 * i + (base + b + 1))
        pool.nop(nofuse=True)
        pool.tensor_copy(hi, raw).then_inc(self.s_hi, 1)
        pool.wait_ge(self.s_hi, 2 * i + (base + b + 1))
        pool.tensor_tensor(lo, raw, hi.bitcast(F32), ALU.subtract).then_inc(self.s_split, 1)

    def first(self, sp=None, by=None, srcs=()):
        for b in range(2):
            if sp:
                sp.dma_start(self.raw[:, b, :], srcs[b]).then_inc(self.s_loaded[b], 16)
            if by:
                if b == 0:
                    by.sem_inc(self.s_split, 2)
                by.wait_ge(self.s_loaded[b], 16)
                by.nop(nofuse=True)
                by.tensor_copy(self.hi[:, b, :], self.raw[:, b, :]).then_inc(self.s_first, 1)
                by.wait_ge(self.s_first, b + 1)
                by.tensor_tensor(self.lo[:, b, :], self.raw[:, b, :], self.hi[:, b, :].bitcast(F32), ALU.subtract).then_inc(self.s_split, 1)

    def after_first(self, pool):
        pool.wait_ge(self.s_split, 4)
        pool.sem_inc(self.s_hi, 2)

    def mult(self, pe, i, base, b, xh, xl, kt=KT):
        pe.wait_ge(self.s_split, 2 * i + (base + b + 3))
        pe.wait_ge(self.s_emptied, 2 * i + (base + b + 1))
        for h in range(0, T, HALF):
            for k in range(kt):
                for t, (w, x) in enumerate(((self.hi, xh), (self.hi, xl), (self.lo, xh))):
                    m = pe.matmul(self.acc[b][:, h:h + HALF], w[:, b, k * P:(k + 1) * P], x[:, k, h:h + HALF],
                                  start=(k == 0 and t == 0), stop=(k == kt - 1 and t == 2))
        m.then_inc(self.s_mult, 1)

    def ready(self, eng, i, base, b):
        eng.wait_ge(self.s_mult, 2 * i + (base + b + 3))

    def empty(self, ins):
        return ins.then_inc(self.s_emptied, 1)

    def emptied(self, eng, i, base, b):
        eng.wait_ge(self.s_emptied, 2 * i + (base + b + 3))


def tile_of(x, i, b=0, step=2):
    return x[:, bass.ds(step * i + b, 1), :].rearrange("p a t -> p (a t)")


class Kernel:
    def __init__(self, nc, ins, out, counts, marks):
        self.nc, self.ins, self.out, self.counts, self.marks = nc, ins, out, counts, marks

    def clear_sems(self, e):
        for s in self.done_sems:
            e.sem_clear(s)

    def stage(self, name):
        return Stage(self.nc, name, self.counts, self.marks)

    def build(self, upto=None):
        nc = self.nc
        with ExitStack() as ctx:
            sb = lambda n, s, d=F32: ctx.enter_context(nc.sbuf_tensor(n, s, d))
            self.cols = sb("cols", [P, NCOLS])
            self.consts = sb("consts", [P, NCONST])
            self.mod = sb("mod", [P, 48])
            self.xh = sb("xh", [P, KT, T], F32R)
            self.xl = sb("xl", [P, KT, T], F32R)
            self.xt_dram = nc.dram_tensor("xt_scratch", (P, KT, T), F32).ap()
            self.h_dram = nc.dram_tensor("h_scratch", (T, D), F32).ap()
            self.y_dram = nc.dram_tensor("y_scratch", ((NBLK + 1) * P, D), F32).ap()
            self.tok_dram = nc.dram_tensor("token_of_slot", ((NBLK + 2) * P, 1), F32).ap()
            with nc.sbuf_tensor("x_first", [P, KT, T], F32) as self.x:
                self.prepare()
            self.mixer_in()
            self.ssd()
            self.gate_norm()
            self.x = sb("x_res", [P, KT, T])
            self.acc_sq = sb("acc_sq", [P, T])
            self.dense_out("mixout", self.ins["w_out"], reload=True, gate=slice(16, 24))
            self.route()
            self.experts()
            self.combine()
            self.attention_in()
            self.attention()
            self.dense_out("attout", self.ins["swa_w_out"])
            self.feed_forward()
            self.finish()

    def col(self, name, k=0, n=1):
        a = COLS[name].start + k
        return self.cols[:, a:a + n]

    def const(self, name, rows=P):
        return self.consts[0:rows, CONSTS[name]]

    def rstd(self, st, sq_sum, total, rstd, name="rstd", after=None):
        def pe(e):
            after(e)
            for h in range(0, T, HALF):
                m = e.matmul(total[:, h:h + HALF], self.const("ones"), sq_sum[:, h:h + HALF], start=True, stop=True)
            st.pe(m, name + "_sum")

        def dve(e):
            st.wait(e, st.pe, name + "_sum")
            st.dve(e.tensor_scalar(rstd[:, :], total[:, :], 1.0 / D, EPS, ALU.mult, ALU.add))
            st.dve.settle()
            st.dve(e.reciprocal(rstd[:, :], rstd[:, :]), name + "_inv")

        def act(e):
            st.wait(e, st.dve, name + "_inv")
            st.act(e.activation(rstd[:, :], rstd[:, :], ACT.Sqrt), name)
        return pe, dve, act

    def scale_split(self, st, rstd, scale, shift, tmp, rstd_name):
        lanes = {0: st.dve, 1: st.dve if shift is not None else st.pool}

        def lo(e, k):
            st.wait(e, st.act, f"hi{k}")
            hi, out, t = self.xh[:, k, :].bitcast(F32), self.xl[:, k, :], tmp[:, k % 4, :]
            if shift is None:
                ins = e.tensor_tensor(out, t, hi, ALU.subtract)
            else:
                ins = e.scalar_tensor_tensor(out, t, shift[:, k:k + 1], hi, ALU.add, ALU.subtract)
            lanes[k % 2](ins, f"lo{k}")

        def dve(e):
            for k in range(KT + 1):
                if k < KT:
                    if k >= 4:
                        st.wait(e, lanes[k % 2], f"lo{k - 4}")
                    elif k == 0:
                        st.wait(e, st.act, rstd_name)
                    st.dve(e.scalar_tensor_tensor(tmp[:, k % 4, :], self.x[:, k, :], scale[:, k:k + 1], rstd[:, :],
                                                  ALU.mult, ALU.mult), f"scaled{k}")
                if k >= 1 and lanes[(k - 1) % 2] is st.dve:
                    lo(e, k - 1)

        def act(e):
            if shift is not None:
                st.wait(e, st.dve, "mod")
            for k in range(KT):
                st.wait(e, st.dve, f"scaled{k}")
                if shift is None:
                    st.act(e.activation(self.xh[:, k, :], tmp[:, k % 4, :], ACT.Copy), f"hi{k}")
                else:
                    st.act(e.activation(self.xh[:, k, :], tmp[:, k % 4, :], ACT.Identity, bias=shift[:, k:k + 1]), f"hi{k}")

        def pool(e):
            for k in range(1, KT, 2) if shift is None else ():
                lo(e, k)
        return dve, act, pool

    def sum_squares(self, st, sq, acc, ready, each=lambda e, k: None):
        def act(e):
            ready(e)
            for k in range(KT):
                if k >= 2:
                    st.wait(e, st.dve, f"sq_added{k - 2}")
                each(e, k)
                st.act(e.activation(sq[:, k % 2, :], self.x[:, k, :], ACT.Square), f"sq{k}")

        def dve(e, ks=range(KT)):
            for k in ks:
                st.wait(e, st.act, f"sq{k}")
                if k == 0:
                    st.dve(e.tensor_copy(acc[:, :], sq[:, 0, :]), "sq_added0")
                else:
                    st.dve.settle()
                    st.dve(e.tensor_tensor(acc[:, :], acc[:, :], sq[:, k % 2, :], ALU.add), f"sq_added{k}")
        return act, dve

    def modulation(self, st, wa, silu_c, s_wa, first, trips, per=3):
        s_ada = st.sem("ada")

        def load(e, i):
            for k in range(per):
                e.wait_ge(s_ada, per * i + (k + 1))
                e.dma_start(wa[:, k, :], self.ins["w_ada"][per * i + (first + k)]).then_inc(s_wa[k], 16)

        def dve(e, i):
            for k in range(per):
                e.wait_ge(s_wa[k], 16 * i + 16)
                e.scalar_tensor_tensor(wa[:, k, :], wa[:, k, :], 1.0, silu_c[:, :], ALU.mult, ALU.mult,
                                       accum_out=self.mod[:, bass.ds(per * i + (first + k), 1)]).then_inc(s_ada, 1)

        def finish(e):
            e.wait_ge(s_ada, per + per * trips)
            ts = slice(first, first + per * trips)
            b = self.cols[:, COLS["b_ada"].start + first:COLS["b_ada"].start + first + per * trips]
            st.dve(e.tensor_tensor(self.mod[:, ts], self.mod[:, ts], b, ALU.add))
            st.dve.settle()
            one = slice(8, 16) if first == 0 else slice(32, 40)
            st.dve(e.tensor_scalar(self.mod[:, one], self.mod[:, one], 1.0, None, ALU.add), "mod")
        return load, dve, finish, s_ada

    def prepare(self):
        ins = self.ins
        with self.stage("prep") as st:
            xtok = st.sb("xtok", [P, 4, D])
            wa, silu_c = st.sb("wa", [P, 6, D]), st.sb("silu_c", [P, D])
            sq, acc, rstd, tmp = st.sb("sq", [P, 2, D]), st.sb("acc", [P, T]), st.sb("rstd", [P, T]), st.sb("tmp", [P, 4, T])
            turned = [st.ps(f"turned{b}", [P, D]) for b in range(2)]
            total = st.ps("total", [P, T])
            s_cols, s_c, s_out = st.sem("cols"), st.sem("c"), st.sem("xt_out")
            s_x, s_wa = [st.sem(f"x{b}") for b in range(4)], [st.sem(f"wa{b}") for b in range(6)]
            rstd_pe, rstd_dve, rstd_act = self.rstd(st, acc, total, rstd, after=lambda e: st.wait(e, st.dve, "sum3"))
            sc_dve, sc_act, sc_pool = self.scale_split(st, rstd, self.mod[:, 8:16], self.mod[:, 0:8], tmp, "rstd")
            ada_load, ada_dve, ada_finish, s_ada = self.modulation(st, wa, silu_c, s_wa, 0, MOD_FIRST // 2, per=6)
            with st.block() as blk:
                @blk.sync
                def _(e):
                    e.dma_start(self.cols[:, :], ins["cols"]).then_inc(s_cols, 16)
                    e.dma_start(self.consts[:, :], ins["consts"]).then_inc(s_cols, 16)
                    with e.Fori(0, NT // 4) as i:
                        for b in range(4):
                            st.wait(e, st.pe, f"turn{b}", i - 1)
                            e.dma_start(xtok[:, b, :], ins["x"][4 * i + b]).then_inc(s_x[b], 16)
                    e.dma_start(silu_c[:, :], ins["c_rows"]).then_inc(s_c, 16)
                    with e.Fori(0, MOD_FIRST // 2) as i:
                        ada_load(e, i)
                    st.wait(e, st.act, "xt3")
                    e.dma_start(self.xt_dram, self.x[:, :, :]).then_inc(s_out, 16)
                    e.wait_ge(s_out, 16)

                @blk.tensor
                def _(e):
                    st.pe.start(e)
                    e.wait_ge(s_cols, 32)
                    with st.pe.loop(NT // 4) as i:
                        for b in range(4):
                            e.wait_ge(s_x[b], 16 * i + 16)
                            st.wait(e, st.act, f"xt{(b - 2) % 4}", i if b >= 2 else i - 1)
                            for k in range(KT):
                                m = e.transpose(turned[b % 2][:, k * P:(k + 1) * P], xtok[:, b, k * P:(k + 1) * P], self.const("ident"))
                            st.pe(m, f"turn{b}")
                    rstd_pe(e)

                @blk.scalar
                def _(e):
                    st.act.start(e)
                    with st.act.loop(NT // 4) as i:
                        for b in range(4):
                            ts = bass.ds(4 * P * i + P * b, P)
                            st.wait(e, st.pe, f"turn{b}", i)
                            st.act(e.activation(self.x[:, :, ts], turned[b % 2][:, :].rearrange("p (k t) -> p k t", t=P), ACT.Copy), f"xt{b}")
                            st.act.settle()
                            st.wait(e, st.dve, f"sum{(b - 2) % 4}", i if b >= 2 else i - 1)
                            e.nop(nofuse=True)
                            st.act(e.activation(sq[:, b % 2, :].rearrange("p (k t) -> p k t", t=P), self.x[:, :, ts], ACT.Square), f"sq{b}")
                    e.wait_ge(s_c, 16)
                    st.act(e.activation(silu_c[:, :], silu_c[:, :], ACT.Silu), "silu_c")
                    rstd_act(e)
                    sc_act(e)

                @blk.vector
                def _(e):
                    st.dve.start(e)
                    e.sem_inc(s_ada, 6)
                    e.wait_ge(s_cols, 32)
                    with st.dve.loop(NT // 4) as i:
                        for b in range(4):
                            st.wait(e, st.act, f"sq{b}", i)
                            st.dve(e.tensor_reduce(acc[:, bass.ds(4 * P * i + P * b, P)], sq[:, b % 2, :].rearrange("p (k t) -> p t k", k=KT),
                                                   AX.X, ALU.add), f"sum{b}")
                    rstd_dve(e)
                    st.wait(e, st.act, "silu_c")
                    with e.Fori(0, MOD_FIRST // 2) as i:
                        ada_dve(e, i)
                    ada_finish(e)
                    st.dve.settle()
                    sc_dve(e)

                @blk.gpsimd
                def _(e):
                    st.pool.start(e)
                    sc_pool(e)
            self.done_sems = st.sems

    def mixer_in(self):
        ins, nc = self.ins, self.nc
        self.keep = ExitStack()
        sb = lambda n, s: self.keep.enter_context(nc.sbuf_tensor(n, s, F32))
        self.xbc = sb("xbc", [P, CONV_T, T])
        self.zs = sb("zs", [P, SSD_T, T])
        self.acs_row = sb("acs_row", [HEADS, T])
        self.dt_tok = sb("dt_tok", [P, NCH * HEADS])
        self.acs_tok = sb("acs_tok", [P, NCH * HEADS])
        PAD = 16
        with self.stage("in") as st:
            g = Gemm(st)
            raw = st.sb("raw", [P, 2, PAD + T])
            wrk = st.sb("wrk", [P, 2, PAD + T])
            wpool = st.sb("wpool", [P, POOL_T, P])
            dta_tok = st.sb("dta_tok", [P, NCH * HEADS])
            nega = st.sb("nega", [HEADS, 1])
            wa = st.sb("wa", [P, 3, D])
            s_wp, s_c = st.sem("wp"), st.sem("c")
            s_wa = [st.sem(f"wa{b}") for b in range(3)]
            turn = st.ps("turn", [P, 2 * HALF])
            c_rows = wrk[:, 1, 0:D]
            ada_load, ada_dve, ada_finish, s_ada = self.modulation(st, wa, turn, s_wa, 3 * MOD_FIRST, 16 - MOD_FIRST)
            mix = [st.ps(f"mix{b}", [P, HALF]) for b in range(2)]
            W = ins["w_in"]
            cw, cb = COLS["conv_w"].start, COLS["conv_b"].start
            N_SILU, N_Z = CONV_T // 2, SSD_T // 2
            BZ, BD = CONV_T, CONV_T + SSD_T
            TAIL = [(0, BD), (1, BD), (0, BD + 2)]
            with st.block() as blk:
                @blk.sync
                def _(e):
                    g.first(sp=e, srcs=[W[b] for b in range(2)])
                    e.dma_start(c_rows, ins["c_rows"]).then_inc(s_c, 16)
                    self.clear_sems(e)
                    with e.Fori(0, N_SILU + N_Z - 1) as i:
                        for b in range(2):
                            g.load(e, i, 2, b, W[2 * i + (2 + b)])
                        ada_load(e, i)
                    ada_load(e, N_SILU + N_Z - 1)
                    e.dma_start(wpool[:, :, :], ins["w_pool"]).then_inc(s_wp, 16)
                    for j, (b, base) in enumerate(TAIL):
                        g.load(e, 0, base, b, W[BD + j])

                @blk.gpsimd
                def _(e):
                    st.pool.start(e)
                    g.after_first(e)
                    with e.Fori(0, N_SILU + N_Z - 1) as i:
                        for b in range(2):
                            g.split(e, i, 2, b)
                    for b, base in TAIL:
                        g.split(e, 0, base, b)

                @blk.tensor
                def _(e):
                    st.pe.start(e)
                    e.sem_inc(g.s_mult, 2)
                    with e.Fori(0, N_SILU + N_Z) as i:
                        for b in range(2):
                            g.mult(e, i, 0, b, self.xh, self.xl)
                    for b, base in TAIL:
                        g.mult(e, 0, base, b, self.xh, self.xl)
                    ident = self.consts[0:HEADS, 0:HEADS]
                    for src, at in ((0, 0), (1, HALF)):
                        st.wait(e, st.dve, "dt" if src == 0 else "dta")
                        for c in range(NCH):
                            m = e.transpose(turn[:, at + c * HEADS:at + (c + 1) * HEADS],
                                            wrk[0:HEADS, src, c * CH:(c + 1) * CH], ident)
                        st.pe(m, f"dt_turned{src}")
                    st.wait(e, st.dve, "dta_tok")
                    m = e.matmul(mix[0][:, 0:NCH * HEADS], self.const("upto"), dta_tok[:, :], start=True, stop=True)
                    st.pe(m, "acs_tok")
                    for c in range(NCH):
                        m = e.matmul(turn[0:HEADS, c * CH:(c + 1) * CH], dta_tok[:, c * HEADS:(c + 1) * HEADS],
                                     self.const("upto"), start=True, stop=True)
                    st.pe(m, "acs_row")
                    e.wait_ge(s_wp, 16)
                    for j in range(POOL_T):
                        st.wait(e, st.dve, f"pool_diff{j}")
                        for h in range(2):
                            if j == 0 and h == 0:
                                st.wait(e, st.act, "acs_tok")
                            if j:
                                st.wait(e, st.dve, f"pool_lo{j - 1}{h}")
                            m = e.matmul(mix[h][:, :], wpool[:, j, :], raw[:, 1 - j, PAD + h * HALF:PAD + (h + 1) * HALF],
                                         start=True, stop=True)
                            st.pe(m, f"pool{j}{h}")

                @blk.scalar
                def _(e):
                    st.act.start(e)
                    e.preload_act_table(ACT.Silu)
                    e.wait_ge(s_c, 16)
                    st.act(e.activation(turn[:, :], c_rows, ACT.Silu), "silu_c")
                    with st.act.loop(N_SILU) as i:
                        for b in range(2):
                            g.ready(e, i, 0, b)
                            if b == 0:
                                st.wait(e, st.dve, "zeros")
                            st.wait(e, st.dve, f"conv{b}", i - 1)
                            g.empty(e.activation(raw[:, b, PAD:PAD + T], g.acc[b][:, :], ACT.Copy))
                            st.wait(e, st.dve, f"conv{b}", i)
                            st.act(e.activation(tile_of(self.xbc, i, b), wrk[:, b, 0:T], ACT.Silu), f"xbc{b}")
                    with st.act.loop(N_Z) as i:
                        for b in range(2):
                            g.ready(e, i, BZ, b)
                            g.empty(e.activation(tile_of(self.zs, i, b), g.acc[b][:, :], ACT.Silu))
                    g.ready(e, 0, BD, 0)
                    bias = self.cols[0:HEADS, COLS["dt_bias"]]
                    e1, v = raw[0:HEADS, 1, PAD:PAD + T], wrk[0:HEADS, 1, 0:T]
                    st.act(e.activation(nega[:, :], self.cols[0:HEADS, COLS["a_log"]], ACT.Exp), "exp_a")
                    st.act.settle()
                    g.empty(e.activation(v, g.acc[0][0:HEADS, :], ACT.Identity, bias=bias))
                    g.emptied(e, 0, BD, 0)
                    st.act(e.activation(e1, v, ACT.Abs))
                    st.act.settle()
                    st.act(e.activation(e1, e1, ACT.Exp, scale=-1.0), "dt_e")
                    st.wait(e, st.dve, "dt_u")
                    st.act(e.activation(raw[0:HEADS, 0, PAD:PAD + T], wrk[0:HEADS, 0, 0:T], ACT.Ln), "dt_ln")
                    for j in range(POOL_T):
                        b, base = TAIL[1 + j]
                        g.ready(e, 0, base, b)
                        if j == 0:
                            st.wait(e, st.dve, "dt")
                        g.empty(e.activation(raw[:, 1 - j, PAD:PAD + T], g.acc[b][:, :], ACT.Copy))
                    st.wait(e, st.pe, "acs_tok")
                    st.act(e.activation(self.acs_tok[:, :], mix[0][:, 0:NCH * HEADS], ACT.Copy), "acs_tok")
                    st.wait(e, st.pe, "acs_row")
                    st.act(e.activation(self.acs_row[:, :], turn[0:HEADS, :], ACT.Copy), "acs_row")
                    g.ready(e, 0, BD + 2, 0)
                    for j in range(POOL_T):
                        for h in range(2):
                            st.wait(e, st.pe, f"pool{j}{h}")
                            st.act(e.activation(self.xh[:, j, h * HALF:(h + 1) * HALF], mix[h][:, :], ACT.Copy,
                                                scale=self.col("pool_scale", j)), f"pool_hi{j}{h}")

                @blk.vector
                def _(e):
                    st.dve.start(e)
                    e.sem_inc(g.s_emptied, 2)
                    e.sem_inc(s_ada, 3)
                    g.first(by=e)
                    st.dve(e.memset(raw[:, :, 0:PAD], 0.0), "zeros")
                    st.wait(e, st.act, "silu_c")
                    with st.dve.loop(N_SILU) as i:
                        ada_dve(e, i)
                        for b in range(2):
                            g.emptied(e, i, 0, b)
                            st.wait(e, st.act, f"xbc{b}", i - 1)
                            at = i * (2 * CONV) + (cw + b * CONV)
                            taps = [self.cols[:, bass.ds(at + j, 1)] for j in range(CONV)]
                            bias = self.cols[:, bass.ds(2 * i + (cb + b), 1)]
                            if b == 0:
                                st.dve.settle()
                            a = wrk[:, b, 0:T]
                            st.dve(e.tensor_scalar(a, raw[:, b, PAD:PAD + T], taps[3], bias, ALU.mult, ALU.add))
                            for j in (2, 1, 0):
                                st.dve.settle()
                                s = PAD - 3 + j
                                st.dve(e.scalar_tensor_tensor(a, raw[:, b, s:s + T], taps[j], a, ALU.mult, ALU.add),
                                       f"conv{b}" if j == 0 else None)
                    with e.Fori(0, N_Z) as i:
                        ada_dve(e, i + N_SILU)
                    ada_finish(e)
                    st.wait(e, st.act, "dt_e")
                    e1, v = raw[0:HEADS, 1, PAD:PAD + T], wrk[0:HEADS, 1, 0:T]
                    u, t, ln = wrk[0:HEADS, 0, 0:T], self.acs_row[:, :], raw[0:HEADS, 0, PAD:PAD + T]
                    st.dve(e.tensor_scalar(u, e1, 1.0, None, ALU.add), "dt_u")
                    st.dve.settle()
                    st.dve(e.scalar_tensor_tensor(t, u, -1.0, e1, ALU.add, ALU.subtract))
                    st.wait(e, st.act, "dt_ln")
                    st.dve(e.reciprocal(u, u))
                    st.dve.settle()
                    st.dve(e.tensor_tensor(t, t, u, ALU.mult))
                    st.dve.settle()
                    st.dve(e.tensor_tensor(ln, ln, t, ALU.subtract))
                    st.dve.settle()
                    st.dve(e.scalar_tensor_tensor(u, v, 0.0, ln, ALU.max, ALU.add), "dt")
                    st.dve(e.tensor_scalar(nega[:, :], nega[:, :], -1.0, None, ALU.mult))
                    st.dve.settle()
                    st.dve(e.tensor_scalar(v, u, nega[:, 0:1], None, ALU.mult), "dta")
                    for src, dst in ((0, self.dt_tok), (1, dta_tok)):
                        st.wait(e, st.pe, f"dt_turned{src}")
                        at = src * HALF
                        st.dve(e.tensor_copy(dst[:, :], turn[:, at:at + NCH * HEADS]), "dta_tok" if src else "dt_tok")
                    W_ = PAD + T
                    for j in range(POOL_T):
                        g.emptied(e, 0, TAIL[1 + j][1], TAIL[1 + j][0])
                        uu, s, r = raw[:, 1 - j, :], wrk[:, 0, :], wrk[:, 1, :]
                        if j == 1:
                            st.dve.settle()
                        st.dve(e.tensor_tensor(s[:, 1:W_], uu[:, 1:W_], uu[:, 0:W_ - 1], ALU.add))
                        st.dve.settle()
                        st.dve(e.tensor_tensor(r[:, 3:W_], s[:, 3:W_], s[:, 1:W_ - 2], ALU.add))
                        if j == 1:
                            st.dve.settle()
                            st.dve(e.tensor_tensor(s[:, 7:W_], r[:, 7:W_], r[:, 3:W_ - 4], ALU.add))
                            st.dve.settle()
                            st.dve(e.tensor_tensor(r[:, 15:W_], s[:, 15:W_], s[:, 7:W_ - 8], ALU.add))
                        st.dve.settle()
                        for half, src in ((0, s), (1, r)):
                            rows = slice(64 * half, 64 * half + 64)
                            first = self.consts[rows, CONSTS["pool_first"].start + 16 * j:CONSTS["pool_first"].start + 16 * j + 16]
                            inv = self.consts[rows, CONSTS["pool_inv"].start + j:CONSTS["pool_inv"].start + j + 1]
                            st.dve(e.tensor_tensor(src[rows, PAD:PAD + 16], src[rows, PAD:PAD + 16], first, ALU.mult))
                            st.dve.settle()
                            st.dve(e.scalar_tensor_tensor(uu[rows, PAD:W_], src[rows, PAD:W_], inv, uu[rows, PAD:W_],
                                                          ALU.mult, ALU.subtract), f"pool_diff{j}" if half else None)
                    for j in range(POOL_T):
                        for h in range(2):
                            st.wait(e, st.act, f"pool_hi{j}{h}")
                            cs = slice(h * HALF, (h + 1) * HALF)
                            st.dve(e.scalar_tensor_tensor(self.xl[:, j, cs], mix[h][:, :], self.col("pool_scale", j),
                                                          self.xh[:, j, cs].bitcast(F32), ALU.mult, ALU.subtract), f"pool_lo{j}{h}")
            self.done_sems = st.sems

    def ssd(self):
        ins, xbc = self.ins, self.xbc
        with self.stage("ssd") as st:
            sel = st.sb("sel", [HEADS, HEADS * P])
            stg_x = st.sb("stg_x", [P, SSD_T, CH])
            stg_b = st.sb("stg_b", [P, 2, GROUPS, CH])
            xdt = st.sb("xdt", [P, HEADS * HD])
            xdte = st.sb("xdte", [P, HEADS * HD])
            btok = st.sb("btok", [P, GROUPS * STATE])
            m = [st.sb(f"m{b}", [P, HEADS * CH])[:, :] for b in range(2)]
            ce = [st.sb(f"ce{b}", [P, HEADS * CH])[:, :] for b in range(2)]
            cbm = st.sb("cbm", [P, GROUPS * CH])
            state = st.sb("state", [P, HEADS * HD])
            dte, cdec = st.sb("dte", [P, 2, HEADS]), st.sb("cdec", [P, 2, HEADS])
            xy = st.ps("xy", [P, 2 * HALF])
            sb_ = st.ps("states", [P, 2 * HALF])
            cb = st.ps("cb", [P, HALF])
            bc = st.ps("bc", [P, 3 * HALF])
            s_sel, s_fill, s_zeros, s_state0 = (st.sem(n) for n in ("sel", "fill", "zeros", "state0"))
            zeros = st.sb("zeros", [P, D])
            heads = lambda a, n: a.rearrange("p (h n) -> p h n", n=n)
            groups = lambda a, n: a.rearrange("p (g r n) -> p g r n", r=HPG, n=n)
            per_head = lambda a, n: a.unsqueeze(2).to_broadcast([P, HEADS, n])
            cols = lambda c: slice(c * CH, (c + 1) * CH) if isinstance(c, int) else bass.ds(c * CH, CH)
            chunk = lambda a, c: a[:, c * HEADS:(c + 1) * HEADS] if isinstance(c, int) else a[:, bass.ds(c * HEADS, HEADS)]
            W_ = HPG * HD
            new_states = sb_[:, :].rearrange("p (b x) -> p b x", x=HALF)[:, :, 0:2 * W_]
            steps = Steps(st, 4, {"pe": ("x_turned", "b_turned", "cb", "bc", "y", "states"),
                                  "act": ("btok", "exp_bc", "dte", "cdec", "exp_seg", "y_out"),
                                  "dve": ("xdt", "min", "dte_arg", "cbm", "ce", "m", "decayed", "state"),
                                  "pool": ("x_staged", "b_staged", "seg", "xdte")})
            done, wait = steps.done, steps.wait

            def chunks(e, body):
                with e.Fori(0, NCH // 2 - 1) as i:
                    for b in range(2):
                        body(2 * i + b, b, 2)
                for c in (NCH - 2, NCH - 1):
                    body(c, c % 2, NCH - 1 - c)
            with st.block() as blk:
                @blk.sync
                def _(e):
                    e.dma_start(sel[:, :], ins["sel"]).then_inc(s_sel, 16)
                    self.clear_sems(e)
                    e.wait_ge(s_zeros, 1)
                    with e.Fori(2 * T // P, NBLK) as i:
                        e.dma_start(self.y_dram[bass.ds(i * P + P, P), :], zeros[:, :]).then_inc(s_fill, 16)
                    e.wait_ge(s_fill, 16 * (NBLK - 2 * T // P))

                @blk.gpsimd
                def _(e):
                    steps.start(e, "pool")

                    def stage_x(c):
                        wait(e, "x_turned", c - 1)
                        e.nop(nofuse=True)
                        done(e.tensor_copy(stg_x[:, :, :], xbc[:, 0:SSD_T, cols(c)]), "x_staged")

                    def stage_b(c, b):
                        wait(e, "b_turned", c - 2)
                        wait(e, "cb", c - 2)
                        e.nop(nofuse=True)
                        done(e.tensor_copy(stg_b[:, b], xbc[:, SSD_T:SSD_T + GROUPS, cols(c)]), "b_staged")

                    def seg(c, b):
                        wait(e, "min", c)
                        e.nop(nofuse=True)
                        done(e.tensor_tensor(heads(m[b], CH), heads(m[b], CH), per_head(chunk(self.acs_tok, c), CH), ALU.subtract), "seg")

                    def body(c, b, more):
                        wait(e, "dte", c)
                        wait(e, "xdt", c)
                        e.nop(nofuse=True)
                        done(e.tensor_tensor(heads(xdte[:, :], HD), heads(xdt[:, :], HD), per_head(dte[:, b, :], HD), ALU.mult), "xdte")
                        if more:
                            stage_x(c + 1)
                            seg(c + 1, 1 - b)
                        if more > 1:
                            stage_b(c + 2, b)
                    stage_x(0)
                    stage_b(0, 0)
                    seg(0, 0)
                    stage_b(1, 1)
                    chunks(e, body)

                @blk.tensor
                def _(e):
                    steps.start(e, "pe")

                    def turn_x(c):
                        wait(e, "x_staged", c)
                        wait(e, "y_out", c - 1)
                        for j in range(SSD_T):
                            k = e.transpose(xy[:, j * P:(j + 1) * P], stg_x[:, j, :], self.const("ident"))
                        done(k, "x_turned")

                    def turn_b(c, b):
                        wait(e, "b_staged", c)
                        wait(e, "state", c - 1)
                        for g in range(GROUPS):
                            k = e.transpose(sb_[:, g * P:(g + 1) * P], stg_b[:, b, g, :], self.const("ident"))
                        done(k, "b_turned")

                    def decays(c, b):
                        wait(e, "dte_arg", c - 1)
                        wait(e, "exp_bc", c - 1)
                        for h in range(HEADS):
                            k = e.matmul(bc[:, h * CH:(h + 1) * CH], sel[:, h * P:(h + 1) * P],
                                         self.acs_row[:, cols(c)], start=True, stop=True)
                        done(k, "bc")
                        wait(e, "b_staged", c)
                        wait(e, "cbm", c - 1)
                        for g in range(GROUPS):
                            k = e.matmul(cb[:, g * CH:(g + 1) * CH], stg_b[:, b, g, :], xbc[:, 10 + g, cols(c)], start=True, stop=True)
                        done(k, "cb")

                    def body(c, b, more):
                        if more:
                            decays(c + 1, 1 - b)
                        wait(e, "xdt", c)
                        wait(e, "ce", c)
                        wait(e, "m", c)
                        wait(e, "state", c - 1)
                        for h in range(HEADS):
                            o = xy[64 * (h % 2):64 * (h % 2) + 64, (h // 2) * CH:(h // 2 + 1) * CH]
                            e.matmul(o, xdt[:, h * HD:(h + 1) * HD], m[b][:, h * CH:(h + 1) * CH], start=True, stop=False)
                            k = e.matmul(o, state[:, h * HD:(h + 1) * HD], ce[b][:, h * CH:(h + 1) * CH], start=False, stop=True)
                        done(k, "y")
                        wait(e, "xdte", c)
                        wait(e, "btok", c)
                        for g in range(GROUPS):
                            at = (g // 2) * HALF + (g % 2) * W_
                            k = e.matmul(sb_[:, at:at + W_], btok[:, g * P:(g + 1) * P], xdte[:, g * W_:(g + 1) * W_], start=True, stop=True)
                        done(k, "states")
                        if more:
                            turn_x(c + 1)
                            turn_b(c + 1, 1 - b)
                    e.wait_ge(s_sel, 16)
                    turn_x(0)
                    turn_b(0, 0)
                    decays(0, 0)
                    e.wait_ge(s_state0, 1)
                    chunks(e, body)

                @blk.scalar
                def _(e):
                    steps.start(e, "act")
                    e.preload_act_table(ACT.Exp)

                    def exps(c, b):
                        wait(e, "dte_arg", c)
                        done(e.activation(ce[b], bc[:, :], ACT.Exp), "exp_bc")
                        done(e.activation(dte[:, b, :], dte[:, b, :], ACT.Exp), "dte")
                        wait(e, "exp_bc", c)
                        done(e.activation(cdec[:, b, :], heads(ce[b], CH)[:, :, CH - 1], ACT.Copy), "cdec")
                        wait(e, "seg", c)
                        done(e.activation(m[b], m[b], ACT.Exp), "exp_seg")

                    def b_out(c):
                        wait(e, "b_turned", c)
                        done(e.activation(btok[:, :], sb_[:, 0:HALF], ACT.Copy), "btok")

                    def body(c, b, more):
                        if more:
                            exps(c + 1, 1 - b)
                        wait(e, "y", c)
                        done(e.activation(xbc[:, SSD_T:2 * SSD_T, cols(c)],
                                          xy[:, 0:SSD_T * P].rearrange("p (j t) -> p j t", t=CH), ACT.Copy), "y_out")
                        if more:
                            b_out(c + 1)
                    b_out(0)
                    exps(0, 0)
                    chunks(e, body)

                @blk.vector
                def _(e):
                    steps.start(e, "dve")
                    mask = self.const("upto").unsqueeze(1).to_broadcast([P, GROUPS, CH])

                    def arguments(c, b):
                        wait(e, "bc", c)
                        wait(e, "y", c - 2)
                        done(e.tensor_tensor(heads(m[b], CH), heads(bc[:, :], CH), per_head(chunk(self.acs_tok, c), CH), ALU.min), "min")
                        done(e.tensor_tensor(dte[:, b, :], heads(bc[:, :], CH)[:, :, CH - 1], chunk(self.acs_tok, c), ALU.subtract), "dte_arg")
                        wait(e, "cb", c)
                        wait(e, "m", c - 1)
                        done(e.tensor_tensor(heads(cbm[:, :], CH), heads(cb[:, :], CH), mask, ALU.mult), "cbm")
                        wait(e, "cdec", c)
                        for g in range(GROUPS):
                            a = ce[b][:, g * HPG * CH:(g + 1) * HPG * CH].rearrange("p (r n) -> p r n", n=CH)
                            k = e.tensor_tensor(a, a, xbc[:, 10 + g, cols(c)].unsqueeze(1).to_broadcast([P, HPG, CH]), ALU.mult)
                        done(k, "ce")

                    def decay_cb(c, b):
                        wait(e, "exp_seg", c)
                        wait(e, "cbm", c)
                        done(e.tensor_tensor(groups(m[b], CH), groups(m[b], CH),
                                             heads(cbm[:, :], CH).unsqueeze(2).to_broadcast([P, GROUPS, HPG, CH]), ALU.mult), "m")

                    def x_dt(c):
                        wait(e, "x_turned", c)
                        done(e.tensor_tensor(heads(xdt[:, :], HD), xy[:, 0:HEADS * HD].rearrange("p (h n) -> p h n", n=HD),
                                             per_head(chunk(self.dt_tok, c), HD), ALU.mult), "xdt")

                    def body(c, b, more):
                        if more:
                            arguments(c + 1, 1 - b)
                            decay_cb(c + 1, 1 - b)
                        wait(e, "y", c)
                        wait(e, "state", c - 1)
                        done(e.tensor_tensor(heads(state[:, :], HD), heads(state[:, :], HD), per_head(cdec[:, b, :], HD), ALU.mult), "decayed")
                        wait(e, "states", c)
                        wait(e, "decayed", c)
                        s2 = state[:, :].rearrange("p (b x) -> p b x", b=2)
                        done(e.tensor_tensor(s2, s2, new_states, ALU.add), "state")
                        if more:
                            x_dt(c + 1)
                    e.memset(state[:, :], 0.0).then_inc(s_state0, 1)
                    e.memset(zeros[:, :], 0.0).then_inc(s_zeros, 1)
                    e.wait_ge(s_state0, 1)
                    x_dt(0)
                    arguments(0, 0)
                    decay_cb(0, 0)
                    chunks(e, body)
            self.done_sems = st.sems

    def gate_norm(self):
        xbc, zs = self.xbc, self.zs
        with self.stage("gate") as st:
            member = st.sb("member", [P, SSD_T, GROUPS])
            member_t = st.sb("member_t", [GROUPS, SSD_T, P])
            rstd, tmp = st.sb("rstd", [GROUPS, T]), st.sb("tmp", [P, 2, T])
            group_sum = st.ps("group_sum", [GROUPS, T])
            total = [st.ps(f"total{b}", [P, T]) for b in range(2)]
            s_member = st.sem("member")
            with st.block() as blk:
                @blk.sync
                def _(e):
                    self.clear_sems(e)
                    e.dma_start(member[:, :, :], self.ins["member"]).then_inc(s_member, 16)
                    e.dma_start(member_t[:, :, :], self.ins["member_t"]).then_inc(s_member, 16)

                @blk.tensor
                def _(e):
                    st.pe.start(e)
                    e.wait_ge(s_member, 32)
                    for j in range(SSD_T):
                        st.wait(e, st.act, f"sq{j}")
                        for h in range(0, T, HALF):
                            k = e.matmul(group_sum[:, h:h + HALF], member[:, j, :], zs[:, j, h:h + HALF], start=(j == 0), stop=(j == SSD_T - 1))
                    st.pe(k, "group_sum")
                    st.wait(e, st.act, "rstd")
                    for j in range(SSD_T):
                        if j >= 2:
                            st.wait(e, st.dve, f"normed{j - 2}")
                        for h in range(0, T, HALF):
                            k = e.matmul(total[j % 2][:, h:h + HALF], member_t[:, j, :], rstd[:, h:h + HALF], start=True, stop=True)
                        st.pe(k, f"spread{j}")

                @blk.scalar
                def _(e):
                    st.act.start(e)
                    for j in range(SSD_T):
                        st.wait(e, st.dve, f"gated{j}")
                        st.act(e.activation(zs[:, j, :], xbc[:, SSD_T + j, :], ACT.Square), f"sq{j}")
                    st.wait(e, st.dve, "inv")
                    st.act(e.activation(rstd[:, :], rstd[:, :], ACT.Sqrt), "rstd")
                    for j in range(SSD_T):
                        st.wait(e, st.dve, f"normed{j}")
                        st.act(e.activation(self.xh[:, POOL_T + j, :], tmp[:, j % 2, :], ACT.Copy), f"hi{j}")

                @blk.gpsimd
                def _(e):
                    st.pool.start(e)
                    for j in range(SSD_T):
                        st.wait(e, st.act, f"hi{j}")
                        st.pool(e.tensor_tensor(self.xl[:, POOL_T + j, :], tmp[:, j % 2, :],
                                                self.xh[:, POOL_T + j, :].bitcast(F32), ALU.subtract), f"lo{j}")

                @blk.vector
                def _(e):
                    st.dve.start(e)
                    for j in range(SSD_T):
                        y = xbc[:, SSD_T + j, :]
                        st.dve(e.scalar_tensor_tensor(y, xbc[:, j, :], self.col("d_skip", j), y, ALU.mult, ALU.add))
                        st.dve.settle()
                        st.dve(e.tensor_tensor(y, y, zs[:, j, :], ALU.mult), f"gated{j}")
                    st.wait(e, st.pe, "group_sum")
                    st.dve(e.tensor_scalar(rstd[:, :], group_sum[:, :], GROUPS / (SSD_T * P), EPS, ALU.mult, ALU.add))
                    st.dve.settle()
                    st.dve(e.reciprocal(rstd[:, :], rstd[:, :]), "inv")
                    for j in range(SSD_T):
                        st.wait(e, st.pe, f"spread{j}")
                        if j >= 2:
                            st.wait(e, st.pool, f"lo{j - 2}")
                        st.dve(e.scalar_tensor_tensor(tmp[:, j % 2, :], xbc[:, SSD_T + j, :], self.col("ssd_norm_w", j),
                                                      total[j % 2][:, :], ALU.mult, ALU.mult), f"normed{j}")
        self.keep.close()

    def dense_out(self, name, W, reload=False, gate=None):
        x, acc = self.x, self.acc_sq
        with self.stage(name) as st:
            g = Gemm(st)
            sq = st.sb("sq", [P, 2, T])
            s_x = st.sem("x")
            with st.block() as blk:
                @blk.sync
                def _(e):
                    g.first(sp=e, srcs=[W[b] for b in range(2)])
                    with e.Fori(0, KT // 2 - 1) as i:
                        for b in range(2):
                            g.load(e, i, 2, b, W[2 * i + (2 + b)])

                @blk.gpsimd
                def _(e):
                    st.pool.start(e)
                    g.after_first(e)
                    with e.Fori(0, KT // 2 - 1) as i:
                        for b in range(2):
                            g.split(e, i, 2, b)

                @blk.tensor
                def _(e):
                    st.pe.start(e)
                    e.sem_inc(g.s_mult, 2)
                    with e.Fori(0, KT // 2) as i:
                        for b in range(2):
                            g.mult(e, i, 0, b, self.xh, self.xl)

                @blk.scalar
                def _(e):
                    st.act.start(e)
                    if reload:
                        e.dma_start(x[:, :, :], self.xt_dram).then_inc(s_x, 16)
                    with st.act.loop(KT // 2) as i:
                        for b in range(2):
                            g.emptied(e, i, 0, b)
                            st.wait(e, st.dve, f"added{b}", i - 1)
                            st.act(e.activation(sq[:, b, :], tile_of(x, i, b), ACT.Square), f"sq{b}")

                @blk.vector
                def _(e):
                    st.dve.start(e)
                    e.sem_inc(g.s_emptied, 2)
                    g.first(by=e)
                    st.dve(e.memset(acc[:, :], 0.0))
                    if reload:
                        e.wait_ge(s_x, 16)
                    with st.dve.loop(KT // 2) as i:
                        for b in range(2):
                            g.ready(e, i, 0, b)
                            xn = tile_of(x, i, b)
                            if gate is None:
                                g.empty(e.tensor_tensor(xn, g.acc[b][:, :], xn, ALU.add))
                            else:
                                s = self.mod[:, bass.ds(2 * i + (gate.start + b), 1)]
                                g.empty(e.scalar_tensor_tensor(xn, g.acc[b][:, :], s, xn, ALU.mult, ALU.add))
                            st.wait(e, st.act, f"sq{b}", i)
                            st.dve.settle()
                            st.dve(e.tensor_tensor(acc[:, :], acc[:, :], sq[:, b, :], ALU.add), f"added{b}")

    def route(self):
        ins, nc, x = self.ins, self.nc, self.x
        self.rkeep = ExitStack()
        sb = lambda n, s, d=F32: self.rkeep.enter_context(nc.sbuf_tensor(n, s, d))
        self.slots = sb("slots", [P, 2 * NT], I32)
        self.gates = sb("gates", [P, 2 * NT])
        self.blocks = sb("blocks", [P, NBLK + 2], I32)
        self.fresh = sb("fresh", [P, NBLK + 1], I32)
        self.order = sb("order", [P, NBLK + 1], I32)
        self.rows = sb("rows", [P, NBLK + 2], I32)
        R = EG + NE
        with self.stage("route") as st:
            rstd, hst = st.sb("rstd", [P, T]), st.sb("hst", [P, 2, KT * P])
            htok = st.sb("htok", [P, 2, D])
            wr = st.sb("wr", [P, KT, R])
            lg = st.sb("lg", [P, NT, R])
            zeros = st.sb("zeros", [P, NBLK + 2])
            total = st.ps("total", [P, T])
            turned = [st.ps(f"turned{b}", [P, D]) for b in range(2)]
            pl = st.ps("logits", [P, HALF])
            s_wr, s_zero, s_scatter, s_rows = (st.sem(n) for n in ("wr", "zero", "scatter", "rows"))
            s_h = [st.sem(f"h{b}") for b in range(2)]
            rstd_pe, rstd_dve, rstd_act = self.rstd(st, self.acc_sq, total, rstd, after=lambda e: None)
            t3 = lambda a, k=KT: a.rearrange("p (k t) -> p k t", k=k)
            table = st.sb("table", [NBLK + 2, P])
            W = {}
            def buf(name, *shape):
                n = int(np.prod(shape))
                if name not in W:
                    W[name] = st.sb(name, [P, n])
                a = W[name][:, 0:n]
                if len(shape) == 2:
                    return a.rearrange("p (a b) -> p a b", b=shape[1])
                if len(shape) == 3:
                    return a.rearrange("p (a b c) -> p a b c", b=shape[1], c=shape[2])
                return a
            both_ = lambda st: buf("both", NT * NE)
            g_exp = lambda st: buf("g_exp", NT, EG)
            e_exp = lambda st: buf("e_exp", NT)
            for n, w in (("both", NT * NE), ("g_exp", NT * EG), ("e_exp", NT)):
                buf(n, w)
            with st.block() as blk:
                @blk.sync
                def _(e):
                    for b in range(2):
                        e.sem_inc(s_h[b], 16)
                    e.dma_start(wr[:, :, :], ins["w_route"]).then_inc(s_wr, 16)
                    st.wait(e, st.dve, "zeros")
                    e.dma_start(self.tok_dram.rearrange("(p n) a -> p (n a)", p=P), zeros[:, :]).then_inc(s_zero, 16)
                    with e.Fori(0, NT // 2) as i:
                        for b in range(2):
                            st.wait(e, st.act, f"htok{b}", i)
                            e.dma_start(self.h_dram[bass.ds(2 * P * i + P * b, P), :], htok[:, b, :]).then_inc(s_h[b], 16)
                    for b in range(2):
                        e.wait_ge(s_h[b], 16 * (NT // 2) + 16)
                    e.wait_ge(s_scatter, 16 * 2 * NT)
                    e.dma_start(table[:, :], self.tok_dram.rearrange("(n p) a -> n (p a)", p=P)).then_inc(s_rows, 16)

                @blk.tensor
                def _(e):
                    st.pe.start(e)
                    rstd_pe(e)
                    e.wait_ge(s_wr, 16)
                    with st.pe.loop(NT // 2) as i:
                        for b in range(2):
                            st.wait(e, st.pool, f"h{b}", i)
                            st.wait(e, st.act, f"htok{b}", i - 1)
                            for k in range(KT):
                                e.transpose(turned[b][:, k * P:(k + 1) * P], hst[:, b, k * P:(k + 1) * P], self.const("ident"))
                            for k in range(KT):
                                m = e.matmul(pl[:, bass.ds(2 * R * i + R * b, R)], hst[:, b, k * P:(k + 1) * P], wr[:, k, :], start=(k == 0), stop=(k == KT - 1))
                            st.pe(m, f"used{b}")
                    st.wait(e, st.dve, "chosen")
                    e.matmul(total[:, 0:NT * NE], self.const("before"), both_(st), start=True, stop=True)
                    m = e.matmul(total[:, HALF:HALF + NT * NE], self.const("ones"), both_(st), start=True, stop=True)
                    st.pe(m, "ranked")
                    e.wait_ge(s_rows, 16)
                    m = e.transpose(pl[:, 0:NBLK + 2], table[:, :], self.consts[0:NBLK + 2, 0:NBLK + 2])
                    st.pe(m, "rows")

                @blk.scalar
                def _(e):
                    st.act.start(e)
                    rstd_act(e)
                    with st.act.loop(NT // 2) as i:
                        for b in range(2):
                            st.wait(e, st.pe, f"used{b}", i)
                            e.wait_ge(s_h[b], 16 * i + 16)
                            st.act(e.activation(htok[:, b, :], turned[b][:, :], ACT.Copy), f"htok{b}")
                    st.wait(e, st.dve, "g_arg")
                    st.act(e.activation(g_exp(st), g_exp(st), ACT.Exp), "g_exp")
                    st.wait(e, st.dve, "e_arg")
                    st.act(e.activation(e_exp(st), e_exp(st), ACT.Exp), "e_exp")

                @blk.gpsimd
                def _(e):
                    st.pool.start(e)
                    shift = self.mod[:, 24:32].unsqueeze(2).to_broadcast([P, KT, P])
                    with st.pool.loop(NT // 2) as i:
                        for b in range(2):
                            st.wait(e, st.dve, f"scaled{b}", i)
                            st.pool(e.tensor_tensor(t3(hst[:, b, :]), t3(hst[:, b, :]), shift, ALU.add), f"h{b}")
                    st.wait(e, st.dve, "slots")
                    e.wait_ge(s_zero, 16)
                    e.nop(nofuse=True)
                    tokid = self.const("tokid")
                    for n in range(2 * NT):
                        e.indirect_dma_start(out=self.tok_dram, out_offset=bass.IndirectOffsetOnAxis(ap=self.slots[:, n:n + 1], axis=0),
                                             in_=tokid[:, n % NT:n % NT + 1], in_offset=None).then_inc(s_scatter, 16)

                @blk.vector
                def _(e):
                    dve = st.dve
                    dve.start(e)
                    dve(e.memset(zeros[:, :], 0.0), "zeros")
                    rstd_dve(e)
                    st.wait(e, st.act, "rstd")
                    scale = self.mod[:, 32:40].unsqueeze(2).to_broadcast([P, KT, P])
                    with dve.loop(NT // 2) as i:
                        for b in range(2):
                            ts = bass.ds(2 * P * i + P * b, P)
                            st.wait(e, st.pe, f"used{b}", i - 1)
                            dve(e.tensor_tensor(t3(hst[:, b, :]), x[:, :, ts], rstd[:, ts].unsqueeze(1).to_broadcast([P, KT, P]), ALU.mult))
                            dve.settle()
                            dve(e.tensor_tensor(t3(hst[:, b, :]), t3(hst[:, b, :]), scale, ALU.mult), f"scaled{b}")
                    st.wait(e, st.pe, "used1")
                    dve(e.tensor_tensor(lg[:, :, :], pl[:, 0:NT * R].rearrange("p (t r) -> p t r", r=R),
                                        self.cols[:, COLS["router_b"]].unsqueeze(1).to_broadcast([P, NT, R]), ALU.add))

                    def do(ins, name=None):
                        dve(ins, name)
                        dve.settle()

                    def over(a, *shape):
                        return a.to_broadcast([P, *shape])
                    iota8 = self.const("iota8")

                    def first_largest(v, n, onehot, most):
                        eq, low = buf(f"eq{n}", NT, n), buf("low", NT)
                        do(e.tensor_reduce(most, v, AX.X, ALU.max))
                        do(e.tensor_tensor(eq, v, over(most.unsqueeze(2), NT, n), ALU.is_equal))
                        do(e.scalar_tensor_tensor(eq, eq, -64.0, over(iota8[:, 0:n].unsqueeze(1), NT, n), ALU.mult, ALU.add))
                        do(e.tensor_reduce(low, eq, AX.X, ALU.min))
                        do(e.tensor_tensor(onehot, eq, over(low.unsqueeze(2), NT, n), ALU.is_equal))

                    dve.settle()
                    g_one, g_most = buf("g_one", NT, EG), buf("g_most", NT)
                    first_largest(lg[:, :, 0:EG], EG, g_one, g_most)
                    do(e.tensor_tensor(g_exp(st), lg[:, :, 0:EG], over(g_most.unsqueeze(2), NT, EG), ALU.subtract), "g_arg")
                    el = lg[:, :, EG:].rearrange("p t (g x) -> p t g x", g=EG)
                    prod, within = buf("prod", NT, EG, EPG), buf("within", NT, EPG)
                    g_wide = over(g_one.unsqueeze(3), NT, EG, EPG)
                    do(e.tensor_tensor(prod, el, g_wide, ALU.mult))
                    do(e.tensor_reduce(within, prod.rearrange("p t g x -> p t x g"), AX.X, ALU.add))
                    one, most = [buf(f"one{k}", NT, EPG) for k in range(2)], [buf(f"most{k}", NT) for k in range(2)]
                    first_largest(within, EPG, one[0], most[0])
                    do(e.scalar_tensor_tensor(within, one[0], -BIG, within, ALU.mult, ALU.add))
                    first_largest(within, EPG, one[1], most[1])
                    do(e.tensor_tensor(e_exp(st), most[1], most[0], ALU.subtract), "e_arg")
                    hot = [buf(f"hot{k}", NT, EG, EPG) for k in range(2)]
                    for k in range(2):
                        do(e.tensor_tensor(hot[k], over(one[k].unsqueeze(2), NT, EG, EPG), g_wide, ALU.mult))
                    flat = [buf(f"hot{k}", NT * NE) for k in range(2)]
                    do(e.tensor_tensor(buf("both", NT * NE), flat[0], flat[1], ALU.add), "chosen")
                    psum_, pg, den = buf("g_sum", NT), buf("pg", NT), buf("den", NT)
                    st.wait(e, st.act, "g_exp")
                    do(e.tensor_reduce(psum_, g_exp(st), AX.X, ALU.add))
                    st.wait(e, st.act, "e_exp")
                    do(e.tensor_scalar(den, e_exp(st), 1.0, None, ALU.add))
                    do(e.tensor_tensor(den, den, psum_, ALU.mult))
                    do(e.reciprocal(self.gates[:, 0:NT], den))
                    do(e.tensor_tensor(self.gates[:, NT:], self.gates[:, 0:NT], e_exp(st), ALU.mult))
                    st.wait(e, st.pe, "ranked")
                    rank, tot = buf("rank", NT, NE), buf("tot", NT, NE)
                    upto, cnt = buf("before_tile", NT, NE), buf("cnt", NE)
                    do(e.tensor_copy(tot, total[:, HALF:HALF + NT * NE].rearrange("p (t x) -> p t x", x=NE)))
                    do(e.memset(upto[:, 0, :], 0.0))
                    for t in range(1, NT):
                        do(e.tensor_tensor(upto[:, t, :], upto[:, t - 1, :], tot[:, t - 1, :], ALU.add))
                    do(e.tensor_tensor(cnt, upto[:, NT - 1, :], tot[:, NT - 1, :], ALU.add))
                    do(e.tensor_tensor(rank, total[:, 0:NT * NE].rearrange("p (t x) -> p t x", x=NE), upto, ALU.add))
                    more, nb = buf("more", NE, NT), buf("nb", NE)
                    do(e.tensor_tensor(more, over(cnt.unsqueeze(2), NE, NT), over(self.const("iota8x128").unsqueeze(1), NE, NT), ALU.is_gt))
                    do(e.tensor_reduce(nb, more, AX.X, ALU.add))
                    run = [buf("run0", NE), buf("run1", NE)]
                    do(e.tensor_copy(run[0], nb))
                    for n, w in enumerate((1, 2, 4, 8, 16)):
                        a, o = run[n % 2], run[1 - n % 2]
                        do(e.tensor_copy(o[:, 0:w], a[:, 0:w]))
                        do(e.tensor_tensor(o[:, w:], a[:, w:], a[:, 0:NE - w], ALU.add))
                    end, start = run[1], buf("start", NE)
                    do(e.tensor_tensor(start, end, nb, ALU.subtract))
                    do(e.tensor_scalar(start, start, float(P), float(P), ALU.mult, ALU.add))
                    do(e.tensor_tensor(rank, rank, over(start.unsqueeze(1), NT, NE), ALU.add))
                    slot = buf("slot", 2, NT)
                    for k in range(2):
                        do(e.tensor_tensor(flat[k], flat[k], buf("rank", NT * NE), ALU.mult))
                        do(e.tensor_reduce(slot[:, k, :], buf(f"hot{k}", NT, NE), AX.X, ALU.add))
                    do(e.tensor_copy(self.slots[:, :], buf("slot", 2 * NT)), "slots")
                    ended, expert = buf("ended", NBLK + 1, NE), buf("expert", NBLK + 1)
                    do(e.tensor_tensor(ended, over(end.unsqueeze(1), NBLK + 1, NE), over(self.const("iotab").unsqueeze(2), NBLK + 1, NE), ALU.is_le))
                    do(e.tensor_reduce(expert, ended, AX.X, ALU.add))
                    do(e.tensor_scalar(expert, expert, float(NE - 1), None, ALU.min))
                    do(e.tensor_copy(self.blocks[:, 0:NBLK + 1], expert))
                    N1 = NBLK + 1
                    run = [buf("changes0", N1), buf("changes1", N1)]
                    do(e.memset(run[0][:, 0:1], 1.0))
                    do(e.tensor_tensor(run[0][:, 1:], expert[:, 1:], expert[:, 0:NBLK], ALU.not_equal))
                    do(e.tensor_copy(self.fresh[:, :], run[0]))
                    for n, w in enumerate((1, 2, 4, 8, 16, 32)):
                        a, o = run[n % 2], run[1 - n % 2]
                        do(e.tensor_copy(o[:, 0:w], a[:, 0:w]))
                        do(e.tensor_tensor(o[:, w:], a[:, w:], a[:, 0:N1 - w], ALU.add))
                    do(e.tensor_scalar(run[0], run[0], -1.0, None, ALU.add))
                    do(e.tensor_copy(self.order[:, :], run[0]))
                    do(e.tensor_copy(self.blocks[:, NBLK + 1:], end[:, NE - 1:NE]))
                    st.wait(e, st.pe, "rows")
                    do(e.tensor_copy(self.rows[:, :], pl[:, 0:NBLK + 2]))

    def experts(self):
        ins = self.ins
        U, RING = KT + FF // P, 6
        EARLY = U - 2
        with self.stage("moe") as st:
            raw = st.sb("raw", [P, 2, U, D])
            hi, lo = self.xh, self.xl
            xt = [a[:, RING, :] for a in (hi, lo)]
            at = [a[:, RING + 1, 0:FF] for a in (hi, lo)]
            xg = st.sb("xg", [P, D])
            idx = st.sb("idx", [P, 1], I32)
            act_ = st.sb("act", [P, FF])
            ysb = self.acc_sq
            hu, yp, xturn = st.ps("hu", [P, 2 * FF]), st.ps("y", [P, D]), st.ps("xturn", [P, D])
            aturn = st.ps("aturn", [P, FF])
            s_w = [st.sem(f"w{u}") for u in range(U)]
            s_g, s_y, s_last = st.sem("gathered"), st.sem("y_out"), st.sem("last_rows")
            order = lambda e, i: e.value_load(self.order[0:1, bass.ds(i, 1)], min_val=0, max_val=NE - 1)
            tile = lambda o, u: raw[:, bass.ds(o % 2, 1), u, :].rearrange("p a d -> p (a d)")
            blocks = lambda e: e.value_load(self.blocks[0:1, NBLK + 1:NBLK + 2], min_val=2 * T // P, max_val=NBLK)
            with st.block() as blk:
                @blk.sync
                def _(e):
                    n = blocks(e)
                    for u in range(U):
                        e.sem_inc(s_w[u], 16)
                    with e.Fori(0, NBLK) as i:
                        fresh = e.value_load(self.fresh[0:1, bass.ds(i, 1)], min_val=0, max_val=1)
                        with e.If(i < n * fresh):
                            ex = e.value_load(self.blocks[0:1, bass.ds(i, 1)], min_val=0, max_val=NE - 1)
                            o = order(e, i)
                            for u in range(U):
                                st.wait(e, st.dve, f"lo{u}", i - 2)
                                e.wait_ge(s_w[u], 16 * o + 16)
                                src = ins["w13"][ex, u * P:(u + 1) * P, :] if u < KT else ins["w2"][ex, (u - KT) * P:(u - KT + 1) * P, :]
                                e.dma_start(tile(o, u), src).then_inc(s_w[u], 16)

                @blk.gpsimd
                def _(e):
                    st.pool.start(e)
                    n = blocks(e)

                    def gather(name, i=None):
                        e.nop(nofuse=True)
                        st.pool(e.tensor_copy(idx[:, :], self.rows[:, 1:2] if i is None else self.rows[:, bass.ds(i + 2, 1)]), name)
                        st.pool.settle()
                        e.nop(nofuse=True)
                        e.indirect_dma_start(out=xg[:, :], out_offset=None, in_=self.h_dram,
                                             in_offset=bass.IndirectOffsetOnAxis(ap=idx[:, 0:1], axis=0)).then_inc(s_g, 16)
                    gather("idx_first")
                    st.wait(e, st.pe, "x_first")
                    with st.pool.loop(NBLK) as i:
                        with e.If(i < n):
                            e.wait_ge(s_g, 16 * i + 16)
                            st.wait(e, st.pe, "x_turned", i - 1)
                            gather("idx", i)

                @blk.tensor
                def _(e):
                    st.pe.start(e)
                    n = blocks(e)

                    def turn_x():
                        for k in range(KT):
                            m = e.transpose(xturn[:, k * P:(k + 1) * P], xg[:, k * P:(k + 1) * P], self.const("ident"))
                        return m

                    def product(i, u, x, k, out):
                        st.wait(e, st.dve, f"lo{u}", i)
                        r = u % RING
                        last = (u == KT - 1) or (u == U - 1)
                        first = u in (0, KT)
                        passes = [(x[0], hi), (x[0], lo), (x[1], hi)]
                        order_ = [(h, t) for h in (0, HALF) for t in range(3)]
                        if u == KT:
                            order_ = [(h, t) for ts in ((0, 1), (2,)) for h in (0, HALF) for t in ts]
                        for n, (h, t) in enumerate(order_):
                            if u == KT and n == 4:
                                st.wait(e, st.dve, "a_lo", i)
                            a, w = passes[t]
                            m = e.matmul(out[:, h:h + HALF], a[:, k * P:(k + 1) * P], w[:, r, h:h + HALF],
                                         start=first and t == 0, stop=last and t == 2)
                            if u == KT - 1 and n == 2:
                                st.pe(m, "gate")
                        st.pe(m, f"mm{u}")
                    for k in range(D // P):
                        m = e.transpose(yp[:, k * P:(k + 1) * P], self.const("ident"), self.const("ident"))
                    st.pe(m, "y_none")
                    e.wait_ge(s_g, 16)
                    st.pe(turn_x(), "x_first")
                    st.wait(e, st.dve, "x_lo_first")
                    with st.pe.loop(NBLK) as i:
                        with e.If(i < n):
                            st.wait(e, st.dve, "x_lo", i - 1)
                            for u in range(KT):
                                product(i, u, xt, u, hu)
                            e.wait_ge(s_g, 16 * i + 32)
                            st.pe(turn_x(), "x_turned")
                            st.wait(e, st.dve, "act", i)
                            for k in range(FF // P):
                                m = e.transpose(aturn[:, k * P:(k + 1) * P], act_[:, k * P:(k + 1) * P], self.const("ident"))
                            st.pe(m, "a_turned")
                            st.wait(e, st.act, "a_hi", i)
                            st.wait(e, st.act, "y0", i)
                            st.wait(e, st.dve, "y1", i)
                            for u in range(KT, U):
                                product(i, u, at, u - KT, yp)

                @blk.scalar
                def _(e):
                    st.act.start(e)
                    n = blocks(e)
                    e.sem_inc(s_y, 16)

                    def high(i, u, o):
                        e.wait_ge(s_w[u], 16 * o + 32)
                        prev, j = (u - RING, i) if u >= RING else (u + RING, i - 1)
                        st.wait(e, st.pe, f"mm{prev}", j)
                        e.nop(nofuse=True)
                        st.act(e.activation(hi[:, u % RING, :], tile(o, u), ACT.Copy), f"hi{u}")

                    def rows_out(i):
                        e.wait_ge(s_y, 16 * i + 16)
                        return e.activation(ysb[:, 0:HALF], yp[:, 0:HALF], ACT.Copy)

                    def send(i):
                        e.dma_start(self.y_dram[bass.ds(i * P, P), :], ysb[:, :]).then_inc(s_y, 16)
                    e.preload_act_table(ACT.Silu)
                    st.wait(e, st.pe, "x_first")
                    st.act(e.activation(xt[0], xturn[:, :], ACT.Copy), "x_hi_first")
                    st.wait(e, st.pe, "y_none")
                    with st.act.loop(NBLK) as i:
                        with e.If(i < n):
                            o = order(e, i)
                            for u in range(EARLY):
                                high(i, u, o)
                                if u == 2:
                                    st.wait(e, st.pe, f"mm{U - 1}", i - 1)
                                    st.act(rows_out(i), "y0")
                                if u == 6:
                                    st.wait(e, st.act, "y0", i)
                                    st.wait(e, st.dve, "y1", i)
                                    send(i)
                            st.wait(e, st.pe, "gate", i)
                            st.act(e.activation(act_[:, :], hu[:, 0:FF], ACT.Silu), "silu")
                            st.wait(e, st.pe, "a_turned", i)
                            st.act(e.activation(at[0], aturn[:, :], ACT.Copy), "a_hi")
                            for u in range(EARLY, U):
                                high(i, u, o)
                            st.wait(e, st.pe, "x_turned", i)
                            st.act(e.activation(xt[0], xturn[:, :], ACT.Copy), "x_hi")
                    st.wait(e, st.pe, f"mm{U - 1}", n - 1)
                    rows_out(n).then_inc(s_last, 1)
                    e.wait_ge(s_last, 2)
                    send(n)
                    e.wait_ge(s_y, 16 * n + 32)
                    e.nop(nofuse=True)

                @blk.vector
                def _(e):
                    st.dve.start(e)
                    n = blocks(e)

                    def low(i, u, o):
                        st.wait(e, st.act, f"hi{u}", i)
                        r = u % RING
                        st.dve(e.tensor_tensor(lo[:, r, :], tile(o, u), hi[:, r, :].bitcast(F32), ALU.subtract), f"lo{u}")
                    st.wait(e, st.act, "x_hi_first")
                    st.dve(e.tensor_tensor(xt[1], xturn[:, :], xt[0].bitcast(F32), ALU.subtract), "x_lo_first")
                    st.wait(e, st.pe, "y_none")
                    with st.dve.loop(NBLK) as i:
                        with e.If(i < n):
                            o = order(e, i)
                            for u in range(EARLY):
                                low(i, u, o)
                                if u == 2:
                                    st.wait(e, st.pe, f"mm{U - 1}", i - 1)
                                    e.wait_ge(s_y, 16 * i + 16)
                                    st.dve(e.tensor_copy(ysb[:, HALF:], yp[:, HALF:]), "y1")
                            st.wait(e, st.act, "silu", i)
                            st.wait(e, st.pe, "mm7", i)
                            st.dve(e.tensor_tensor(act_[:, :], act_[:, :], hu[:, FF:2 * FF], ALU.mult), "act")
                            st.wait(e, st.act, "a_hi", i)
                            st.dve(e.tensor_tensor(at[1], aturn[:, :], at[0].bitcast(F32), ALU.subtract), "a_lo")
                            for u in range(EARLY, U):
                                low(i, u, o)
                            st.wait(e, st.act, "x_hi", i)
                            st.dve(e.tensor_tensor(xt[1], xturn[:, :], xt[0].bitcast(F32), ALU.subtract), "x_lo")
                    st.wait(e, st.pe, f"mm{U - 1}", n - 1)
                    e.wait_ge(s_y, 16 * n + 16)
                    e.tensor_copy(ysb[:, HALF:], yp[:, HALF:]).then_inc(s_last, 1)

    def combine(self):
        x = self.x
        with self.stage("comb") as st:
            ys = [st.sb(f"y{k}", [P, 2, D]) for k in range(2)]
            idx = st.sb("idx", [P, 4], I32)
            sq, tmp = st.sb("sq", [P, 2, KT * P]), st.sb("tmp", [P, KT * P])
            turned = [st.ps(f"turned{b}", [P, D]) for b in range(2)]
            s_g = [st.sem(f"g{b}") for b in range(2)]
            t3 = lambda a: a.rearrange("p (k t) -> p k t", k=KT)
            gate = self.mod[:, 40:48].unsqueeze(2).to_broadcast([P, KT, P])
            steps = Steps(st, 2, {"pe": ("turned",), "act": ("sq",), "pool": ("idx",),
                                  "dve": ("scaled", "mixed", "gated", "x", "sum")})
            done, wait = steps.done, steps.wait
            tokens = lambda n: slice(n * P, (n + 1) * P) if isinstance(n, int) else bass.ds(n * P, P)
            column = lambda a, n: a[:, n:n + 1] if isinstance(n, int) else a[:, bass.ds(n, 1)]

            def tiles_(e, body):
                with e.Fori(0, NT // 2 - 1) as i:
                    for b in range(2):
                        body(2 * i + b, b, True)
                for n in (NT - 2, NT - 1):
                    body(n, n % 2, n < NT - 1)
            with st.block() as blk:
                @blk.gpsimd
                def _(e):
                    steps.start(e, "pool")

                    def gather(n, b, more):
                        wait(e, "turned", n - 2)
                        e.nop(nofuse=True)
                        e.tensor_copy(idx[:, 2 * b:2 * b + 1], column(self.slots, n))
                        done(e.tensor_copy(idx[:, 2 * b + 1:2 * b + 2], column(self.slots, n + NT)), "idx")
                        wait(e, "idx", n)
                        e.nop(nofuse=True)
                        for k in range(2):
                            e.indirect_dma_start(out=ys[k][:, b, :], out_offset=None, in_=self.y_dram,
                                                 in_offset=bass.IndirectOffsetOnAxis(ap=idx[:, 2 * b + k:2 * b + k + 1], axis=0)).then_inc(s_g[b], 16)
                    tiles_(e, gather)

                @blk.tensor
                def _(e):
                    steps.start(e, "pe")

                    def turn(n, b, more):
                        wait(e, "mixed", n)
                        wait(e, "gated", n - 2)
                        for k in range(KT):
                            m = e.transpose(turned[b][:, k * P:(k + 1) * P], ys[0][:, b, k * P:(k + 1) * P], self.const("ident"))
                        done(m, "turned")
                    tiles_(e, turn)

                @blk.scalar
                def _(e):
                    steps.start(e, "act")

                    def square(n, b, more):
                        wait(e, "sum", n - 2)
                        wait(e, "x", n)
                        e.nop(nofuse=True)
                        done(e.activation(t3(sq[:, b, :]), x[:, :, tokens(n)], ACT.Square), "sq")
                    tiles_(e, square)

                @blk.vector
                def _(e):
                    steps.start(e, "dve")

                    def mix(n, b, so_far):
                        y0, y1 = (y[:, b, :] for y in ys)
                        e.wait_ge(s_g[b], so_far)
                        done(e.tensor_scalar(y0, y0, column(self.gates, n), None, ALU.mult), "scaled")
                        wait(e, "scaled", n)
                        done(e.scalar_tensor_tensor(y0, y1, column(self.gates, n + NT), y0, ALU.mult, ALU.add), "mixed")

                    def total(n, b):
                        wait(e, "sq", n)
                        done(e.tensor_reduce(self.acc_sq[:, tokens(n)], sq[:, b, :].rearrange("p (k t) -> p t k", k=KT), AX.X, ALU.add), "sum")

                    def body(n, b, more):
                        if more:
                            mix(n + 1, 1 - b, (n + 1 - (1 - b)) * 16 + 32)
                        wait(e, "turned", n)
                        wait(e, "x", n - 1)
                        done(e.tensor_tensor(t3(tmp[:, :]), t3(turned[b][:, :]), gate, ALU.mult), "gated")
                        wait(e, "gated", n)
                        done(e.tensor_tensor(x[:, :, tokens(n)], x[:, :, tokens(n)], t3(tmp[:, :]), ALU.add), "x")

                    mix(0, 0, 32)
                    body(0, 0, True)
                    with e.Fori(0, NT // 2 - 1) as i:
                        for b in (1, 0):
                            n = 2 * i + (2 - b)
                            body(n, b, True)
                            total(n - 1, 1 - b)
                    body(NT - 1, 1, False)
                    for n in (NT - 2, NT - 1):
                        total(n, n % 2)
        self.rkeep.close()

    def attention_in(self):
        self.keep = ExitStack()
        QKV = (Q_HEADS + 2 * KV_HEADS) * HD // P
        self.qkv = self.keep.enter_context(self.nc.sbuf_tensor("qkv", [P, QKV, T], F32))
        gemm_stage = self.stage("qkv")
        gemm_stage.__enter__()
        g = Gemm(gemm_stage, psum=False)
        with self.stage("renorm") as st:
            rstd, tmp, sq = st.sb("rstd", [P, T]), st.sb("tmp", [P, 4, T]), st.sb("sq", [P, 2, T])
            total = st.ps("total", [P, T])
            pe1, dve1, act1 = self.rstd(st, self.acc_sq, total, rstd, "rstd_a", after=lambda e: None)
            sq_act, sq_dve = self.sum_squares(st, sq, self.acc_sq, ready=lambda e: None,
                                              each=lambda e, k: st.wait(e, st.dve, f"normed{k}"))
            pe2, dve2, act2 = self.rstd(st, self.acc_sq, total, rstd, "rstd_b", after=lambda e: st.wait(e, st.dve, "sq_added7"))
            sc_dve, sc_act, sc_pool = self.scale_split(st, rstd, self.col("norm_mix", 0, KT), None, tmp, "rstd_b")
            with st.block() as blk:
                @blk.sync
                def _(e):
                    g.first(sp=e, srcs=[self.ins["w_qkv"][b] for b in range(2)])

                @blk.tensor
                def _(e):
                    st.pe.start(e)
                    pe1(e)
                    pe2(e)

                @blk.scalar
                def _(e):
                    st.act.start(e)
                    act1(e)
                    sq_act(e)
                    act2(e)
                    sc_act(e)

                @blk.gpsimd
                def _(e):
                    st.pool.start(e)
                    g.first(by=e)
                    sc_pool(e)

                @blk.vector
                def _(e):
                    st.dve.start(e)
                    dve1(e)
                    st.wait(e, st.act, "rstd_a")
                    for k in range(KT):
                        st.dve(e.scalar_tensor_tensor(self.x[:, k, :], self.x[:, k, :], self.col("final_norm_w", k), rstd[:, :],
                                                      ALU.mult, ALU.mult), f"normed{k}")
                        sq_dve(e, range(k - 1, k) if k else ())
                    sq_dve(e, range(KT - 1, KT))
                    st.dve.settle()
                    dve2(e)
                    sc_dve(e)
        with gemm_stage as st:
            g.banks()
            with st.block() as blk:
                @blk.sync
                def _(e):
                    with e.Fori(0, QKV // 2 - 1) as i:
                        for b in range(2):
                            g.load(e, i, 2, b, self.ins["w_qkv"][2 * i + (2 + b)])

                @blk.gpsimd
                def _(e):
                    g.after_first(e)
                    with e.Fori(0, QKV // 2 - 1) as i:
                        for b in range(2):
                            g.split(e, i, 2, b)

                @blk.tensor
                def _(e):
                    e.sem_inc(g.s_mult, 2)
                    with e.Fori(0, QKV // 2) as i:
                        for b in range(2):
                            g.mult(e, i, 0, b, self.xh, self.xl)

                @blk.scalar
                def _(e):
                    e.sem_inc(g.s_emptied, 2)
                    with e.Fori(0, QKV // 2) as i:
                        for b in range(2):
                            g.ready(e, i, 0, b)
                            g.empty(e.activation(tile_of(self.qkv, i, b), g.acc[b][:, :], ACT.Copy))

    def attention(self):
        qkv, QT, G4 = self.qkv, Q_HEADS * HD // P, Q_HEADS // KV_HEADS
        K0, V0 = QT, QT + 2
        LEAD = 2 * KV_HEADS
        with self.stage("att") as st:
            bias = st.sb("bias", [P, Q_HEADS, 2 * P])
            dist = st.sb("dist", [P, 2, 2 * P])
            qs, vs = st.sb("qs", [P, QT, P]), st.sb("vs", [P, 2, KV_HEADS * HD])
            vtok = qkv[:, V0:V0 + 2, :].rearrange("p k (t d) -> p (k t) d", d=KV_HEADS * HD)
            p = st.sb("p", [P, KV_HEADS, G4 * 2 * P])
            pt = st.sb("pt", [P, 2, 2 * HALF])
            diag = st.sb("diag", [P, KV_HEADS, G4 * P])
            small = lambda name: st.sb(name, [P, KV_HEADS, G4])
            ks = dist
            mx, neg, sums, esink, rden = (small(n) for n in ("mx", "neg", "sums", "esink", "rden"))
            nsink = self.cols[:, COLS["sinks"]].rearrange("p (j h) -> p j h", h=G4)
            sc = [st.ps(f"scores{b}", [P, G4 * 2 * P]) for b in range(2)]
            tp = st.ps("turned", [P, 2 * HALF])
            op = [st.ps(f"o{b}", [P, HALF]) for b in range(2)]
            s_dist, s_setup, s_vturned, s_vtok = (st.sem(n) for n in ("dist", "setup", "v_turned", "vtok"))
            owner = {"pe": ("scores", "turned", "pv"), "act": ("exp", "pt_prev", "o_hi"),
                     "dve": ("scored", "maxed", "neg", "shift", "den", "rden", "pt_cur", "o_lo"),
                     "pool": ("diag", "q_staged", "v_staged")}
            steps = Steps(st, LEAD, owner)
            start, done, wait = steps.start, steps.done, steps.wait
            mask_slopes = [2.0 ** (-8.0 * (h + 1) / Q_HEADS) for h in range(Q_HEADS)]

            def cols(n):
                return slice(0, P) if isinstance(n, int) and n == 0 else bass.ds(n * P, P)

            def is_first(n):
                return isinstance(n, int) and n == 0

            def keys(n):
                return slice(P, 2 * P) if is_first(n) else slice(0, 2 * P)

            def blocks(e, body):
                body(0, False)
                with e.Fori(0, NT - 2) as m:
                    body(m + 1, False)
                body(NT - 1, True)

            def ahead(n, j, k, last, f):
                if not (last and j + k >= KV_HEADS):
                    f(n + (j + k) // KV_HEADS, (j + k) % KV_HEADS)

            heads = lambda a: a.rearrange("p (h k) -> p h k", h=G4)
            half = lambda j: slice(64 * (j % 2), 64 * (j % 2) + 64)
            with st.block() as blk:
                @blk.sync
                def _(e):
                    e.dma_start(dist[:, :, :], self.ins["dist"]).then_inc(s_dist, 16)

                @blk.gpsimd
                def _(e):
                    start(e, "pool")

                    def stage_q(n, jj):
                        wait(e, "scores", 4 * n + (2 * jj - 3))
                        e.nop(nofuse=True)
                        k = slice(0, P) if is_first(n) else bass.ds((n - 1) * P, 2 * P)
                        e.tensor_copy(ks[:, jj, keys(n)], qkv[:, K0 + jj, k])
                        done(e.tensor_copy(qs[:, G4 * jj:G4 * (jj + 1), :], qkv[:, G4 * jj:G4 * (jj + 1), cols(n)]), "q_staged")

                    def stage_v(n, jj):
                        wait(e, "pv", 4 * n + (2 * jj - 3))
                        e.nop(nofuse=True)
                        c = slice(jj * P, (jj + 1) * P)
                        if is_first(n):
                            done(e.tensor_copy(vs[:, 1, c], vtok[:, 0, c]), "v_staged")
                        else:
                            done(e.tensor_copy(vs[:, :, c], vtok[:, bass.ds(n - 1, 2), c]), "v_staged")

                    def make_diag(n, j):
                        wait(e, "rden", 4 * n + j)
                        e.nop(nofuse=True)
                        done(e.tensor_tensor(heads(diag[:, j, :]), self.const("ident").unsqueeze(1).to_broadcast([P, G4, P]),
                                             rden[:, j, :].unsqueeze(2).to_broadcast([P, G4, P]), ALU.mult), "diag")

                    def body(n, last):
                        for j in range(KV_HEADS):
                            if j == 0 and not last:
                                stage_q(n + 1, 0)
                            ahead(n, j, 2, last, make_diag)
                            if j == 0:
                                stage_v(n, 1)
                            elif j == 1 and not last:
                                stage_q(n + 1, 1)
                            elif j == 3 and not last:
                                stage_v(n + 1, 0)
                    e.wait_ge(s_setup, Q_HEADS + 1)
                    stage_q(0, 0)
                    stage_q(0, 1)
                    e.wait_ge(s_vtok, 2)
                    stage_v(0, 0)
                    make_diag(0, 0)
                    make_diag(0, 1)
                    blocks(e, body)

                @blk.tensor
                def _(e):
                    start(e, "pe")

                    def scores(n, j):
                        b, jj = j % 2, j // 2
                        wait(e, "q_staged", 2 * n + jj)
                        wait(e, "scored", 4 * n + (j - 2))
                        for h in range(G4):
                            m = e.matmul(heads(sc[b][:, :])[:, h, keys(n)], qs[half(j), G4 * jj + h, :],
                                         ks[half(j), jj, keys(n)], start=True, stop=True)
                        done(m, "scores")

                    def body(n, last):
                        for j in range(KV_HEADS):
                            b, jj, g = j % 2, j // 2, 4 * n + j
                            ws = (1,) if is_first(n) else (0, 1)
                            wait(e, "diag", g)
                            wait(e, "pt_prev", g - 1)
                            wait(e, "pt_cur", g - 1)
                            for w in ws:
                                for h in range(G4):
                                    m = e.matmul(tp[:, w * HALF + h * P:w * HALF + (h + 1) * P],
                                                 p[:, j, (2 * h + w) * P:(2 * h + w + 1) * P],
                                                 diag[:, j, h * P:(h + 1) * P], start=True, stop=True)
                            done(m, "turned")
                            ahead(n, j, 3, last, scores)
                            wait(e, "pt_prev", g)
                            wait(e, "pt_cur", g)
                            wait(e, "v_staged", 2 * n + jj)
                            wait(e, "o_lo", g - 2)
                            for w in ws:
                                m = e.matmul(op[b][:, :], vs[:, w, jj * P:(jj + 1) * P], pt[:, b, w * HALF:(w + 1) * HALF],
                                             start=(w == ws[0]), stop=(w == 1))
                            done(m, "pv")
                    for s in range(2):
                        for t in range(NT // 2):
                            for k in range(2):
                                m = e.transpose(sc[s][:, (2 * t + k) * P:(2 * t + k + 1) * P],
                                                qkv[:, V0 + k, (NT // 2 * s + t) * P:(NT // 2 * s + t + 1) * P], self.const("ident"))
                        m.then_inc(s_vturned, 1)
                    e.wait_ge(s_vtok, 2)
                    for j in range(3):
                        scores(0, j)
                    blocks(e, body)

                @blk.scalar
                def _(e):
                    start(e, "act")

                    def exps(n, j):
                        wait(e, "shift", 4 * n + j)
                        e.activation(esink[:, j, :], esink[:, j, :], ACT.Exp)
                        for h in range(G4):
                            a = heads(p[:, j, :])[:, h, keys(n)]
                            m = e.activation(a, a, ACT.Exp, bias=neg[:, j, h:h + 1], accum_out=sums[:, j, h:h + 1])
                        done(m, "exp")

                    def body(n, last):
                        for j in range(KV_HEADS):
                            b, jj, g = j % 2, j // 2, 4 * n + j
                            if is_first(n):
                                steps.skip(e, "pt_prev")
                            else:
                                wait(e, "turned", g)
                                wait(e, "pv", g - 2)
                                done(e.activation(pt[:, b, 0:HALF], tp[:, 0:HALF], ACT.Copy), "pt_prev")
                            ahead(n, j, 2, last, exps)
                            wait(e, "pv", g)
                            done(e.activation(self.xh[half(j), G4 * jj:G4 * (jj + 1), cols(n)], heads(op[b][half(j), :]), ACT.Copy), "o_hi")
                    e.wait_ge(s_vturned, 2)
                    for s in range(2):
                        e.activation(vtok[:, NT // 2 * s:NT // 2 * (s + 1), :].rearrange("p t d -> p (t d)"), sc[s][:, :],
                                     ACT.Copy).then_inc(s_vtok, 1)
                    exps(0, 0)
                    exps(0, 1)
                    blocks(e, body)

                @blk.vector
                def _(e):
                    start(e, "dve")

                    def score(n, j):
                        g = 4 * n + j
                        wait(e, "scores", g)
                        wait(e, "turned", g - 4)
                        v = heads(p[:, j, :])[:, :, keys(n)]
                        done(e.scalar_tensor_tensor(v, heads(sc[j % 2][:, :])[:, :, keys(n)], HD ** -0.5,
                                                    bias[:, G4 * j:G4 * j + G4, keys(n)], ALU.mult, ALU.add), "scored")
                        wait(e, "scored", g)
                        done(e.tensor_reduce(mx[:, j, :], v, AX.X, ALU.max), "maxed")
                        wait(e, "maxed", g)
                        done(e.scalar_tensor_tensor(neg[:, j, :], mx[:, j, :], -1.0, nsink[:, j, :], ALU.mult, ALU.min), "neg")
                        wait(e, "neg", g)
                        done(e.tensor_tensor(esink[:, j, :], neg[:, j, :], nsink[:, j, :], ALU.subtract), "shift")

                    def inverse(n, j):
                        g = 4 * n + j
                        wait(e, "exp", g)
                        done(e.tensor_tensor(sums[:, j, :], sums[:, j, :], esink[:, j, :], ALU.add), "den")
                        wait(e, "den", g)
                        done(e.reciprocal(rden[:, j, :], sums[:, j, :]), "rden")

                    def body(n, last):
                        for j in range(KV_HEADS):
                            b, jj, g = j % 2, j // 2, 4 * n + j
                            wait(e, "turned", g)
                            wait(e, "pv", g - 2)
                            done(e.tensor_copy(pt[:, b, HALF:], tp[:, HALF:]), "pt_cur")
                            ahead(n, j, 3, last, score)
                            ahead(n, j, 2, last, inverse)
                            wait(e, "o_hi", g)
                            x = slice(G4 * jj, G4 * (jj + 1))
                            done(e.tensor_tensor(self.xl[half(j), x, cols(n)], heads(op[b][half(j), :]),
                                                 self.xh[half(j), x, cols(n)].bitcast(F32), ALU.subtract), "o_lo")
                    e.wait_ge(s_dist, 16)
                    for h in range(Q_HEADS):
                        e.scalar_tensor_tensor(bias[:, h, :], dist[:, 0, :], mask_slopes[h], dist[:, 1, :], ALU.mult, ALU.add).then_inc(s_setup, 1)
                    e.tensor_scalar(nsink, nsink, -1.0, None, ALU.mult).then_inc(s_setup, 1)
                    e.wait_ge(s_setup, Q_HEADS + 1)
                    for j in range(3):
                        score(0, j)
                    inverse(0, 0)
                    inverse(0, 1)
                    blocks(e, body)
        self.keep.close()

    def feed_forward(self):
        x = self.x
        gemm_stage = self.stage("ff")
        gemm_stage.__enter__()
        g = Gemm(gemm_stage, psum=False)
        with self.stage("ffnorm") as st:
            rstd, tmp = st.sb("rstd", [P, T]), st.sb("tmp", [P, 4, T])
            total = st.ps("total", [P, T])
            pe1, dve1, act1 = self.rstd(st, self.acc_sq, total, rstd, after=lambda e: None)
            sc_dve, sc_act, sc_pool = self.scale_split(st, rstd, self.col("norm_ffn", 0, KT), None, tmp, "rstd")
            with st.block() as blk:
                @blk.sync
                def _(e):
                    g.first(sp=e, srcs=[self.ins["w_up"][b] for b in range(2)])

                @blk.tensor
                def _(e):
                    st.pe.start(e)
                    pe1(e)

                @blk.scalar
                def _(e):
                    st.act.start(e)
                    act1(e)
                    sc_act(e)

                @blk.gpsimd
                def _(e):
                    st.pool.start(e)
                    g.first(by=e)
                    sc_pool(e)

                @blk.vector
                def _(e):
                    st.dve.start(e)
                    dve1(e)
                    sc_dve(e)
        with gemm_stage as st:
            g.banks()
            ah, al = st.sb("ah", [P, max(FF_PARTS), T], F32R), st.sb("al", [P, max(FF_PARTS), T], F32R)
            a, sq = st.sb("a", [P, T]), st.sb("sq", [P, T])
            parts, base, wide = [], 0, 0
            for n, w in enumerate(FF_PARTS):
                parts.append((n, w, wide, base, base + 2 * w))
                base += 2 * w + KT
                wide += w
            up, down = self.ins["w_up"], [self.ins[f"w_down{n}"] for n in range(len(FF_PARTS))]
            with st.block() as blk:
                @blk.sync
                def _(e):
                    for n, w, at, b_up, b_down in parts:
                        skip = 1 if n == 0 else 0
                        with e.Fori(0, w - skip) as i:
                            for b in range(2):
                                g.load(e, i, b_up + 2 * skip, b, up[2 * i + (2 * at + 2 * skip + b)])
                        with e.Fori(0, KT // 2) as i:
                            for b in range(2):
                                g.load(e, i, b_down, b, down[n][2 * i + b], kt=w)

                @blk.gpsimd
                def _(e):
                    g.after_first(e)
                    for n, w, at, b_up, b_down in parts:
                        skip = 1 if n == 0 else 0
                        with e.Fori(0, w - skip) as i:
                            for b in range(2):
                                g.split(e, i, b_up + 2 * skip, b)
                        with e.Fori(0, KT // 2) as i:
                            for b in range(2):
                                g.split(e, i, b_down, b, kt=w)

                @blk.tensor
                def _(e):
                    e.sem_inc(g.s_mult, 2)
                    for n, w, at, b_up, b_down in parts:
                        with e.Fori(0, w) as i:
                            for b in range(2):
                                g.mult(e, i, b_up, b, self.xh, self.xl)
                        st.wait(e, st.dve, f"a_lo{n}")
                        with e.Fori(0, KT // 2) as i:
                            for b in range(2):
                                g.mult(e, i, b_down, b, ah, al, kt=w)

                @blk.scalar
                def _(e):
                    st.act.start(e)
                    e.preload_act_table(ACT.Silu)
                    for n, w, at, b_up, b_down in parts:
                        e.wait_ge(g.s_mult, b_up + 2)
                        with st.act.loop(w) as i:
                            g.ready(e, i, b_up, 0)
                            g.emptied(e, i - 1, b_up, 1)
                            g.empty(e.activation(sq[:, :], g.acc[0][:, :], ACT.Silu))
                            g.emptied(e, i, b_up, 1)
                            st.act(e.activation(tile_of(ah, i, 0, 1), a[:, :], ACT.Copy), f"hi{n}")
                    with st.act.loop(KT // 2) as i:
                        for b in range(2):
                            g.emptied(e, i, parts[-1][4], b)
                            st.wait(e, st.dve, "sum1" if b == 0 else "sum0", i - 1 if b == 0 else i)
                            st.act(e.activation(sq[:, :], tile_of(x, i, b), ACT.Square), f"sq{b}")

                @blk.vector
                def _(e):
                    st.dve.start(e)
                    e.sem_inc(g.s_emptied, 2)
                    st.dve(e.memset(self.acc_sq[:, :], 0.0))
                    for n, w, at, b_up, b_down in parts:
                        with st.dve.loop(w) as i:
                            g.emptied(e, i, b_up, 0)
                            g.ready(e, i, b_up, 1)
                            st.dve.settle()
                            g.empty(e.tensor_tensor(a[:, :], sq[:, :], g.acc[1][:, :], ALU.mult))
                            st.wait(e, st.act, f"hi{n}", i)
                            g.emptied(e, i, b_up, 1)
                            st.dve(e.tensor_tensor(tile_of(al, i, 0, 1), a[:, :], tile_of(ah, i, 0, 1).bitcast(F32), ALU.subtract), f"a_lo{n}")
                        last = n == len(parts) - 1
                        with st.dve.loop(KT // 2) as i:
                            for b in range(2):
                                g.ready(e, i, b_down, b)
                                xn = tile_of(x, i, b)
                                g.empty(e.tensor_tensor(xn, g.acc[b][:, :], xn, ALU.add))
                                if last:
                                    st.wait(e, st.act, f"sq{b}", i)
                                    st.dve.settle()
                                    st.dve(e.tensor_tensor(self.acc_sq[:, :], self.acc_sq[:, :], sq[:, :], ALU.add), f"sum{b}")

    def finish(self):
        x = self.x
        with self.stage("out") as st:
            rstd, ost, otok = st.sb("rstd", [P, T]), st.sb("ost", [P, 2, KT * P]), st.sb("otok", [P, 2, D])
            total = st.ps("total", [P, T])
            turned = [st.ps(f"turned{b}", [P, D]) for b in range(2)]
            s_o = [st.sem(f"o{b}") for b in range(2)]
            pe1, dve1, act1 = self.rstd(st, self.acc_sq, total, rstd, after=lambda e: None)
            t3 = lambda a: a.rearrange("p (k t) -> p k t", k=KT)
            with st.block() as blk:
                @blk.sync
                def _(e):
                    for b in range(2):
                        e.sem_inc(s_o[b], 16)
                    with e.Fori(0, NT // 2) as i:
                        for b in range(2):
                            st.wait(e, st.act, f"otok{b}", i)
                            e.dma_start(self.out[bass.ds(2 * P * i + P * b, P), :], otok[:, b, :]).then_inc(s_o[b], 16)
                    for b in range(2):
                        e.wait_ge(s_o[b], 16 * (NT // 2) + 16)

                @blk.tensor
                def _(e):
                    st.pe.start(e)
                    pe1(e)
                    with st.pe.loop(NT // 2) as i:
                        for b in range(2):
                            st.wait(e, st.dve, f"scaled{b}", i)
                            st.wait(e, st.act, f"otok{b}", i - 1)
                            for k in range(KT):
                                m = e.transpose(turned[b][:, k * P:(k + 1) * P], ost[:, b, k * P:(k + 1) * P], self.const("ident"))
                            st.pe(m, f"turned{b}")

                @blk.scalar
                def _(e):
                    st.act.start(e)
                    act1(e)
                    with st.act.loop(NT // 2) as i:
                        for b in range(2):
                            st.wait(e, st.pe, f"turned{b}", i)
                            e.wait_ge(s_o[b], 16 * i + 16)
                            st.act(e.activation(otok[:, b, :], turned[b][:, :], ACT.Copy), f"otok{b}")

                @blk.vector
                def _(e):
                    st.dve.start(e)
                    dve1(e)
                    st.wait(e, st.act, "rstd")
                    w = self.col("final_norm", 0, KT).unsqueeze(2).to_broadcast([P, KT, P])
                    with st.dve.loop(NT // 2) as i:
                        for b in range(2):
                            ts = bass.ds(2 * P * i + P * b, P)
                            st.wait(e, st.pe, f"turned{b}", i - 1)
                            st.dve(e.tensor_tensor(t3(ost[:, b, :]), x[:, :, ts], rstd[:, ts].unsqueeze(1).to_broadcast([P, KT, P]), ALU.mult))
                            st.dve.settle()
                            st.dve(e.tensor_tensor(t3(ost[:, b, :]), t3(ost[:, b, :]), w, ALU.mult), f"scaled{b}")


def tiles(w, kt=None):
    K, N = w.shape
    return np.ascontiguousarray(w.reshape(K // P, P, N // P, P).transpose(2, 1, 0, 3)).reshape(N // P, P, K)


def layout(a):
    def per_tile(v):
        return v.reshape(-1, P).T
    f = np.float32
    first = a["w_in"][0]
    u, z, xbc, dt = np.split(first, [256, 1024, 2816], axis=1)
    pad = np.zeros((D, P - HEADS), f)
    heads = np.arange(Q_HEADS).reshape(2, 2, 4).transpose(0, 2, 1).reshape(-1)
    qcols = (heads[:, None] * HD + np.arange(HD)).reshape(-1)
    wqkv = a["swa_w_in_2"][0]
    wqkv = np.concatenate([wqkv[:, :Q_HEADS * HD][:, qcols], wqkv[:, Q_HEADS * HD:]], axis=1)
    gu = a["ffn_w_gate_up_2"][0]
    gu = gu.reshape(D, 2, FFT, P).transpose(0, 2, 1, 3).reshape(D, -1)
    cols = np.zeros((P, NCOLS), f)
    cols[:, COLS["b_ada"]] = per_tile(a["b_ada"][0])
    cols[:, COLS["conv_w"]] = a["conv_w"][0].reshape(CONV, CONV_T, P).transpose(2, 1, 0).reshape(P, -1)
    cols[:, COLS["conv_b"]] = per_tile(a["conv_b"][0])
    cols[:, COLS["d_skip"]] = per_tile(np.repeat(a["d_skip"][0], HD))
    cols[:, COLS["pool_scale"]] = per_tile(a["pool_scale"][0])
    cols[:, COLS["ssd_norm_w"]] = per_tile(a["ssd_norm_w"][0])
    cols[:, COLS["final_norm_w"]] = per_tile(a["final_norm_w"])
    cols[:, COLS["norm_mix"]] = per_tile(a["norm_mix_2"][0])
    cols[:, COLS["norm_ffn"]] = per_tile(a["norm_ffn_2"][0])
    cols[:, COLS["final_norm"]] = per_tile(a["final_norm_2"])
    cols[:, COLS["router_b"]] = np.concatenate([a["b_group"][0], a["b_router"][0]])[None]
    cols[:, COLS["sinks"]] = a["swa_sinks_2"][0][None]
    cols[:HEADS, COLS["dt_bias"]] = a["dt_bias"][0][:, None]
    cols[:HEADS, COLS["a_log"]] = a["a_log"][0][:, None]
    k = np.arange(P)
    consts = np.zeros((P, NCONST), f)
    consts[:, CONSTS["ident"]] = np.eye(P)
    consts[:, CONSTS["ones"]] = 1
    consts[:, CONSTS["upto"]] = k[:, None] <= k[None]
    consts[:, CONSTS["before"]] = k[:, None] < k[None]
    window = np.array([[2, 4], [8, 16]])[:, k // 64].T
    consts[:, CONSTS["pool_first"]] = (window[:, :, None] / np.minimum(np.arange(1, 17), window[:, :, None])).reshape(P, 32)
    consts[:, CONSTS["pool_inv"]] = 1.0 / window
    consts[:, CONSTS["iota8"]] = np.arange(8)
    consts[:, CONSTS["iota8x128"]] = np.arange(8) * P
    consts[:, CONSTS["iotab"]] = np.arange(NBLK + 1)
    consts[:, CONSTS["tokid"]] = k[:, None] + P * np.arange(NT)
    sel = np.zeros((HEADS, HEADS, P), f)
    sel[np.arange(HEADS), np.arange(HEADS)] = 1
    group = np.arange(SSD_T * P).reshape(SSD_T, P) // (SSD_T * P // GROUPS)
    member = (group.T[:, :, None] == np.arange(GROUPS)).astype(f)
    d = P + k[:, None] - np.arange(2 * P)[None]
    ok = (d >= 0) & (d < P)
    wpool = np.zeros((P, POOL_T, P), f)
    for g in range(4):
        wpool[64 * (g % 2):64 * (g % 2) + 64, g // 2, 64 * (g % 2):64 * (g % 2) + 64] = a["w_pool"][0, g]
    down = a["ffn_w_down_2"][0]
    at = np.cumsum((0,) + FF_PARTS) * P
    return {
        "cols": cols, "consts": consts, "sel": sel.reshape(HEADS, -1), "member": member,
        "member_t": np.ascontiguousarray(member.transpose(2, 1, 0)),
        "dist": np.stack([np.where(ok, -d, 0), np.where(ok, 0, -BIG)], 1).astype(f),
        "x": np.ascontiguousarray(a["x"][0]).reshape(NT, P, D),
        "w_ada": np.ascontiguousarray(a["w_ada"][0].T).reshape(-1, P, D),
        "c_rows": np.tile(a["c"][0].reshape(1, D), (P, 1)),
        "w_in": tiles(np.concatenate([xbc, z, dt, pad, u], axis=1)),
        "w_pool": wpool,
        "w_out": tiles(a["w_out"][0]),
        "w_route": np.ascontiguousarray(np.concatenate([a["w_group"][0], a["w_router"][0]], 1).reshape(KT, P, EG + NE).transpose(1, 0, 2)),
        "w13": np.ascontiguousarray(a["w13"][0]), "w2": np.ascontiguousarray(a["w2"][0]),
        "w_qkv": tiles(wqkv),
        "swa_w_out": tiles(a["swa_w_out_2"][0][qcols]),
        "w_up": tiles(gu),
        **{f"w_down{n}": tiles(down[at[n]:at[n + 1]]) for n in range(len(FF_PARTS))},
    }


def program(nc, shapes, counts):
    ins = {k: nc.dram_tensor(f"in_{k}", s, F32, kind="ExternalInput").ap() for k, s in shapes.items()}
    out = nc.dram_tensor("out", (T, D), F32, kind="ExternalOutput").ap()
    marks = {}
    Kernel(nc, ins, out, counts, marks).build()
    return marks


def kernel(**inputs):
    import concourse.bacc as bacc
    from concourse.bass_utils import run_bass_kernel_spmd
    arrays = layout({k: np.asarray(v) for k, v in inputs.items()})
    shapes = {k: v.shape for k, v in arrays.items()}
    counts = {}
    for _ in range(3):
        nc = bacc.Bacc("TRN2", target_bir_lowering=False, num_devices=1)
        counts = program(nc, shapes, counts)
    r = run_bass_kernel_spmd(nc, [{f"in_{k}": v for k, v in arrays.items()}], core_ids=[0])
    return r.results[0]["out"].reshape(1, T, D)
```
